# Optimizing a Trainium2 kernel written in Bass

```python
import math
import jax
import jax.numpy as jnp
from jax import lax
import numpy as np

D_MODEL = 2048
BATCH = 1
SEQ = 256
DEPTH = 1

N_META = 16
NORM_EPS = 1e-6
L2_EPS = 1e-6

GDN_HEADS = 8
GDN_DK = 128
GDN_DV = 128
GDN_CONV = 4
GDN_CHUNK = 64

MLA_HEADS = 8
MLA_Q_LORA = 768
MLA_KV_LORA = 512
MLA_D_NOPE = 128
MLA_D_ROPE = 64
MLA_DV = 128
ROPE_THETA = 10000.0
ATTN_BLOCK = 128

RWKV_HEADS = 16
RWKV_N = 64
RWKV_W = RWKV_HEADS * RWKV_N
RWKV_DECAY_LORA = 64
RWKV_A_LORA = 64
RWKV_G_LORA = 160
RWKV_LN_EPS = 64e-5
RWKV_IN = 3 * RWKV_W + RWKV_DECAY_LORA + RWKV_A_LORA + RWKV_G_LORA

N_BRANCH = 3
BRANCH_W = 1024

N_GROUPS = 4
EXPERTS_PER_GROUP = 8
N_EXPERTS = N_GROUPS * EXPERTS_PER_GROUP
TOP_K = 2
D_EXPERT = 512
MOE_BLOCK = 128

GDN_QK = GDN_HEADS * GDN_DK
GDN_VW = GDN_HEADS * GDN_DV
IN_SPLITS = (GDN_QK, GDN_QK, GDN_VW, GDN_VW, GDN_HEADS, GDN_HEADS,
             MLA_Q_LORA, MLA_KV_LORA, MLA_D_ROPE, RWKV_IN, N_BRANCH * D_MODEL)
D_IN = sum(IN_SPLITS)

kernel_name = 'hybrid_gdn_mla_rwkv7_hmoe'

F32 = jnp.float32

def _split(x, sizes):
    return jnp.split(x, np.cumsum(sizes)[:-1].tolist(), axis=-1)

def rmsnorm(x, w, eps=NORM_EPS):
    x32 = x.astype(F32)
    y = x32 * lax.rsqrt(jnp.mean(jnp.square(x32), axis=-1, keepdims=True) + eps)
    return (y * w.astype(F32)).astype(x.dtype)

def l2norm(x, eps=L2_EPS):
    return x * lax.rsqrt(jnp.sum(jnp.square(x), axis=-1, keepdims=True) + eps)

def causal_depthwise_conv(x, w):
    K, C = w.shape
    return lax.conv_general_dilated(
        x, w[:, None, :].astype(x.dtype), window_strides=(1,), padding=[(K - 1, 0)],
        dimension_numbers=('NWC', 'WIO', 'NWC'), feature_group_count=C)

def rotary(x, cos, sin):
    x1, x2 = jnp.split(x, 2, axis=-1)
    return jnp.concatenate([x1 * cos - x2 * sin, x2 * cos + x1 * sin], axis=-1)

def gated_deltanet(q, k, v, z, b, a, conv_w, a_log, dt_bias, norm_w):
    B, T, _ = q.shape
    H, DK, DV, C = GDN_HEADS, GDN_DK, GDN_DV, GDN_CHUNK
    qkv = jax.nn.silu(causal_depthwise_conv(jnp.concatenate([q, k, v], axis=-1), conv_w))
    q, k, v = _split(qkv.astype(F32), (GDN_QK, GDN_QK, GDN_VW))
    q = l2norm(q.reshape(B, T, H, DK)) * DK ** -0.5
    k = l2norm(k.reshape(B, T, H, DK))
    v = v.reshape(B, T, H, DV)
    beta = jax.nn.sigmoid(b.astype(F32))
    g = -jnp.exp(a_log.astype(F32)) * jax.nn.softplus(a.astype(F32) + dt_bias.astype(F32))
    front = (-N_META) % C
    n_chunks = -(-(T + front) // C)
    back = n_chunks * C - T - front

    def to_chunks(t):
        t = jnp.pad(t, [(0, 0), (front, back)] + [(0, 0)] * (t.ndim - 2))
        return jnp.moveaxis(t.reshape((B, n_chunks, C) + t.shape[2:]), 3, 1)

    q, k, v, beta, g = [to_chunks(t) for t in (q, k, v, beta, g)]
    gc = jnp.cumsum(g, axis=-1)
    causal = jnp.tril(jnp.ones((C, C), bool))
    strict = jnp.tril(jnp.ones((C, C), bool), -1)
    decay = jnp.where(causal, jnp.exp(jnp.where(causal, gc[..., :, None] - gc[..., None, :], 0.0)), 0.0)
    kb = k * beta[..., None]
    A = jnp.where(strict, jnp.einsum('bhncd,bhnsd->bhncs', kb, k) * decay, 0.0)
    eye = jnp.eye(C, dtype=F32)
    t_inv = lax.linalg.triangular_solve(A + eye, jnp.broadcast_to(eye, A.shape),
                                        left_side=True, lower=True, unit_diagonal=True)
    u = t_inv @ (v * beta[..., None])
    w = t_inv @ (kb * jnp.exp(gc)[..., None])
    attn = jnp.einsum('bhncd,bhnsd->bhncs', q, k) * decay
    q_dec = q * jnp.exp(gc)[..., None]
    k_dec = k * jnp.exp(gc[..., -1:] - gc)[..., None]
    g_last = jnp.exp(gc[..., -1])
    xs = tuple(jnp.moveaxis(t, 2, 0) for t in (u, w, attn, q_dec, k_dec, g_last))

    def chunk_step(S, inp):
        u_n, w_n, attn_n, q_n, k_n, gl_n = inp
        v_new = u_n - jnp.einsum('bhcd,bhde->bhce', w_n, S)
        o = jnp.einsum('bhcd,bhde->bhce', q_n, S) + jnp.einsum('bhcs,bhse->bhce', attn_n, v_new)
        S = S * gl_n[..., None, None] + jnp.einsum('bhcd,bhce->bhde', k_n, v_new)
        return S, o

    _, o = lax.scan(chunk_step, jnp.zeros((B, H, DK, DV), F32), xs)
    o = jnp.moveaxis(o, 0, 2).reshape(B, H, n_chunks * C, DV)
    o = jnp.transpose(o, (0, 2, 1, 3))[:, front:front + T]
    o = rmsnorm(o, norm_w) * jax.nn.silu(z.reshape(B, T, H, DV).astype(F32))
    return o.reshape(B, T, GDN_VW).astype(z.dtype)

def causal_block_attention(q_nope, q_rope, k_nope, k_rope, v, scale):
    B, T, H, _ = q_nope.shape
    n_blk = -(-T // ATTN_BLOCK)
    pad = n_blk * ATTN_BLOCK - T

    def blocks(t):
        t = jnp.pad(t, [(0, 0), (0, pad), (0, 0), (0, 0)])
        return jnp.moveaxis(t.reshape((B, n_blk, ATTN_BLOCK) + t.shape[2:]), 1, 0)

    key_pos = jnp.arange(T)

    def one_block(args):
        qn, qr, start = args
        s = (jnp.einsum('bqhd,bkhd->bhqk', qn, k_nope)
             + jnp.einsum('bqhd,bkd->bhqk', qr, k_rope)).astype(F32) * scale
        q_pos = start + jnp.arange(ATTN_BLOCK)
        s = jnp.where(key_pos[None, :] <= q_pos[:, None], s, -jnp.inf)
        p = jax.nn.softmax(s, axis=-1)
        return jnp.einsum('bhqk,bkhd->bqhd', p.astype(v.dtype), v)

    starts = jnp.arange(n_blk) * ATTN_BLOCK
    out = lax.map(one_block, (blocks(q_nope), blocks(q_rope), starts))
    return jnp.moveaxis(out, 0, 1).reshape(B, n_blk * ATTN_BLOCK, H, v.shape[-1])[:, :T]

def mla(cq, ckv, k_pe, q_norm, w_q_up, kv_norm, w_kv_up, cos, sin):
    B, T, _ = cq.shape
    H = MLA_HEADS
    q = (rmsnorm(cq, q_norm) @ w_q_up).reshape(B, T, H, MLA_D_NOPE + MLA_D_ROPE).astype(F32)
    q_nope, q_pe = q[..., :MLA_D_NOPE], rotary(q[..., MLA_D_NOPE:], cos, sin)
    kv = (rmsnorm(ckv, kv_norm) @ w_kv_up).reshape(B, T, H, MLA_D_NOPE + MLA_DV).astype(F32)
    k_nope, v = kv[..., :MLA_D_NOPE], kv[..., MLA_D_NOPE:]
    k_pe = rotary(k_pe.astype(F32)[:, :, None, :], cos, sin)[:, :, 0]
    o = causal_block_attention(q_nope, q_pe, k_nope, k_pe, v, (MLA_D_NOPE + MLA_D_ROPE) ** -0.5)
    return o.reshape(B, T, H * MLA_DV).astype(cq.dtype)

def rwkv7_time_mix(xin, mu, w0, w2, a0, a2, g2, k_k, k_a, r_k, ln_w, ln_b):
    B, T, _ = xin.shape
    H, N, C = RWKV_HEADS, RWKV_N, RWKV_W
    dtype = xin.dtype
    xin = xin.astype(F32)
    prev = jnp.pad(xin, [(0, 0), (1, 0), (0, 0)])[:, :-1]
    xm = xin + (prev - xin) * mu
    r, k, v, xw, xa, xg = _split(xm, (C, C, C, RWKV_DECAY_LORA, RWKV_A_LORA, RWKV_G_LORA))
    w_log = -jax.nn.softplus(-(w0 + jnp.tanh(xw) @ w2)) - 0.5
    decay = jnp.exp(-jnp.exp(w_log))
    a = jax.nn.sigmoid(a0 + xa @ a2)
    g = jax.nn.sigmoid(xg) @ g2

    def heads(t):
        return t.reshape(B, T, H, N)

    kk = l2norm(heads(k * k_k))
    k = k * (1.0 + (a - 1.0) * k_a)
    r_h, k_h, v_h, a_h = heads(r), heads(k), heads(v), heads(a)
    seq = tuple(jnp.moveaxis(t, 1, 0) for t in (r_h, heads(decay), k_h, v_h, -kk, kk * a_h))

    def step(S, inp):
        r_t, w_t, k_t, v_t, a_t, b_t = inp
        sa = jnp.einsum('bhij,bhj->bhi', S, a_t)
        S = S * w_t[:, :, None, :] + sa[..., None] * b_t[:, :, None, :] + v_t[..., None] * k_t[:, :, None, :]
        return S, jnp.einsum('bhij,bhj->bhi', S, r_t)

    _, y = lax.scan(step, jnp.zeros((B, H, N, N), F32), seq)
    y = jnp.moveaxis(y, 0, 1)
    mean = jnp.mean(y, axis=-1, keepdims=True)
    var = jnp.mean(jnp.square(y - mean), axis=-1, keepdims=True)
    y = ((y - mean) * lax.rsqrt(var + RWKV_LN_EPS)).reshape(B, T, C) * ln_w + ln_b
    y = y + (jnp.sum(r_h * k_h * r_k, axis=-1, keepdims=True) * v_h).reshape(B, T, C)
    return (y * g).astype(dtype)

def hybrid_mixer(h, w_in, gdn_p, mla_p, rwkv_p, w_branch, w_out, cos, sin):
    B, T, _ = h.shape
    proj = h @ w_in
    gq, gk, gv, gz, gb, ga, cq, ckv, kpe, rw, gate_logits = _split(proj, IN_SPLITS)
    y_a = gated_deltanet(gq, gk, gv, gz, gb, ga, *gdn_p)
    y_b = mla(cq, ckv, kpe, *mla_p, cos, sin)
    y_c = rwkv7_time_mix(rw, *rwkv_p)
    gate = jax.nn.sigmoid(gate_logits.astype(F32)).reshape(B, T, N_BRANCH, D_MODEL)
    merged = (gate[:, :, 0] * (y_a @ w_branch[0]).astype(F32)
              + gate[:, :, 1] * (y_b @ w_branch[1]).astype(F32)
              + gate[:, :, 2] * (y_c @ w_branch[2]).astype(F32))
    return (merged.astype(h.dtype) @ w_out).astype(h.dtype)

def hierarchical_moe(h, w_rg, b_rg, w_re, b_re, w_gate, w_up, w_down):
    B, T, D = h.shape
    n = B * T
    xt = h.reshape(n, D)
    g_logits = (xt @ w_rg + b_rg).astype(F32)
    g_top, g_idx = lax.top_k(g_logits, 1)
    p_group = jnp.exp(g_top - jax.nn.logsumexp(g_logits, axis=-1, keepdims=True))
    e_logits = (xt @ w_re + b_re).astype(F32).reshape(n, N_GROUPS, EXPERTS_PER_GROUP)
    e_in_group = e_logits[jnp.arange(n), g_idx[:, 0]]
    e_top, e_idx = lax.top_k(e_in_group, TOP_K)
    gate_w = jax.nn.softmax(e_top, axis=-1) * p_group
    expert = (g_idx * EXPERTS_PER_GROUP + e_idx).reshape(-1)
    n_assign = n * TOP_K
    order = jnp.argsort(expert)
    sorted_expert = expert[order]
    counts = jnp.bincount(expert, length=N_EXPERTS)
    starts = jnp.cumsum(counts) - counts
    padded = (counts + MOE_BLOCK - 1) // MOE_BLOCK * MOE_BLOCK
    padded_end = jnp.cumsum(padded)
    padded_start = padded_end - padded
    dest_sorted = (padded_start[sorted_expert] + jnp.arange(n_assign) - starts[sorted_expert]).astype(jnp.int32)
    n_rows = -(-n_assign // MOE_BLOCK) * MOE_BLOCK + N_EXPERTS * MOE_BLOCK
    n_blocks = n_rows // MOE_BLOCK
    row_token = jnp.full((n_rows,), n, jnp.int32).at[dest_sorted].set((order // TOP_K).astype(jnp.int32))
    block_expert = jnp.minimum(
        jnp.searchsorted(padded_end, jnp.arange(n_blocks) * MOE_BLOCK, side='right'), N_EXPERTS - 1)
    x_rows = jnp.concatenate([xt, jnp.zeros((1, D), xt.dtype)], axis=0)[row_token]
    x_rows = x_rows.reshape(n_blocks, MOE_BLOCK, D)

    def expert_block(args):
        xb, e = args
        return (jax.nn.silu(xb @ w_gate[e]) * (xb @ w_up[e])) @ w_down[e]

    y_rows = lax.map(expert_block, (x_rows, block_expert)).reshape(n_rows, D)
    dest = jnp.zeros((n_assign,), jnp.int32).at[order].set(dest_sorted)
    y = y_rows[dest].reshape(n, TOP_K, D).astype(F32)
    out = jnp.sum(gate_w[..., None] * y, axis=1)
    return out.reshape(B, T, D).astype(h.dtype)

def setup_inputs(seed: int = 0) -> dict:
    key = jax.random.key(seed)
    ks = iter(jax.random.split(key, 48))
    L, D = DEPTH, D_MODEL

    def nrm(shape, scale):
        return jax.random.normal(next(ks), shape, F32) * scale

    def gain(shape):
        return 1.0 + 0.02 * jax.random.normal(next(ks), shape, F32)

    def unif(shape, lo, hi):
        return jax.random.uniform(next(ks), shape, F32, lo, hi)

    dt = jnp.exp(unif((L, GDN_HEADS), math.log(1e-3), math.log(1e-1)))
    return {
        'x': nrm((BATCH, SEQ, D), 1.0),
        'meta_tokens': nrm((N_META, D), 1.0),
        'norm_mix': gain((L, D)),
        'w_in': nrm((L, D, D_IN), D ** -0.5),
        'gdn_conv': nrm((L, GDN_CONV, 2 * GDN_QK + GDN_VW), GDN_CONV ** -0.5),
        'gdn_a_log': jnp.log(unif((L, GDN_HEADS), 1.0, 16.0)),
        'gdn_dt_bias': dt + jnp.log(-jnp.expm1(-dt)),
        'gdn_norm': gain((L, GDN_DV)),
        'mla_q_norm': gain((L, MLA_Q_LORA)),
        'mla_w_q_up': nrm((L, MLA_Q_LORA, MLA_HEADS * (MLA_D_NOPE + MLA_D_ROPE)), MLA_Q_LORA ** -0.5),
        'mla_kv_norm': gain((L, MLA_KV_LORA)),
        'mla_w_kv_up': nrm((L, MLA_KV_LORA, MLA_HEADS * (MLA_D_NOPE + MLA_DV)), MLA_KV_LORA ** -0.5),
        'rwkv_mu': unif((L, RWKV_IN), 0.0, 1.0),
        'rwkv_w0': unif((L, RWKV_W), -6.0, 1.0),
        'rwkv_w2': nrm((L, RWKV_DECAY_LORA, RWKV_W), 0.1),
        'rwkv_a0': nrm((L, RWKV_W), 0.1),
        'rwkv_a2': nrm((L, RWKV_A_LORA, RWKV_W), 0.1),
        'rwkv_g2': nrm((L, RWKV_G_LORA, RWKV_W), RWKV_G_LORA ** -0.5),
        'rwkv_k_k': 0.85 + nrm((L, RWKV_W), 0.02),
        'rwkv_k_a': 1.0 + nrm((L, RWKV_W), 0.02),
        'rwkv_r_k': nrm((L, RWKV_HEADS, RWKV_N), 0.1),
        'rwkv_ln_w': gain((L, RWKV_W)),
        'rwkv_ln_b': nrm((L, RWKV_W), 0.01),
        'w_branch': nrm((L, N_BRANCH, BRANCH_W, D), BRANCH_W ** -0.5),
        'w_out': nrm((L, D, D), D ** -0.5),
        'norm_ffn': gain((L, D)),
        'w_router_group': nrm((L, D, N_GROUPS), D ** -0.5),
        'b_router_group': nrm((L, N_GROUPS), 0.01),
        'w_router_expert': nrm((L, D, N_EXPERTS), D ** -0.5),
        'b_router_expert': nrm((L, N_EXPERTS), 0.01),
        'w_exp_gate': nrm((L, N_EXPERTS, D, D_EXPERT), D ** -0.5),
        'w_exp_up': nrm((L, N_EXPERTS, D, D_EXPERT), D ** -0.5),
        'w_exp_down': nrm((L, N_EXPERTS, D_EXPERT, D), D_EXPERT ** -0.5),
        'norm_final': gain((D,)),
    }

def reference(x, meta_tokens, norm_mix, w_in, gdn_conv, gdn_a_log, gdn_dt_bias, gdn_norm,
              mla_q_norm, mla_w_q_up, mla_kv_norm, mla_w_kv_up,
              rwkv_mu, rwkv_w0, rwkv_w2, rwkv_a0, rwkv_a2, rwkv_g2, rwkv_k_k, rwkv_k_a,
              rwkv_r_k, rwkv_ln_w, rwkv_ln_b, w_branch, w_out, norm_ffn,
              w_router_group, b_router_group, w_router_expert, b_router_expert,
              w_exp_gate, w_exp_up, w_exp_down, norm_final):
    B = x.shape[0]
    meta = jnp.broadcast_to(meta_tokens[None].astype(x.dtype), (B, N_META, D_MODEL))
    h = jnp.concatenate([meta, x], axis=1)
    T = h.shape[1]
    pos = jnp.arange(T, dtype=F32)
    inv_freq = ROPE_THETA ** (-jnp.arange(0, MLA_D_ROPE, 2, dtype=F32) / MLA_D_ROPE)
    ang = pos[:, None] * inv_freq[None, :]
    cos, sin = jnp.cos(ang)[:, None, :], jnp.sin(ang)[:, None, :]
    for l in range(DEPTH):
        h = h + hybrid_mixer(
            rmsnorm(h, norm_mix[l]), w_in[l],
            (gdn_conv[l], gdn_a_log[l], gdn_dt_bias[l], gdn_norm[l]),
            (mla_q_norm[l], mla_w_q_up[l], mla_kv_norm[l], mla_w_kv_up[l]),
            (rwkv_mu[l], rwkv_w0[l], rwkv_w2[l], rwkv_a0[l], rwkv_a2[l], rwkv_g2[l],
             rwkv_k_k[l], rwkv_k_a[l], rwkv_r_k[l], rwkv_ln_w[l], rwkv_ln_b[l]),
            w_branch[l], w_out[l], cos, sin)
        h = h + hierarchical_moe(
            rmsnorm(h, norm_ffn[l]), w_router_group[l], b_router_group[l],
            w_router_expert[l], b_router_expert[l], w_exp_gate[l], w_exp_up[l], w_exp_down[l])
    return rmsnorm(h, norm_final)[:, N_META:]


_drawn_inputs = setup_inputs


def setup_inputs(seed=0):
    import zlib

    import numpy as np

    out = dict(_drawn_inputs(seed))
    spreads = {}
    factors = {'gdn_norm': 28.288,
     'mla_q_norm': 8.0,
     'mla_kv_norm': 8.0,
     'rwkv_w2': 3.072,
     'rwkv_a0': 3.051,
     'rwkv_k_k': 64.0,
     'rwkv_k_a': 16.139,
     'rwkv_ln_w': 34.312,
     'rwkv_ln_b': 64.0,
     'b_router_group': 51.358,
     'b_router_expert': 33.553,
     'norm_final': 8.078,
     'norm_ffn': 8.0}
    for name, (base, spread) in spreads.items():
        noise = np.random.default_rng([zlib.crc32(name.encode()), seed]).standard_normal(out[name].shape)
        drawn = base * np.exp(spread * noise) if base else spread * noise
        out[name] = jnp.asarray(drawn.astype(out[name].dtype))
    for name, factor in factors.items():
        out[name] = (out[name] * factor).astype(out[name].dtype)
    return out
```

```python
from contextlib import ExitStack

import numpy as np

import concourse.bass as bass
from concourse import mybir

ALU = mybir.AluOpType
ACT = mybir.ActivationFunctionType
AX = mybir.AxisListType
F32 = mybir.dt.float32
I32 = mybir.dt.int32
U32 = mybir.dt.uint32
ds = bass.ds

D, SEQ, META = 2048, 256, 16
T = SEQ + META
PAD = 16
TP = T + PAD
C = 32
NC = TP // C
KT = D // 128
GH = 8
GQ = GH // 4
RH = 16
RQ = RH // 4
QL, KVL, ROPE, MH = 768, 512, 64, 8
BR = 1024
EPS = 1e-6
RLN_EPS = 64e-5
NE, NG, EPG, DE = 32, 4, 8, 512
CAP = 64
IN0_BA = 4096
IN0_CQ = IN0_BA + 16
IN0_CKV = IN0_CQ + QL
IN0_KPE = IN0_CKV + KVL
IN0_RKV = IN0_KPE + ROPE
IN0_LORA = IN0_RKV + 3 * BR
IN0_GATE = IN0_LORA + 288


class Columns:

    def __init__(self, widths):
        self.at, self.width, n = {}, {}, 0
        for name, w in widths:
            self.at[name], self.width[name] = n, w
            n += w
        self.n = n


PAR = Columns([("norm_mix", 16), ("conv", 96), ("alog", 2), ("dtb", 2), ("gdn_norm", 1), ("qnorm", 6),
               ("kvnorm", 4), ("mu", 24), ("mu_wa", 1), ("mu_g1", 1), ("mu_g2", 1), ("w0", 8), ("a0", 8),
               ("k_k", 8), ("k_a", 8), ("r_k", 8), ("ln_w", 8), ("ln_b", 8)])
CON = Columns([("ident", 128), ("bd_le", 128), ("bd_gt", 128), ("bd_one", 128), ("ones", 128),
               ("one64", 128), ("lt", 128), ("m_le", 32), ("m_gt", 32), ("m4", 128), ("hm", 4), ("rot", 64),
               ("cos", T), ("sin", T), ("causal", T), ("eps", 1), ("rln_eps", 1), ("scan", TP),
               ("iota8", 8), ("iota32", 32), ("slot", 128), ("half", 1), ("trash", 1), ("tok2", 2)])


def constants():
    p = np.arange(128)
    q = np.arange(32)
    out = np.zeros((128, CON.n), np.float32)

    def put(name, a):
        a = np.asarray(a, np.float32).reshape(len(a), -1)
        out[:len(a), CON.at[name]:CON.at[name] + CON.width[name]] = a

    same = (p[:, None] // 32) == (p[None] // 32)
    put("ident", np.eye(128))
    put("bd_le", same & (p[:, None] <= p[None]))
    put("bd_gt", same & (p[:, None] > p[None]))
    put("bd_one", same)
    put("ones", np.ones((128, 128)))
    put("one64", (p[:, None] // 64) == (p[None] // 64))
    put("lt", p[:, None] < p[None])
    le = (p % 32)[:, None] <= q[None]
    gt = (p % 32)[:, None] > q[None]
    lt = (p % 32)[:, None] < q[None]
    put("m_le", le)
    put("m_gt", gt)
    put("m4", np.concatenate([gt, le, lt, le], 1))
    put("hm", (p // 32)[:, None] == np.arange(4)[None])
    rot = np.zeros((64, 64))
    for i in range(32):
        rot[i + 32, i] = -1.0
        rot[i, i + 32] = 1.0
    put("rot", rot)
    inv = np.float32(10000.0) ** (-np.arange(0, 64, 2, dtype=np.float32) / np.float32(64))
    ang = (np.arange(T, dtype=np.float32)[:, None] * inv[None].astype(np.float32)).T
    put("cos", np.concatenate([np.cos(ang)] * 2, 0))
    put("sin", np.concatenate([np.sin(ang)] * 2, 0))
    causal = np.zeros((128, T))
    causal[:, T - 128:] = np.where(p[None] <= p[:, None], 0.0, -1e30)
    put("causal", causal)
    put("eps", np.full((128, 1), EPS))
    put("rln_eps", np.full((128, 1), RLN_EPS))
    put("scan", np.tile((np.arange(TP) % C != 0)[None], (128, 1)))
    put("iota8", np.tile(np.arange(8)[None], (128, 1)))
    put("iota32", np.tile(np.arange(32)[None], (128, 1)))
    put("slot", np.tile((p % CAP)[None], (128, 1)))
    put("half", (p // CAP)[:, None])
    put("trash", 2.0 * (512 + p % CAP)[:, None])
    put("tok2", np.stack([p, 128 + p], 1))
    return out


def per_channel(inputs):
    out = np.zeros((128, PAR.n), np.float32)

    def put(name, a):
        out[:a.shape[0], PAR.at[name]:PAR.at[name] + PAR.width[name]] = a

    def cols(a):
        return np.ascontiguousarray(a.reshape(-1, 128).T)

    put("norm_mix", cols(inputs["norm_mix"][0]))
    put("conv", np.ascontiguousarray(inputs["gdn_conv"][0].reshape(4, 24, 128).transpose(2, 0, 1).reshape(128, 96)))
    put("alog", np.repeat(inputs["gdn_a_log"][0].reshape(2, 4).T, 32, 0))
    put("dtb", np.repeat(inputs["gdn_dt_bias"][0].reshape(2, 4).T, 32, 0))
    put("gdn_norm", inputs["gdn_norm"][0][:, None])
    put("qnorm", cols(inputs["mla_q_norm"][0]))
    put("kvnorm", cols(inputs["mla_kv_norm"][0]))
    mu = inputs["rwkv_mu"][0]
    put("mu", cols(mu[:3072]))
    put("mu_wa", mu[3072:3200, None])
    put("mu_g1", mu[3200:3328, None])
    put("mu_g2", mu[3328:3360, None])
    for name, key in (("w0", "rwkv_w0"), ("a0", "rwkv_a0"), ("k_k", "rwkv_k_k"), ("k_a", "rwkv_k_a"),
                      ("r_k", "rwkv_r_k"), ("ln_w", "rwkv_ln_w"), ("ln_b", "rwkv_ln_b")):
        put(name, cols(inputs[key][0].reshape(-1)))
    return out


N_SMALL, N_QKV, N_QUP, N_KVUP, N_Z, N_RKV, N_LORA = 0, 15, 39, 47, 51, 59, 83
N_MERGE = 86
N_OUT = N_MERGE + 72
M_SMALL, M_QKV, M_QUP, M_KVUP, M_Z, M_RKV, M_LORA = 0, 15, 39, 55, 75, 83, 107
M_MERGE = 131
M_OUT = M_MERGE + 96


def uses_with(n):
    if n < N_QUP:
        return n + 1
    if n < N_KVUP:
        return M_QUP + 2 * (n - N_QUP) + 2
    if n < N_Z:
        return M_KVUP + 5 * (n - N_KVUP) + 5
    if n < N_LORA:
        return M_Z + n - N_Z + 1
    if n < N_MERGE:
        return M_LORA + (16 if n == N_LORA else 24)
    if n < N_OUT:
        pair, what = divmod(n - N_MERGE, 3)
        return M_MERGE + 4 * pair + (4, 1, 3)[what]
    return M_OUT + 2 * ((n - N_OUT) // 2) + 2


BRANCHES = (1, 0, 2)


def program(nc, x, meta, par, con, w_in, w_q_up, w_kv_up, w2, a2, g2, w_branch, w_out,
            norm_ffn, norm_final, w_rg, w_re, b_rg, b_re, e_gate, e_up, e_down, out):
    nc_dram = {}

    def dram(name, shape, dt=F32):
        return nc.dram_tensor(name, shape, dt, kind="Internal").ap()

    gdn_a = dram("gdn_a", [GQ * 4 * NC, C * C])
    gdn_u = dram("gdn_u", [GQ * 4 * NC, C * C])
    rwkv_a = dram("rwkv_a", [RQ * 4 * NC, C * C])
    rwkv_u = dram("rwkv_u", [RQ * 4 * NC, C * C])

    with ExitStack() as ctx:
        def sem(name):
            return ctx.enter_context(nc.semaphore(name))

        arena = ctx.enter_context(nc.sbuf_tensor("arena", [128, 53200], F32))
        psum = [ctx.enter_context(nc.psum_tensor(f"bank{i}", [128, 512], F32)) for i in range(8)]
        place = [0]

        def view(at, *shape):
            n = int(np.prod(shape))
            a = arena[:, at:at + n]
            if len(shape) == 2:
                a = a.rearrange("p (a b) -> p a b", a=shape[0])
            if len(shape) == 3:
                a = a.rearrange("p (a b c) -> p a b c", a=shape[0], b=shape[1])
            if len(shape) == 4:
                a = a.rearrange("p (a b c d) -> p a b c d", a=shape[0], b=shape[1], c=shape[2])
            return a

        def new(*shape):
            at = place[0]
            place[0] += int(np.prod(shape))
            assert place[0] <= 53200, place[0]
            return view(at, *shape)

        CONST = new(CON.n)
        PARAM = new(PAR.n)

        def con_(name, rows=128):
            return CONST[0:rows, CON.at[name]:CON.at[name] + CON.width[name]]

        def par_(name, j=0, rows=128):
            return PARAM[0:rows, PAR.at[name] + j:PAR.at[name] + j + 1]

        ident = con_("ident")
        stats = new(400)
        A_RING = place[0]
        ring = new(4, 2048)
        HT = new(KT, T)
        A_Y = place[0]
        Y = new(3, 8, SEQ)
        A_MG = place[0]
        MG = new(KT, SEQ)
        W0 = place[0]
        Z = ZR = new(8, SEQ)
        CV = new(24, TP)
        AT = new(NC, GQ, C)
        AM = new(NC, GQ, C)
        TT = new(NC, GQ, C)
        DT = new(NC * GQ, C)
        DA = new(NC * GQ, C)
        S = new(8, 128)
        KD = new(2, GQ, 128)
        VB = new(2, GQ, 128)
        R = new(GQ, 128)
        VN = new(GQ, 128)
        O1 = new(GQ, 128)
        GU = view(A_MG + 3072, NC * GQ, C)
        BT = new(NC, 4)
        GS_ = new(8, NC * GQ)
        GL = new(NC * GQ, 4)
        A_SQ = place[0]
        SQ = new(2, TP)
        RN = new(2, TP)
        GM = view(A_SQ, NC * GQ, 4)
        A_RAW = place[0]
        RAW = new(24, TP)
        A_TAIL = place[0]
        CQKV = new(10, T)
        KPE = new(T)
        LR = new(3, TP)
        BA = new(TP)
        KN = view(A_RAW, 8, T)
        VT = view(A_RAW + 8 * T, 3, 1024)
        QN = view(A_Y + 2 * 8 * SEQ, 8, SEQ)
        QPE = view(A_MG, 8, SEQ)
        A_MT = A_MG + 8 * SEQ
        SS = view(A_MT, 2, T)
        PX = view(A_MT + 2 * T, 2, T)
        PT = view(A_MT + 4 * T, 2, 384)
        IA = view(A_MG, 1024)
        IU = view(A_MG + 1024, 1024)
        IT = view(A_MG + 2048, 1024)
        GU2 = view(A_MG + 2048, NC * GQ, C)
        O = view(A_MG, 8, GQ, 128)

        ld = sem("inputs_loaded")
        zeroed = sem("pads_zeroed")
        sq0 = sem("token_squares")
        rt0 = sem("token_roots")
        xn_ready = sem("tokens_normed")
        ht_t = sem("tokens_transposed")
        ht_ready = sem("ht_ready")
        wld = [sem(f"weights_loaded{i}") for i in range(4)]
        pdone = sem("products_done")
        pev = sem("products_evacuated")
        s_csq = sem("latent_squared")
        s_csqf = sem("latent_square_read")
        s_crt = sem("latent_rooted")
        s_cn = sem("latent_normed")
        s_lr = sem("lora_mixed")
        s_conv = sem("conv_done")
        s_rot = sem("rotated_by_pe")
        s_rotd = sem("rotated")
        a_sc, a_sm, a_ex, a_pn = sem("scores"), sem("masked"), sem("exps"), sem("probs")
        a_pt, a_pc, a_o, a_oc = sem("probs_turned"), sem("probs_copied"), sem("heads_out"), sem("heads_kept")

        XT = view(W0, 2, D)
        XM = view(W0 + 2 * D, D)
        XJ = view(W0 + 3 * D, D)

        b_t, b_b, b_c, b_g, b_p = sem("ba_turned"), sem("ba_copied"), sem("ba_functions"), sem("log_decays"), sem("log_decay_sums")
        b_x, b_gt, b_d = sem("decay_exps"), sem("gc_differences"), sem("decays_masked")
        l_sq, l_ss, l_rt, l_n = sem("qk_squared"), sem("qk_sums"), sem("qk_roots"), sem("qk_normed")
        s_silu = sem("conv_silu")
        g_a, g_am = sem("gdn_products"), sem("gdn_a_masked")
        d_aw, d_al, d_inv, d_uw, d_ul = sem("a_stored"), sem("a_loaded"), sem("a_inverted"), sem("inverse_stored"), sem("inverse_loaded")
        k_tok, k_tc, k_ks, k_r, k_vn, k_vc = (sem("gdn_tokens_turned"), sem("gdn_tokens_kept"), sem("state_products"),
                                              sem("gdn_rhs"), sem("v_new"), sem("v_new_kept"))
        k_su, k_s, k_o1, k_oo = sem("state_increments"), sem("state_updated"), sem("state_outputs"), sem("chunk_outputs")
        k_n, k_nr, k_t, k_y = sem("o_squares"), sem("o_roots"), sem("o_normed"), sem("o_turned")
        k_yd = sem("gdn_output")
        raw_free = sem("raw_pads_zeroed_again")
        SCQ = 128.0 ** -0.5
        INC = ((2, 0), (3, 0), (6, 256), (7, 256))
        QK = CV.rearrange("p (a h) t -> p a h t", a=3)

        def grow(j):
            return GS_[:, j, :]

        def pool_gdn(pool):
            pool.wait_ge(g_am, NC)
            for h in range(4):
                pool.dma_start(gdn_a.rearrange("(h c) (t s) -> h t c s", h=4, t=C)[h],
                             AM.rearrange("p c q s -> p (c q) s")[32 * h:32 * h + 32]).then_inc(d_aw, 16)
            pool.wait_ge(d_aw, 64)
            pool.dma_start(IA[0:72], gdn_a).then_inc(d_al, 16)
            pool.wait_ge(d_inv, 1)
            pool.dma_start(gdn_u, IU[0:72]).then_inc(d_uw, 16)
            pool.wait_ge(d_uw, 16)
            for h in range(4):
                pool.dma_start(TT.rearrange("p c q s -> p (c q) s")[32 * h:32 * h + 32],
                             gdn_u.rearrange("(h c) (s t) -> h s c t", h=4, s=C)[h]).then_inc(d_ul, 16)

        def rkv_block(pe, j):
            in_block(pe, N_RKV + j, M_RKV + j)

        def rkv_evac(act, j):
            evac(act, M_RKV + j, RAW[:, j, PAD:TP])

        def pe_gdn(pe):
            pe.wait_ge(a_oc, 16)
            pe.wait_ge(a_pc, 16)
            for c in range(NC):
                for h in range(4):
                    mm = pe.matmul(psum[6][32 * h:32 * h + 32, 4 * c:4 * c + 4], BA[0:16, C * c:C * c + C],
                                   ident[0:16, h:16:4], start=True, stop=True, tile_position=(0, 32 * h))
            mm.then_inc(b_t, 1)
            pe.wait_ge(b_g, 1)
            g = grow(1)
            pe.matmul(psum[6][:, 64:82], con_("bd_le"), g, start=True, stop=True)
            pe.matmul(psum[6][:, 96:114], con_("bd_one"), g, start=True, stop=True)
            pe.matmul(psum[6][:, 128:200], con_("ones"), GM.rearrange("p a b -> p (a b)"), start=True, stop=True).then_inc(b_p, 1)
            GUf = GU.rearrange("p a b -> p (a b)")
            for a in range(2):
                mm = pe.matmul(psum[4 + a][:, 0:288], con_("bd_gt"), GUf[:, 288 * a:288 * a + 288], start=True, stop=True)
            mm.then_inc(b_p, 1)
            pe.wait_ge(b_g, 2)
            GUf = GU2.rearrange("p a b -> p (a b)")
            pe.matmul(psum[7][:, 0:288], con_("bd_le"), GUf[:, 0:288], start=True, stop=True).then_inc(b_p, 1)
            pe.wait_ge(b_x, 2)
            pe.matmul(psum[4][:, 0:288], con_("bd_le"), GUf[:, 288:576], start=True, stop=True).then_inc(b_p, 1)
            for i in range(16):
                pe.wait_ge(l_sq, i + 1)
                if i == 0:
                    pe.wait_ge(b_x, 4)
                if i >= 2:
                    pe.wait_ge(l_rt, i - 1)
                pe.matmul(psum[4 + i % 2][:, 0:TP], con_("ones"), SQ[:, i % 2, :], start=True, stop=True).then_inc(l_ss, 1)
                if i % 4 == 3:
                    rkv_block(pe, i // 4)
            pe.wait_ge(l_n, 16)
            for c in range(NC):
                if c >= 2:
                    pe.wait_ge(g_am, c - 1)
                for h in range(8):
                    mm = pe.matmul(psum[4 + c % 2][32 * (h % 4):32 * (h % 4) + 32, 64 * (h // 4):64 * (h // 4) + 64],
                                   QK[:, 1, h, C * c:C * c + C], QK[:, 0:2, h, C * c:C * c + C],
                                   start=True, stop=True, tile_position=(0, 32 * (h % 4)))
                mm.then_inc(g_a, 1)
            for j in range(4, 13):
                rkv_block(pe, j)

            def tokens(c):
                if c:
                    pe.wait_ge(k_tc, c)
                for a in range(2):
                    for h in range(8):
                        at = 256 * a + 128 * (h // 4)
                        mm = pe.matmul(psum[4][32 * (h % 4):32 * (h % 4) + 32, at:at + 128], QK[:, 1 + a, h, C * c:C * c + C],
                                       ident, start=True, stop=True, tile_position=(0, 32 * (h % 4)))
                mm.then_inc(k_tok, 1)

            pe.wait_ge(g_am, NC)
            tokens(0)
            pe.wait_ge(d_ul, 64)
            for c in range(NC):
                if c:
                    pe.wait_ge(k_s, c)
                    if c > 1:
                        pe.wait_ge(k_o1, c - 1)
                    for a in range(2):
                        for h in range(8):
                            at = 256 * a + 128 * (h // 4)
                            mm = pe.matmul(psum[5][32 * (h % 4):32 * (h % 4) + 32, at:at + 128],
                                           QK[:, 1 - a, h, C * c:C * c + C], S[:, h, :],
                                           start=True, stop=True, tile_position=(0, 32 * (h % 4)))
                    mm.then_inc(k_ks, 1)
                pe.wait_ge(k_r, c + 1)
                for h in range(8):
                    p = slice(32 * (h % 4), 32 * (h % 4) + 32)
                    at = 128 * (h // 4)
                    mm = pe.matmul(psum[6][p, at:at + 128], TT[p, c, h // 4, :], R[p, h // 4, :], start=True, stop=True,
                                   tile_position=(32 * (h % 4), 32 * (h % 4)))
                mm.then_inc(k_vn, 1)
                if c + 1 < NC:
                    tokens(c + 1)
                pe.wait_ge(k_vc, c + 1)
                for h in range(8):
                    p = slice(32 * (h % 4), 32 * (h % 4) + 32)
                    b, at = INC[h % 4]
                    mm = pe.matmul(psum[b][:, at + 128 * (h // 4):at + 128 * (h // 4) + 128], KD[p, c % 2, h // 4, :], VN[p, h // 4, :],
                                   start=True, stop=True, tile_position=(32 * (h % 4), 0))
                mm.then_inc(k_su, 1)
                if c:
                    if c > 1:
                        pe.wait_ge(k_oo, c - 1)
                    for h in range(8):
                        p = slice(32 * (h % 4), 32 * (h % 4) + 32)
                        at = 128 * (h // 4)
                        mm = pe.matmul(psum[7][p, at:at + 128], AT[p, c, h // 4, :], VN[p, h // 4, :], start=True, stop=True,
                                       tile_position=(32 * (h % 4), 32 * (h % 4)))
                    mm.then_inc(k_t, 1)
                rkv_block(pe, 13 + c)
            rkv_block(pe, 22)
            rkv_block(pe, 23)
            pe.wait_ge(k_n, 3)
            for g in range(4):
                if g >= 2:
                    pe.wait_ge(k_yd, g - 1)
                for j in range(4):
                    mm = pe.transpose(psum[4 + g % 2][:, 128 * j:128 * j + 128], O[:, 2 * g + j // 2, j % 2, :], ident)
                mm.then_inc(k_y, 1)

        def act_gdn(act):
            act.wait_ge(s_conv, 24)
            act.activation(Z, ZR, ACT.Silu)
            for a in range(3):
                act.activation(CV[:, 8 * a:8 * a + 8, PAD:TP], CV[:, 8 * a:8 * a + 8, PAD:TP], ACT.Silu)
            act.drain().then_inc(s_silu, 1)
            act.wait_ge(b_b, 1)
            act.activation(grow(0).rearrange("p (c q) -> p c q", c=NC), BT[:, :, 0:2], ACT.Sigmoid)
            act.activation(grow(7), grow(6), ACT.Abs)
            act.activation(stats[:, 20:22], PARAM[:, PAR.at["alog"]:PAR.at["alog"] + 2], ACT.Exp)
            act.drain()
            act.activation(grow(7), grow(7), ACT.Exp, scale=-1.0)
            act.drain()
            act.activation(grow(7), grow(7), ACT.Ln, bias=con_("ones")[:, 0:1])
            act.drain().then_inc(b_c, 1)
            act.wait_ge(b_gt, 1)
            act.activation(grow(5), grow(2), ACT.Exp)
            act.activation(grow(3), grow(3), ACT.Exp)
            act.activation(GL.rearrange("p a b -> p (a b)"), psum[6][:, 128:200], ACT.Exp)
            act.drain().then_inc(b_x, 1)
            act.wait_ge(b_p, 2)
            for a in range(2):
                act.activation(DT[:, 9 * a:9 * a + 9, :], psum[4 + a][:, 0:288].rearrange("p (a b) -> p a b", a=9), ACT.Exp)
            act.drain().then_inc(b_x, 1)
            act.wait_ge(b_p, 3)
            act.activation(DA[:, 0:9, :], psum[7][:, 0:288].rearrange("p (a b) -> p a b", a=9), ACT.Exp).then_inc(b_x, 1)
            act.wait_ge(b_p, 4)
            act.activation(DA[:, 9:18, :], psum[4][:, 0:288].rearrange("p (a b) -> p a b", a=9), ACT.Exp).then_inc(b_x, 1)
            act.drain()
            for i in range(17):
                if i < 16:
                    if i >= 2:
                        act.wait_ge(l_ss, i - 1)
                    act.activation(SQ[:, i % 2, :], CV[:, i, :], ACT.Square).then_inc(l_sq, 1)
                if i:
                    act.wait_ge(l_ss, i)
                    if i > 2:
                        act.wait_ge(l_n, i - 2)
                    act.activation(RN[:, (i - 1) % 2, :], psum[4 + (i - 1) % 2][:, 0:TP], ACT.Sqrt, bias=con_("eps")).then_inc(l_rt, 1)
                    if i % 4 == 0:
                        act.wait_ge(raw_free, 1)
                        rkv_evac(act, i // 4 - 1)
            for j in range(4, 13):
                rkv_evac(act, j)

            def keep(c):
                act.wait_ge(k_tok, c + 1)
                if c >= 2:
                    act.wait_ge(k_su, c - 1)
                    act.wait_ge(k_r, c - 1)
                for q in range(GQ):
                    act.activation(KD[:, c % 2, q, :], psum[4][:, 128 * q:128 * q + 128], ACT.Copy,
                                   scale=grow(3)[:, 2 * c + q:2 * c + q + 1])
                    act.activation(VB[:, c % 2, q, :], psum[4][:, 256 + 128 * q:384 + 128 * q], ACT.Copy,
                                   scale=grow(0)[:, 2 * c + q:2 * c + q + 1])
                act.drain().then_inc(k_tc, 1)

            keep(0)
            for c in range(NC):
                act.wait_ge(k_vn, c + 1)
                if c:
                    act.wait_ge(k_su, c)
                    if c > 1:
                        act.wait_ge(k_t, c - 1)
                act.activation(VN.rearrange("p a b -> p (a b)"), psum[6][:, 0:256], ACT.Copy).then_inc(k_vc, 1)
                if c:
                    if c > 1:
                        act.wait_ge(k_oo, c - 1)
                    for q in range(GQ):
                        act.activation(O1[:, q, :], psum[5][:, 256 + 128 * q:384 + 128 * q], ACT.Copy,
                                       scale=grow(5)[:, 2 * c + q:2 * c + q + 1])
                    act.drain().then_inc(k_o1, 1)
                if c + 1 < NC:
                    keep(c + 1)
                rkv_evac(act, 13 + c)
            rkv_evac(act, 22)
            rkv_evac(act, 23)
            act.wait_ge(k_n, 1)
            act.activation(stats[:, 40:56], stats[:, 24:40], ACT.Sqrt, scale=1.0 / 128, bias=con_("eps")).then_inc(k_nr, 1)

        def invert(v, A, U, tmp, z):
            for t in range(1, C):
                a = A[:, :, t, 0:t].unsqueeze(2).broadcast_to([72, z, t, t])
                w = tmp[:, 0:z * t * t].rearrange("p (z s k) -> p z s k", z=z, s=t)
                if z == 1:
                    v.tensor_tensor(w[:, 0], U[:, 0, 0:t, 0:t], a[:, 0], ALU.mult)
                else:
                    for y in range(z):
                        v.tensor_tensor(w[:, y], U[:, y, 0:t, 0:t], a[:, y], ALU.mult)
                v.drain()
                for y in range(z):
                    v.tensor_reduce(U[:, y, 0:t, t:t + 1], w[:, y], AX.X, ALU.add)
                v.drain()

        def unit(v, U, z):
            v.memset(U, 0.0)
            v.drain()
            v.memset(U.rearrange("p (z a) -> p z a", z=z)[:, :, 0:C * C:C + 1], 1.0)
            v.drain()

        def v_gdn(v):
            v.wait_ge(a_oc, 16)
            v.memset(RAW[:, :, 0:PAD], 0.0).then_inc(raw_free, 1)
            v.wait_ge(b_t, 1)
            v.tensor_copy(BT.rearrange("p a b -> p (a b)"), psum[6][:, 0:36])
            v.drain()
            dtb = PARAM[:, PAR.at["dtb"]:PAR.at["dtb"] + 2].unsqueeze(1).broadcast_to([128, NC, 2])
            v.tensor_tensor(grow(6).rearrange("p (c q) -> p c q", c=NC), BT[:, :, 2:4], dtb, ALU.add).then_inc(b_b, 1)
            v.wait_ge(b_c, 1)
            v.scalar_tensor_tensor(grow(7), grow(6), 0.0, grow(7), ALU.max, ALU.add)
            v.drain()
            ea = stats[:, 20:22].unsqueeze(1).broadcast_to([128, NC, 2])
            v.scalar_tensor_tensor(grow(1).rearrange("p (c q) -> p c q", c=NC), grow(7).rearrange("p (c q) -> p c q", c=NC),
                                   -1.0, ea, ALU.mult, ALU.mult)
            v.drain()
            n = NC * GQ
            g4 = grow(1).unsqueeze(2)
            v.tensor_tensor(GM, g4.broadcast_to([128, n, 4]), con_("hm").unsqueeze(1).broadcast_to([128, n, 4]), ALU.mult)
            v.tensor_tensor(GU, g4.broadcast_to([128, n, C]), con_("m_le").unsqueeze(1).broadcast_to([128, n, C]), ALU.mult)
            v.drain().then_inc(b_g, 1)
            v.tensor_tensor(GU2, g4.broadcast_to([128, n, C]), con_("m_gt").unsqueeze(1).broadcast_to([128, n, C]), ALU.mult).then_inc(b_g, 1)
            v.wait_ge(b_p, 1)
            v.tensor_copy(grow(2), psum[6][:, 64:82])
            v.drain()
            v.tensor_tensor(grow(3), psum[6][:, 96:114], grow(2), ALU.subtract)
            v.drain().then_inc(b_gt, 1)
            v.wait_ge(b_x, 4)
            v.scalar_tensor_tensor(grow(4), grow(0), -1.0, grow(5), ALU.mult, ALU.mult)
            v.scalar_tensor_tensor(DT, DT, SCQ, con_("m_le").unsqueeze(1).broadcast_to([128, n, C]), ALU.mult, ALU.mult)
            v.scalar_tensor_tensor(DA, DA, -1.0, con_("m_gt").unsqueeze(1).broadcast_to([128, n, C]), ALU.mult, ALU.mult)
            v.drain()
            v.tensor_scalar(grow(5), grow(5), SCQ, None, ALU.mult)
            v.tensor_tensor(DA, DA, grow(0).unsqueeze(2).broadcast_to([128, n, C]), ALU.mult)
            v.drain()
            for i in range(16):
                v.wait_ge(l_rt, i + 1)
                v.reciprocal(RN[:, i % 2, :], RN[:, i % 2, :])
                v.drain()
                v.tensor_tensor(CV[:, i, :], CV[:, i, :], RN[:, i % 2, :], ALU.mult).then_inc(l_n, 1)
            unit(v, IU[0:72], 1)
            for c in range(NC):
                v.wait_ge(g_a, c + 1)
                b = psum[4 + c % 2][:, 0:128].rearrange("p (q a t) -> p q a t", q=2, a=2)
                v.tensor_tensor(AT[:, c], b[:, :, 0], DT[:, 2 * c:2 * c + 2], ALU.mult)
                v.tensor_tensor(AM[:, c], b[:, :, 1], DA[:, 2 * c:2 * c + 2], ALU.mult)
                v.drain().then_inc(g_am, 1)
            v.wait_ge(d_al, 16)
            invert(v, IA[0:72].rearrange("p (z t s) -> p z t s", z=1, t=C), IU[0:72].rearrange("p (z s t) -> p z s t", z=1, s=C),
                   IT[0:72], 1)
            v.drain().then_inc(d_inv, 1)
            for c in range(NC):
                v.wait_ge(k_tc, c + 1)
                if c:
                    v.wait_ge(k_ks, c)
                    v.wait_ge(k_vn, c)
                    for q in range(GQ):
                        v.scalar_tensor_tensor(R[:, q, :], psum[5][:, 128 * q:128 * q + 128], grow(4)[:, 2 * c + q:2 * c + q + 1],
                                               VB[:, c % 2, q, :], ALU.mult, ALU.add)
                else:
                    v.tensor_copy(R, VB[:, 0])
                v.drain().then_inc(k_r, 1)
                v.wait_ge(k_su, c + 1)
                if c:
                    for h in (0, 4, 1, 5, 2, 6, 3, 7):
                        b, at = INC[h % 4]
                        if h == 3:
                            v.wait_ge(k_t, c)
                        v.scalar_tensor_tensor(S[:, h, :], S[:, h, :], GL[:, 2 * c + h // 4, h % 4:h % 4 + 1],
                                               psum[b][:, at + 128 * (h // 4):at + 128 * (h // 4) + 128], ALU.mult, ALU.add)
                else:
                    for a in range(4):
                        b, at = INC[a]
                        v.tensor_copy(S[:, a:8:4, :], psum[b][:, at:at + 256].rearrange("p (a b) -> p a b", a=2))
                v.drain().then_inc(k_s, 1)
                if c:
                    v.wait_ge(k_o1, c)
                    v.tensor_tensor(O[:, c - 1], psum[7][:, 0:256].rearrange("p (a b) -> p a b", a=2), O1, ALU.add).then_inc(k_oo, 1)
            v.drain()
            O3, Q3 = O.rearrange("p c q n -> p (c q) n"), view(A_MG + 2048, 16, 128)
            v.tensor_tensor(Q3, O3, O3, ALU.mult)
            v.drain()
            v.tensor_reduce(stats[:, 24:40].unsqueeze(2), Q3, AX.X, ALU.add)
            v.drain().then_inc(k_n, 1)
            v.wait_ge(k_nr, 1)
            v.reciprocal(stats[:, 40:56], stats[:, 40:56])
            v.drain()
            v.tensor_tensor(O3, O3, stats[:, 40:56].unsqueeze(2).broadcast_to([128, 16, 128]), ALU.mult)
            v.drain().then_inc(k_n, 2)
            for g in range(4):
                v.wait_ge(k_y, g + 1)
                for j in range(4):
                    c, q = 2 * g + j // 2, j % 2
                    v.scalar_tensor_tensor(Y[:, 0, 4 * q:4 * q + 4, C * c:C * c + C],
                                           psum[4 + g % 2][:, 128 * j:128 * j + 128].rearrange("p (h t) -> p h t", h=4), par_("gdn_norm"),
                                           Z[:, 4 * q:4 * q + 4, C * c:C * c + C], ALU.mult, ALU.mult)
                v.drain().then_inc(k_yd, 1)

        CW = float(np.exp(-0.5))
        XR = view(W0, 3, 8, TP)
        XR24 = view(W0, 24, TP)
        SG = view(W0 + 24 * TP, 8, TP)
        CS = view(W0 + 32 * TP, 8, TP)
        RA = view(W0 + 40 * TP, 8, TP)
        RG = view(W0 + 48 * TP, 8, SEQ)
        PC = view(W0 + 48 * TP + 8 * SEQ, 8, NC)
        assert W0 + 48 * TP + 8 * SEQ + 8 * NC <= A_RAW
        T1, T2, T3 = (view(A_RAW + 8 * TP * i, 8, TP) for i in range(3))
        BON = Y[:, 2]
        BPR = view(W0 + 32 * TP, 8, SEQ)
        GB = view(A_TAIL, 2, SEQ)
        BB = view(A_TAIL + 512, 2, SEQ)
        IT2 = view(A_TAIL + 1024, 2 * 31 * 31)
        YO = view(A_TAIL + 1024, NC - 1, RQ, 64)
        AM4 = view(W0 + 32 * TP, NC, RQ, 128)
        IA2, IU2 = view(A_RAW, 2 * C * C), view(A_RAW + 8 * TP, 2 * C * C)
        TT2 = view(A_RAW, NC, RQ, C)
        SR = view(A_RAW + 1152, RQ, 64)
        SK = view(A_RAW + 1408, RQ, 64)
        RS = view(A_RAW + 1664, 8, 64)
        BK = view(A_RAW + 8 * TP, 2, RQ, 2, 64)
        VV = view(A_RAW + 8 * TP + 1024, 2, RQ, 64)
        YD = view(W0 + 16 * TP, 32, 64)
        YT = view(A_RAW + 8 * TP, 8, SEQ)
        RK = arena[:, W0:W0 + 48 * TP].rearrange("p (a h t) -> p a h t", a=2, h=24)[:, :, 0:8, :]
        H2 = view(A_RING + 8192, 2, D)

        r_lr, r_mix = sem("lora_inputs"), sem("rkv_mixed")
        r_ksq, r_kss, r_krt = sem("kk_squared"), sem("kk_sums"), sem("kk_roots")
        r_bin, r_bs, r_bd = sem("bonus_inputs"), sem("bonus_sums"), sem("bonus_done")
        r_cs, r_ex, r_el = sem("decay_sums"), sem("decay_factors"), sem("rwkv_operands")
        r_a, r_am = sem("rwkv_products"), sem("rwkv_products_masked")
        q_aw, q_al, q_inv, q_uw, q_ul = (sem("rwkv_a_stored"), sem("rwkv_a_loaded"), sem("rwkv_a_inverted"),
                                         sem("rwkv_inverse_stored"), sem("rwkv_inverse_loaded"))
        r_tok, r_tk, r_s0, r_sr, r_sa, r_ss = (sem("rwkv_tokens_turned"), sem("rwkv_tokens_kept"), sem("sa_rhs"),
                                               sem("sa_rhs_kept"), sem("sa_solved"), sem("sa_kept"))
        r_up, r_st, r_yo, r_yp = sem("rwkv_increments"), sem("rwkv_state"), sem("rwkv_chunk_kept"), sem("rwkv_chunk_out")
        r_yn, r_yt, r_v1, r_v2, r_y = sem("y_normed"), sem("y_turned"), sem("y_variance"), sem("y_root"), sem("rwkv_output")
        mg_in, mg_done = sem("merge_inputs"), sem("merged")
        xh, h2s = sem("residual_loaded"), sem("residual_added")

        U_SUMS, U_EXPS, U_PREP, U_CHAIN = 4, 7, 10, 20
        FILL = [U_CHAIN + 2 * c if c < 3 else U_CHAIN + 3 + c for c in range(NC)]
        FILL2 = [U_CHAIN + 2 * c + 1 if c < 3 else None for c in range(NC)]

        def half(h):
            return slice(64 * (h % 2), 64 * (h % 2) + 64)

        def quad(h):
            return slice(32 * (h % 4), 32 * (h % 4) + 32)

        def sp_rest(sp, load):
            load(N_LORA, w2, ring[0:64, N_LORA % 4, 0:BR])
            sp.dma_start(ring[64:128, N_LORA % 4, 0:BR], a2).then_inc(wld[N_LORA % 4], 16)
            load(N_LORA + 1, g2[0:128], ring[:, (N_LORA + 1) % 4, 0:BR])
            load(N_LORA + 2, g2[128:160], ring[0:32, (N_LORA + 2) % 4, 0:BR])
            win = w_in.rearrange("(k p) n -> p k n", p=128)

            def merge_loads(turn, s):
                b = BRANCHES[turn]
                wb = w_branch[b].rearrange("(k p) n -> p k n", p=128)
                for pair in range(4):
                    n = N_MERGE + 24 * turn + 12 * s + 3 * pair
                    at = BR * s + 256 * pair
                    load_w(n, wb[:, :, at:at + 256], 8, 256)
                    for j in range(2):
                        load_w(n + 1 + j, win[:, :, IN0_GATE + D * b + at + 128 * j:IN0_GATE + D * b + at + 128 * (j + 1)], 16, 128)

            def load_w(n, src, k, width):
                load(n, src, ring[:, n % 4, :].rearrange("p (k n) -> p k n", k=k))

            for turn in range(3):
                for s in range(2):
                    merge_loads(turn, s)
            wo = w_out.rearrange("(k p) n -> p k n", p=128)
            for p in range(8):
                n = N_OUT + 2 * p
                sp.wait_ge(pdone, uses_with(n - 3))
                for a in range(2):
                    sp.dma_start(ring[:, (n + a) % 4, :].rearrange("p (k n) -> p k n", k=8),
                                 wo[:, 8 * a:8 * a + 8, 256 * p:256 * (p + 1)]).then_inc(wld[(n + a) % 4], 16)
                if p == 0:
                    sp.wait_ge(pdone, M_OUT)
                    sp.dma_start(H2, x.rearrange("(a p) d -> p a d", a=2)).then_inc(xh, 16)
            if STOP == "mix":
                return
            sp_moe(sp)

        def pe_rest(pe):
            pe.wait_ge(r_lr, 1)
            n = N_LORA
            pe.wait_ge(wld[n % 4], 16 * (n // 4 + 1) + 16)
            m = M_LORA
            for p, rows in ((slice(0, 64), 0), (slice(64, 128), 64)):
                for j in range(8):
                    pe.wait_ge(pev, m - 1)
                    pe.matmul(psum[m % 2][:, 0:T], ring[p, n % 4, 128 * j:128 * (j + 1)], LR[p, 0, PAD:TP],
                              start=True, stop=True, tile_position=(rows, 0)).then_inc(pdone, 1)
                    m += 1
            weights1(pe, n + 1)
            weights1(pe, n + 2)
            for j in range(8):
                dense(pe, m, [(128, SEQ, ring[:, (n + 1) % 4, 128 * j:128 * (j + 1)], LR[:, 1, PAD + META:TP], True, False),
                              (128, SEQ, ring[0:32, (n + 2) % 4, 128 * j:128 * (j + 1)], LR[0:32, 2, PAD + META:TP], False, True)])
                m += 1
            for u in range(U_SUMS):
                merge_block(pe, u)
            for i in range(8):
                pe.wait_ge(r_ksq, 1)
                if i >= 2:
                    pe.wait_ge(r_krt, i - 1)
                pe.matmul(psum[4 + i % 2][:, 0:TP], con_("one64"), T2[:, i, :], start=True, stop=True).then_inc(r_kss, 1)
            for i in range(8):
                pe.wait_ge(r_bin, 1)
                if i >= 2:
                    pe.wait_ge(r_bd, i - 1)
                pe.matmul(psum[6 + i % 2][:, 0:SEQ], con_("one64"), BPR[:, i, :], start=True, stop=True).then_inc(r_bs, 1)
            for u in range(U_SUMS, U_PREP):
                merge_block(pe, u)
            pe.wait_ge(r_el, 1)
            for c in range(NC):
                if c >= 2:
                    pe.wait_ge(r_am, c - 1)
                t = slice(C * c, C * c + C)
                for h in range(RH):
                    i, at, b = h // 2, 128 * (h // 4), psum[4 + c % 2]
                    tp = (64 * (h % 2), 32 * (h % 4))
                    pe.matmul(b[quad(h), at:at + 32], SG[half(h), i, t], T3[half(h), i, t], start=True, stop=True, tile_position=tp)
                    pe.matmul(b[quad(h), at + 32:at + 96], XR[half(h), 1, i, t], RK[half(h), :, i, t],
                              start=True, stop=True, tile_position=tp)
                    mm = pe.matmul(b[quad(h), at + 96:at + 128], T3[half(h), i, t], XR[half(h), 0, i, t],
                                   start=True, stop=True, tile_position=tp)
                mm.then_inc(r_a, 1)
            for u in range(U_PREP, U_CHAIN):
                merge_block(pe, u)

            def tokens(c):
                if c:
                    pe.wait_ge(r_tk, c)
                    pe.wait_ge(r_st, c)
                t = slice(C * c, C * c + C)
                for h in range(RH):
                    i, q = h // 2, h // 4
                    for j, src in enumerate((T3[half(h), i, t], XR[half(h), 1, i, t], XR[half(h), 2, i, t])):
                        b, at = (psum[4], 128 * q + 64 * j) if j < 2 else (psum[5], 64 * q)
                        mm = pe.matmul(b[quad(h), at:at + 64], src, ident[half(h), half(h)], start=True, stop=True,
                                       tile_position=(64 * (h % 2), 32 * (h % 4)))
                mm.then_inc(r_tok, 1)

            pe.wait_ge(r_am, NC)
            tokens(0)
            pe.wait_ge(q_ul, 64)
            for c in range(NC):
                t = slice(C * c, C * c + C)
                pe.wait_ge(r_tk, c + 1)
                if c:
                    pe.wait_ge(r_st, c)
                for h in range(RH):
                    q, o = h // 4, psum[6][quad(h), 64 * (h // 4):64 * (h // 4) + 64]
                    if c:
                        pe.matmul(o, SG[half(h), h // 2, t], RS[half(h), h // 2, :], start=h < 4, stop=False,
                                  tile_position=(64 * (h % 2), 32 * (h % 4)), skip_group_check=True)
                for h in range(RH):
                    q, o = h // 4, psum[6][quad(h), 64 * (h // 4):64 * (h // 4) + 64]
                    mm = pe.matmul(o, AM4[quad(h), c, q, 64:96], VV[quad(h), c % 2, q, :], start=not c and h < 4, stop=True,
                                   tile_position=(32 * (h % 4), 32 * (h % 4)), skip_group_check=True)
                mm.then_inc(r_s0, 1)
                merge_block(pe, FILL[c])
                pe.wait_ge(r_sr, c + 1)
                for h in range(RH):
                    q = h // 4
                    mm = pe.matmul(psum[6][quad(h), 256 + 64 * q:320 + 64 * q], TT2[quad(h), c, q, :], SR[quad(h), q, :],
                                   start=True, stop=True, tile_position=(32 * (h % 4), 32 * (h % 4)))
                mm.then_inc(r_sa, 1)
                if FILL2[c] is not None:
                    merge_block(pe, FILL2[c])
                pe.wait_ge(r_ss, c + 1)
                for j, (what, src) in enumerate(((0, SK), (1, None))):
                    for h in range(RH):
                        q = h // 4
                        rhs = SK[quad(h), q, :] if j == 0 else VV[quad(h), c % 2, q, :]
                        mm = pe.matmul(psum[5 + 2 * ((h % 4) // 2)][half(h), 256 + 64 * q:320 + 64 * q],
                                       BK[quad(h), c % 2, q, j, :], rhs, start=j == 0 and h < 4, stop=j == 1,
                                       tile_position=(32 * (h % 4), 64 * (h % 2)), skip_group_check=True)
                mm.then_inc(r_up, 1)
                if c:
                    if c > 1:
                        pe.wait_ge(r_yo, c - 1)
                    for h in range(RH):
                        o = psum[2][quad(h), 64 * (h // 4):64 * (h // 4) + 64]
                        pe.matmul(o, XR[half(h), 0, h // 2, t], RS[half(h), h // 2, :], start=h < 4, stop=False,
                                  tile_position=(64 * (h % 2), 32 * (h % 4)), skip_group_check=True)
                    for h in range(RH):
                        q, o = h // 4, psum[2][quad(h), 64 * (h // 4):64 * (h // 4) + 64]
                        pe.matmul(o, AM4[quad(h), c, q, 32:64], VV[quad(h), c % 2, q, :], start=False, stop=False,
                                  tile_position=(32 * (h % 4), 32 * (h % 4)), skip_group_check=True)
                        mm = pe.matmul(o, AM4[quad(h), c, q, 96:128], SK[quad(h), q, :], start=False, stop=True,
                                       tile_position=(32 * (h % 4), 32 * (h % 4)), skip_group_check=True)
                    mm.then_inc(r_yp, 1)
                if c + 1 < NC:
                    tokens(c + 1)
            pe.wait_ge(r_yn, 1)
            for g in range(2):
                for c in range(4 * g, 4 * g + 4):
                    for h in range(RH):
                        mm = pe.matmul(psum[4 + 2 * g + (h % 4) // 2][half(h), 128 * (c % 4) + 32 * (h // 4):128 * (c % 4) + 32 * (h // 4) + 32],
                                       YD[quad(h), 4 * c + h // 4, :], ident[quad(h), quad(h)], start=True, stop=True,
                                       tile_position=(32 * (h % 4), 64 * (h % 2)))
                mm.then_inc(r_yt, 1)
            pe.wait_ge(r_y, 1)
            for u in range(32, 48):
                merge_block(pe, u)
            pe.wait_ge(mg_done, 48)
            for p in range(8):
                n = N_OUT + 2 * p
                weights1(pe, n)
                weights1(pe, n + 1)
                w = ring[:, n % 4:n % 4 + 2, :].rearrange("p s (k n) -> p (s k) n", k=8)
                for a in range(2):
                    m = M_OUT + 2 * p + a
                    if m < M_OUT + 2:
                        pe.wait_ge(pev, m - 1)
                    else:
                        pe.wait_ge(h2s, m - 1 - M_OUT)
                    for k in range(KT):
                        mm = pe.matmul(psum[m % 2][:, 0:256], MG[:, k, 128 * a:128 * (a + 1)], w[:, k, :], start=k == 0, stop=k == KT - 1)
                    mm.then_inc(pdone, 1)
            if STOP == "mix":
                return
            pe_moe(pe)

        def weights1(eng, n):
            eng.wait_ge(wld[n % 4], 16 * (n // 4 + 1) + (16 if n % 4 == N_LORA % 4 else 0))

        def merge_block(pe, u):
            turn, blk = divmod(u, 16)
            b = BRANCHES[turn]
            pair, j = divmod(blk, 2)
            n = N_MERGE + 24 * turn + 3 * pair
            m = M_MERGE + 2 * u
            weights1(pe, n + 1 + j)
            wg = ring[:, (n + 1 + j) % 4, :].rearrange("p (k n) -> p k n", k=KT)
            dense(pe, m, [(128, SEQ, wg[:, k, :], HT[:, k, META:T], k == 0, k == KT - 1) for k in range(KT)])
            weights1(pe, n)
            wb = ring[:, n % 4, :].rearrange("p (k n) -> p k n", k=8)
            dense(pe, m + 1, [(128, SEQ, wb[:, k, 128 * j:128 * (j + 1)], Y[:, b, k, :], k == 0, k == 7) for k in range(8)])

        def merge_evac(act, u):
            m = M_MERGE + 2 * u
            if u >= 2:
                act.wait_ge(mg_done, u - 1)
            evac(act, m, GB[:, u % 2, :], ACT.Sigmoid, cols=SEQ)
            evac(act, m + 1, BB[:, u % 2, :], cols=SEQ)

        def act_rest(act):
            act.wait_ge(s_lr, 1)
            act.activation(LR[0:64, 0, PAD:TP], LR[0:64, 0, PAD:TP], ACT.Tanh)
            act.activation(LR[:, 1, PAD:TP], LR[:, 1, PAD:TP], ACT.Sigmoid)
            act.activation(LR[0:32, 2, PAD:TP], LR[0:32, 2, PAD:TP], ACT.Sigmoid)
            act.drain().then_inc(r_lr, 1)
            act.wait_ge(k_yd, 4)
            m = M_LORA
            for dst, bias in ((SG, "w0"), (RA, "a0")):
                for j in range(8):
                    evac(act, m, dst[:, j, PAD:TP], ACT.Sigmoid, bias=par_(bias, j))
                    m += 1
            for j in range(8):
                evac(act, m, RG[:, j, :], cols=SEQ)
                m += 1
            for u in range(U_SUMS):
                merge_evac(act, u)
            for i in range(8):
                act.wait_ge(r_kss, i + 1)
                act.activation(T3[:, i, :], psum[4 + i % 2][:, 0:TP], ACT.Sqrt, bias=con_("eps")).then_inc(r_krt, 1)
            for u in range(U_SUMS, U_EXPS):
                merge_evac(act, u)
            act.wait_ge(r_cs, 1)
            act.activation(T3, T3, ACT.Exp, scale=-CW)
            act.activation(T2, CS, ACT.Exp, scale=-CW)
            act.drain()
            act.activation(CS, CS, ACT.Exp, scale=CW)
            act.drain().then_inc(r_ex, 1)
            for u in range(U_EXPS, U_CHAIN):
                merge_evac(act, u)

            def keep(c):
                act.wait_ge(r_tok, c + 1)
                if c == 0:
                    act.wait_ge(q_uw, 16)
                if c >= 2:
                    act.wait_ge(r_up, c - 1)
                    act.wait_ge(r_yp, c - 2) if c > 2 else None
                act.activation(BK[:, c % 2], psum[4][:, :].rearrange("p (q a n) -> p q a n", q=4, a=2), ACT.Copy)
                act.activation(VV[:, c % 2], psum[5][:, 0:256].rearrange("p (q n) -> p q n", q=4), ACT.Copy)
                act.drain().then_inc(r_tk, 1)

            keep(0)
            for c in range(NC):
                act.wait_ge(r_s0, c + 1)
                if c == 0:
                    act.wait_ge(q_inv, 1)
                act.activation(SR.rearrange("p a b -> p (a b)"), psum[6][:, 0:256], ACT.Copy).then_inc(r_sr, 1)
                merge_evac(act, FILL[c])
                act.wait_ge(r_sa, c + 1)
                if c > 1:
                    act.wait_ge(r_yp, c - 1)
                act.activation(SK.rearrange("p a b -> p (a b)"), psum[6][:, 256:512], ACT.Copy).then_inc(r_ss, 1)
                if FILL2[c] is not None:
                    merge_evac(act, FILL2[c])
                if c:
                    act.wait_ge(r_yp, c)
                    act.activation(YO[:, c - 1].rearrange("p a b -> p (a b)"), psum[2][:, 0:256], ACT.Copy).then_inc(r_yo, 1)
                if c + 1 < NC:
                    keep(c + 1)
            act.wait_ge(r_v1, 1)
            act.activation(stats[:, 96:128], stats[:, 96:128], ACT.Sqrt, scale=1.0 / 64, bias=con_("rln_eps")).then_inc(r_v2, 1)
            for u in range(32, 48):
                merge_evac(act, u)
            if STOP == "mix":
                return
            act_moe(act)

        def bc(name, n, j=0):
            at = PAR.at[name] + j
            return PARAM[:, at:at + 8].unsqueeze(2).broadcast_to([128, 8, n])

        def v_rest(v):
            XK, XRr, XV = XR[:, 1], XR[:, 0], XR[:, 2]
            v.wait_ge(pev, M_LORA)
            v.memset(SG[:, :, 0:PAD], 0.0)
            v.memset(RA[:, :, 0:PAD], 0.0)
            v.memset(XR24[:, :, 0:PAD], 0.0)
            v.tensor_tensor(XR24[:, :, PAD:TP], RAW[:, :, PAD - 1:TP - 1], RAW[:, :, PAD:TP], ALU.subtract)
            v.drain()
            with v.Fori(0, 24) as i:
                d = XR24[:, ds(i, 1), PAD:TP]
                v.scalar_tensor_tensor(d, d, PARAM[:, ds(i + PAR.at["mu"], 1)], RAW[:, ds(i, 1), PAD:TP], ALU.mult, ALU.add)
            v.drain()
            v.tensor_tensor(T1, XK, bc("k_k", TP), ALU.mult)
            v.drain()
            v.tensor_tensor(T2, T1, T1, ALU.mult).then_inc(r_ksq, 1)
            v.wait_ge(pev, M_MERGE)
            v.scalar_tensor_tensor(CS, RA, -1.0, bc("k_a", TP), ALU.add, ALU.mult)
            v.drain()
            v.scalar_tensor_tensor(XK, CS, 1.0, XK, ALU.add, ALU.mult)
            v.drain()
            v.tensor_tensor(BPR, XRr[:, :, 2 * PAD:TP], XK[:, :, 2 * PAD:TP], ALU.mult)
            v.drain()
            v.tensor_tensor(BPR, BPR, bc("r_k", SEQ), ALU.mult).then_inc(r_bin, 1)
            for i in range(8):
                v.wait_ge(r_krt, i + 1)
                v.reciprocal(T3[:, i, :], T3[:, i, :])
            v.drain()
            v.tensor_tensor(T1, T1, T3, ALU.mult)
            for i in range(8):
                v.wait_ge(r_bs, i + 1)
                v.tensor_tensor(BON[:, i, :], psum[6 + i % 2][:, 0:SEQ], XV[:, i, 2 * PAD:TP], ALU.mult).then_inc(r_bd, 1)
            v.drain()
            for i in range(8):
                v.tensor_tensor_scan(CS[:, i, :], con_("scan"), SG[:, i, :], 0.0, ALU.mult, ALU.add)
            v.drain()
            v.tensor_tensor(T3, CS, SG, ALU.subtract)
            v.drain().then_inc(r_cs, 1)
            v.wait_ge(r_ex, 1)
            v.scalar_tensor_tensor(SG, T1, -1.0, T3, ALU.mult, ALU.mult)
            v.tensor_tensor(XRr, XRr, T2, ALU.mult)
            v.tensor_copy(PC, T2[:, :, C - 1:TP:C])
            v.tensor_tensor(XK, XK, CS, ALU.mult)
            v.drain()
            v.tensor_tensor(T3, T1, RA, ALU.mult)
            v.drain()
            v.tensor_tensor(T3, T3, CS, ALU.mult)
            v.drain().then_inc(r_el, 1)
            unit(v, IU2[0:72], 2)
            for c in range(NC):
                v.wait_ge(r_a, c + 1)
                v.tensor_tensor(AM4[:, c], psum[4 + c % 2][:, :].rearrange("p (q n) -> p q n", q=4),
                                con_("m4").unsqueeze(1).broadcast_to([128, 4, 128]), ALU.mult).then_inc(r_am, 1)
            v.wait_ge(q_al, 16)
            invert(v, IA2[0:72].rearrange("p (z t s) -> p z t s", z=2, t=C), IU2[0:72].rearrange("p (z s t) -> p z s t", z=2, s=C),
                   IT2[0:72], 2)
            v.drain().then_inc(q_inv, 1)
            for c in range(NC):
                v.wait_ge(r_up, c + 1)
                if c:
                    v.wait_ge(r_yp, c)
                S4 = RS.rearrange("p (q j) n -> p q j n", j=2)
                for j in range(2):
                    inc = psum[5 + 2 * j][:, 256:512].rearrange("p (q n) -> p q n", q=4)
                    if c:
                        v.tensor_tensor(S4[:, :, j], S4[:, :, j], inc, ALU.add)
                    else:
                        v.tensor_copy(S4[:, :, j], inc)
                v.drain()
                v.tensor_tensor(RS, RS, PC[:, :, c:c + 1].broadcast_to([128, 8, 64]), ALU.mult)
                v.drain().then_inc(r_st, 1)
            v.wait_ge(r_yo, NC - 1)
            Y3 = YO.rearrange("p c q n -> p (c q) n")
            st = stats[:, 64:96]
            v.tensor_reduce(st.unsqueeze(2), Y3, AX.X, ALU.add)
            v.drain()
            v.tensor_scalar(st, st, 1.0 / 64, None, ALU.mult)
            v.drain()
            v.tensor_tensor(Y3, Y3, st.unsqueeze(2).broadcast_to([128, 32, 64]), ALU.subtract)
            v.drain()
            v.tensor_tensor(YD, Y3, Y3, ALU.mult)
            v.drain()
            v.tensor_reduce(stats[:, 96:128].unsqueeze(2), YD, AX.X, ALU.add)
            v.drain().then_inc(r_v1, 1)
            v.wait_ge(r_v2, 1)
            v.reciprocal(stats[:, 96:128], stats[:, 96:128])
            v.drain()
            v.tensor_tensor(YD, Y3, stats[:, 96:128].unsqueeze(2).broadcast_to([128, 32, 64]), ALU.mult)
            v.drain().then_inc(r_yn, 1)
            for g in range(2):
                v.wait_ge(r_yt, g + 1)
                for j in range(2):
                    src = psum[4 + 2 * g + j][:, :].rearrange("p (c q t) -> p q c t", c=4, q=4)
                    dst = YT[:, j:8:2, 128 * g:128 * g + 128].rearrange("p q (c t) -> p q c t", c=4)
                    w = PARAM[:, PAR.at["ln_w"] + j:PAR.at["ln_w"] + 8:2].unsqueeze(2).unsqueeze(3).broadcast_to([128, 4, 4, C])
                    v.tensor_tensor(dst, src, w, ALU.mult)
            v.drain()
            v.tensor_tensor(YT, YT, bc("ln_b", SEQ), ALU.add)
            v.drain()
            v.tensor_tensor(YT, YT, BON, ALU.add)
            v.drain()
            v.tensor_tensor(BON, YT, RG, ALU.mult)
            v.drain().then_inc(r_y, 1)
            v.drain()
            v.sem_inc(e_used, 2)
            v.wait_ge(xh, 16)
            for p in range(8):
                for a in range(2):
                    m = M_OUT + 2 * p + a
                    v.wait_ge(pdone, m + 1)
                    h = H2[:, a, 256 * p:256 * (p + 1)]
                    v.tensor_tensor(h, h, psum[m % 2][:, 0:256], ALU.add).then_inc(h2s, 1)
            if STOP == "mix":
                return
            v_moe(v)

        def pool_rest(pool):
            pool.wait_ge(k_yd, 4)
            for turn in range(3):
                for j in range(16):
                    u = 16 * turn + j
                    if u == U_PREP:
                        pool.wait_ge(r_am, NC)
                        for h in range(4):
                            pool.dma_start(rwkv_a.rearrange("(h c) (t s) -> h t c s", h=4, t=C)[h],
                                           AM4.rearrange("p c q s -> p (c q) s")[32 * h:32 * h + 32, :, 0:C]).then_inc(q_aw, 16)
                        pool.wait_ge(q_aw, 64)
                        pool.dma_start(IA2[0:72], rwkv_a.rearrange("(p z) a -> p (z a)", z=2)).then_inc(q_al, 16)
                    if u == U_CHAIN:
                        pool.wait_ge(q_inv, 1)
                        pool.dma_start(rwkv_u.rearrange("(p z) a -> p (z a)", z=2), IU2[0:72]).then_inc(q_uw, 16)
                        pool.wait_ge(q_uw, 16)
                        for h in range(4):
                            pool.dma_start(TT2.rearrange("p c q s -> p (c q) s")[32 * h:32 * h + 32],
                                           rwkv_u.rearrange("(h c) (s t) -> h s c t", h=4, s=C)[h]).then_inc(q_ul, 16)
                    pool.wait_ge(pev, M_MERGE + 2 * u + 2)
                    dst = MG[:, j, :]
                    if turn == 0:
                        pool.tensor_tensor(dst, GB[:, u % 2, :], BB[:, u % 2, :], ALU.mult).then_inc(mg_done, 1)
                    else:
                        pool.tensor_tensor(BB[:, u % 2, :], GB[:, u % 2, :], BB[:, u % 2, :], ALU.mult)
                        pool.drain()
                        pool.tensor_tensor(dst, dst, BB[:, u % 2, :], ALU.add).then_inc(mg_done, 1)
            if STOP == "mix":
                return
            pool_moe(pool)

        hn_d = dram("normed_tokens", [2 * SEQ, D // 2])
        y_d = dram("expert_rows", [2 * (2 * SEQ + CAP), D // 2])
        HN = view(A_RING + 8192 + 4096, 2, D)
        HNT = view(A_RING, KT, SEQ)
        FN = view(A_RING + 4096, D)
        WR = view(A_RING + 6144, KT, 36)
        A_RS = A_RING + 6720
        RB = view(A_RS, 36)
        LG = view(A_RS + 36, 2, 36)
        G8 = view(A_RS + 108, 2, 8)
        M8 = view(A_RS + 124, 2, 8)
        I8 = view(A_RS + 140, 2, 8).bitcast(U32)
        F8 = view(A_RS + 156, 2, 4)
        GH_ = view(A_RS + 164, 2, 4)
        E8 = view(A_RS + 172, 2, 8)
        O01 = view(A_RS + 188, 2, 2, NE)
        OS = view(A_RS + 316, 2, NE)
        RKM = view(A_RS + 380, 2, NE + 1)
        VALS = view(A_RS + 446, 2, NE + 1, 3)
        WT = view(A_RS + 644, 2, 2)
        RC = view(A_RS + 648, 8)
        RI = view(A_RS + 656, 4).bitcast(I32)
        IF_ = view(A_RS + 660, 4)
        IG = view(A_RS + 664, 2, 2).bitcast(I32)
        SEL = view(A_RS + 668, 2, 2, 128)
        assert A_RS + 668 + 512 <= A_RING + 8192
        XG = view(A_RING + 8192 + 4096, 2, 1024)
        YS = view(A_RING + 8192 + 4096 + 2048, 1024)
        XGT = view(A_RING, 2, 8, 128)
        SL = view(A_RING + 2048, 256)
        AA = view(A_RING + 2304, 256)
        ATT = view(A_RING + 2560, 2, 128)
        A_E = 53200 - 4 * 8192
        ering = view(A_E, 4, 8192)
        YA = view(A_E, 2, 2, D)
        NF = view(A_E + 8192, D)
        OUT = view(A_E + 8192 + 2048, 2, D)
        OJ = view(A_E + 8192 + 2048 + 4096, D)

        eld = [sem(f"expert_weights_loaded{i}") for i in range(4)]
        e_used = sem("expert_slots_free")
        f_sq, f_rt, f_hn, f_ld = sem("ffn_squares"), sem("ffn_roots"), sem("ffn_normed"), sem("router_loaded")
        f_st = sem("normed_stored")
        f_t, f_tc, f_lg = sem("ffn_turned"), sem("ffn_turned_kept"), sem("logits")
        f_l, f_ex, f_oh, f_rk, f_rd = sem("gate_inputs"), sem("gate_exps"), sem("chosen"), sem("ranks"), sem("rounds_known")
        x_sel, x_idx, x_ig, x_g = sem("rows_selected"), sem("row_numbers"), sem("row_indices"), sem("rows_gathered")
        x_t, x_gt, x_sl, x_a, x_tt, x_at = (sem("rows_turned"), sem("rows_turned_kept"), sem("silu_done"), sem("hidden_done"),
                                            sem("hidden_turned"), sem("hidden_turned_kept"))
        x_sd = sem("result_rows_in_memory")
        x_go = sem("indirect_dma_issued")
        x_y1, x_y2, x_s, x_end = sem("result_kept_low"), sem("result_kept_high"), sem("result_scattered"), sem("rounds_done")
        z_ld, z_sq, z_rt, z_out, z_st = sem("results_loaded"), sem("final_squares"), sem("final_roots"), sem("final_normed"), sem("stored")

        def rounds(eng):
            eng.wait_ge(f_rd, 1)
            return eng.value_load(RI[0:1, 0:1], min_val=1, max_val=SEQ // CAP)

        def sp_moe(sp):
            sp.wait_ge(pdone, M_OUT + 16)
            sp.dma_start(FN, norm_ffn.broadcast_to([128, D])).then_inc(f_ld, 16)
            sp.dma_start(WR[:, :, 0:NG], w_rg.rearrange("(k p) n -> p k n", p=128)).then_inc(f_ld, 16)
            sp.dma_start(WR[:, :, NG:36], w_re.rearrange("(k p) n -> p k n", p=128)).then_inc(f_ld, 16)
            sp.dma_start(RB[:, 0:NG], b_rg.broadcast_to([128, NG])).then_inc(f_ld, 16)
            sp.dma_start(RB[:, NG:36], b_re.broadcast_to([128, NE])).then_inc(f_ld, 16)
            sp.wait_ge(f_hn, 1)
            sp.dma_start(hn_d.rearrange("(a p h) n -> p a (h n)", a=2, p=128), HN).then_inc(f_st, 16)
            n_rounds = rounds(sp)

            with sp.Fori(0, n_rounds) as r:
                with sp.Fori(0, NE // 4) as i:
                    for j in range(4):
                        for part in range(3):
                            c = 3 * j + part
                            sp.wait_ge(e_used, (r * (NE // 4) + i) * 12 + (c + 1))
                            slot = (c + 1) % 4
                            if part < 2:
                                dst = ering[:, slot, :].rearrange("p (a j n) -> p a j n", a=2, j=8)
                                for a, w in enumerate((e_gate, e_up)):
                                    src = w[ds(i * 4 + j, 1), 1024 * part:1024 * (part + 1), :].rearrange("e (p j) n -> p (e j) n", j=8)
                                    sp.dma_start(dst[:, a], src).then_inc(eld[slot], 16)
                            else:
                                dst = ering[:, slot, :].rearrange("p (k n) -> p k n", k=4)
                                src = e_down[ds(i * 4 + j, 1), :, :].rearrange("e (k p) n -> p (e k) n", p=128)
                                for a in range(2):
                                    sp.dma_start(dst[:, 2 * a:2 * a + 2], src[:, 2 * a:2 * a + 2]).then_inc(eld[slot], 16)
            sp.wait_ge(x_end, 1)
            sp.dma_start(YA, y_d[0:4 * SEQ].rearrange("(a p k h) n -> p a k (h n)", a=2, p=128, k=2)).then_inc(z_ld, 16)
            sp.dma_start(NF, norm_final.broadcast_to([128, D])).then_inc(z_ld, 16)
            for a in range(2):
                sp.wait_ge(z_out, a + 1)
                sp.dma_start(out[128 * a:128 * (a + 1)], OUT[:, a]).then_inc(z_st, 16)
            sp.wait_ge(z_st, 32)

        def pe_moe(pe):
            pe.drain()
            pe.sem_inc(e_used, 1)
            pe.wait_ge(f_hn, 1)
            for k in range(KT):
                if k >= 4:
                    pe.wait_ge(f_tc, k - 3)
                else:
                    pe.wait_ge(h2s, 16)
                for a in range(2):
                    mm = pe.transpose(psum[k % 4][:, 128 * a:128 * (a + 1)], HN[:, a, 128 * k:128 * (k + 1)], ident)
                mm.then_inc(f_t, 1)
            pe.wait_ge(f_tc, KT)
            pe.wait_ge(f_ld, 80)
            for a in range(2):
                for k in range(KT):
                    mm = pe.matmul(psum[6][:, 64 * a:64 * a + 36], HNT[:, k, 128 * a:128 * (a + 1)], WR[:, k, :],
                                   start=k == 0, stop=k == KT - 1)
            mm.then_inc(f_lg, 1)
            pe.wait_ge(f_oh, 1)
            pe.matmul(psum[7][:, 0:32], con_("lt"), OS[:, 0], start=True, stop=True)
            pe.matmul(psum[7][:, 32:64], con_("ones"), OS[:, 0], start=True, stop=False)
            pe.matmul(psum[7][:, 32:64], con_("lt"), OS[:, 1], start=False, stop=True)
            pe.matmul(psum[7][:, 64:96], con_("ones"), OS[:, 0], start=True, stop=False)
            pe.matmul(psum[7][:, 64:96], con_("ones"), OS[:, 1], start=False, stop=True).then_inc(f_rk, 1)
            n_rounds = rounds(pe)
            for s, by in ((x_t, 1), (x_tt, 1)):
                pe.sem_inc(s, by)

            def numbers(r, n, buf):
                at = r * (NE + 1) + n
                pe.wait_ge(x_sel, at + 1)
                pe.wait_ge(x_ig, at + 1)
                for a in range(2):
                    mm = pe.matmul(psum[6][:, 0:3], SEL[:, buf, a, :], VALS[:, a, ds(n, 1), :] if not isinstance(n, int) else VALS[:, a, n, :],
                                   start=a == 0, stop=a == 1)
                mm.then_inc(x_idx, 1)

            def turn(r, n, buf):
                at = r * (NE + 1) + n
                pe.wait_ge(x_g, at * 16 + 16)
                pe.wait_ge(x_gt, at + 1)
                for j in range(8):
                    mm = pe.transpose(psum[j // 4][:, 128 * (j % 4):128 * (j % 4) + 128], XG[:, buf, j:1024:8], ident)
                mm.then_inc(x_t, 1)

            with pe.Fori(0, n_rounds) as r:
                numbers(r, 0, 0)
                turn(r, 0, 0)
                with pe.Fori(0, NE // 4) as i:
                    for j in range(4):
                        b = j % 2
                        at = r * NE + i * 4 + j
                        numbers(r, i * 4 + (j + 1), 1 - b)
                        pe.wait_ge(x_gt, r * (NE + 1) + i * 4 + (j + 2))
                        pe.wait_ge(x_a, at + 1)
                        for h in range(2):
                            c = 3 * j + h
                            pe.wait_ge(eld[(c + 1) % 4], ((r * (NE // 4) + i) * 3 + (c // 4 + 1)) * 32)
                            w = ering[:, (c + 1) % 4, :].rearrange("p (a j n) -> p a j n", a=2, j=8)
                            for k in range(8):
                                for n in range(2):
                                    mm = pe.matmul(psum[2 + b][64 * n:64 * n + 64, :], XGT[:, b, k, 64 * h:64 * h + 64],
                                                   w[:, :, k, 256 * n:256 * n + 256], start=h == 0 and k == 0, stop=h == 1 and k == 7,
                                                   tile_position=(0, 64 * n), skip_group_check=True)
                            mm.then_inc(e_used, 1)
                        turn(r, i * 4 + (j + 1), 1 - b)
                        pe.wait_ge(x_a, at + 2)
                        pe.wait_ge(x_at, at + 1)
                        for k in range(2):
                            mm = pe.transpose(psum[7][:, 128 * k:128 * k + 128], AA[:, 128 * k:128 * k + 128], ident)
                        mm.then_inc(x_tt, 1)
                        pe.wait_ge(x_at, at + 2)
                        pe.wait_ge(x_y1, at + 1)
                        pe.wait_ge(x_y2, at + 1)
                        c = 3 * j + 2
                        pe.wait_ge(eld[(c + 1) % 4], ((r * (NE // 4) + i) * 3 + (c // 4 + 1)) * 32)
                        w = ering[:, (c + 1) % 4, :].rearrange("p (k n) -> p k n", k=4)
                        for q in range(2):
                            for k in range(4):
                                for m in range(2):
                                    mm = pe.matmul(psum[4 + q][64 * m:64 * m + 64, :], ATT[:, k % 2, 64 * (k // 2):64 * (k // 2) + 64],
                                                   w[:, k, 1024 * m + 512 * q:1024 * m + 512 * (q + 1)], start=k == 0, stop=k == 3,
                                                   tile_position=(0, 64 * m), skip_group_check=True)
                        mm.then_inc(e_used, 1)

        def act_moe(act):
            act.wait_ge(h2s, 16)
            for a in range(2):
                act.activation(HN[:, a, :], H2[:, a, :], ACT.Square, accum_out=stats[:, 130 + a:131 + a])
            act.drain()
            act.activation(stats[:, 132:134], stats[:, 130:132], ACT.Sqrt, scale=1.0 / D, bias=con_("eps")).then_inc(f_rt, 1)
            for k in range(KT):
                act.wait_ge(f_t, k + 1)
                act.activation(HNT[:, k, :], psum[k % 4][:, 0:SEQ], ACT.Copy).then_inc(f_tc, 1)
            act.wait_ge(f_l, 1)
            for a in range(2):
                act.activation(GH_[:, a, :], LG[:, a, 0:NG], ACT.Exp, bias=F8[:, a, 1:2], accum_out=F8[:, a, 2:3])
                act.activation(F8[:, a, 3:4], F8[:, a, 3:4], ACT.Exp)
            act.drain().then_inc(f_ex, 1)
            n_rounds = rounds(act)
            for s, by in ((x_gt, 1), (x_y2, 1),):
                act.sem_inc(s, by)

            def keep(r, n, buf):
                at = r * (NE + 1) + n
                act.wait_ge(x_t, at + 2)
                act.wait_ge(e_used, (r * NE + n) * 3 + 1)
                for a in range(2):
                    act.activation(XGT[:, buf, 4 * a:4 * a + 4, :].rearrange("p a b -> p (a b)"), psum[a][:, :], ACT.Copy)
                act.drain().then_inc(x_gt, 1)

            with act.Fori(0, n_rounds) as r:
                keep(r, 0, 0)
                with act.Fori(0, NE // 4) as i:
                    for j in range(4):
                        b = j % 2
                        at = r * NE + i * 4 + j
                        act.wait_ge(e_used, at * 3 + 6)
                        act.wait_ge(x_a, at + 1)
                        act.activation(SL, psum[2 + b][:, 0:256], ACT.Silu).then_inc(x_sl, 1)
                        keep(r, i * 4 + (j + 1), 1 - b)
                        act.wait_ge(e_used, at * 3 + 7)
                        act.wait_ge(x_sd, at + 1)
                        act.activation(YS[:, 512:1024], psum[5][:, :], ACT.Copy).then_inc(x_y2, 1)
            act.wait_ge(z_sq, 1)
            act.activation(stats[:, 142:144], stats[:, 140:142], ACT.Sqrt, scale=1.0 / D, bias=con_("eps")).then_inc(z_rt, 1)

        def v_moe(v):
            v.wait_ge(f_rt, 1)
            v.reciprocal(stats[:, 132:134], stats[:, 132:134])
            v.wait_ge(f_ld, 80)
            v.drain()
            for a in range(2):
                v.scalar_tensor_tensor(HN[:, a, :], H2[:, a, :], stats[:, 132 + a:133 + a], FN, ALU.mult, ALU.mult)
            v.drain().then_inc(f_hn, 1)
            v.memset(G8, -3e38)
            v.wait_ge(f_lg, 1)
            v.tensor_tensor(LG, psum[6][:, 0:128].rearrange("p (a n) -> p a n", a=2)[:, :, 0:36],
                            RB.unsqueeze(1).broadcast_to([128, 2, 36]), ALU.add)
            v.drain()
            v.tensor_copy(G8[:, :, 0:NG], LG[:, :, 0:NG])
            v.drain()
            for a in range(2):
                v.max(M8[:, a, :], G8[:, a, :])
                v.drain()
                v.max_index(I8[:, a, :], M8[:, a, :], G8[:, a, :])
                v.tensor_scalar(F8[:, a, 1:2], M8[:, a, 0:1], -1.0, None, ALU.mult)
                v.drain()
                v.tensor_copy(F8[:, a, 0:1], I8[:, a, 0:1])
                v.drain()
                v.tensor_scalar(GH_[:, a, :], con_("iota8")[:, 0:NG], F8[:, a, 0:1], None, ALU.is_equal)
                v.drain()
                v.tensor_scalar(E8[:, a, :], LG[:, a, NG:NG + 8], GH_[:, a, 0:1], None, ALU.mult)
                for g in range(1, NG):
                    v.drain()
                    v.scalar_tensor_tensor(E8[:, a, :], LG[:, a, NG + 8 * g:NG + 8 * g + 8], GH_[:, a, g:g + 1], E8[:, a, :], ALU.mult, ALU.add)
                v.drain()
                v.max(M8[:, a, :], E8[:, a, :])
                v.drain()
                v.max_index(I8[:, a, :], M8[:, a, :], E8[:, a, :])
                v.tensor_tensor(F8[:, a, 3:4], M8[:, a, 1:2], M8[:, a, 0:1], ALU.subtract)
                v.drain()
                v.tensor_copy(G8[:, a, 0:2], I8[:, a, 0:2])
                v.drain()
                v.tensor_scalar(F8[:, a, 0:1], F8[:, a, 0:1], float(EPG), None, ALU.mult)
                v.drain()
                v.tensor_scalar(G8[:, a, 0:2], G8[:, a, 0:2], F8[:, a, 0:1], None, ALU.add)
                v.drain()
                for c in range(2):
                    v.tensor_scalar(O01[:, a, c, :], con_("iota32"), G8[:, a, c:c + 1], None, ALU.is_equal)
                v.drain()
                v.tensor_tensor(OS[:, a, :], O01[:, a, 0, :], O01[:, a, 1, :], ALU.add)
            v.drain().then_inc(f_l, 1)
            v.nop().then_inc(f_oh, 1)
            v.memset(RKM, -1e4)
            v.memset(VALS, 1.0)
            v.wait_ge(f_rk, 1)
            v.wait_ge(f_ex, 1)
            v.drain()
            for a in range(2):
                tok = con_("tok2")[:, a:a + 1]
                v.scalar_tensor_tensor(RKM[:, a, 0:NE], OS[:, a, :], 1e4, psum[7][:, 32 * a:32 * a + 32], ALU.mult, ALU.add)
                v.tensor_scalar(VALS[:, a, 0:NE, 0], VALS[:, a, 0:NE, 0], tok, None, ALU.mult)
                v.tensor_scalar(VALS[:, a, 0:NE, 1], O01[:, a, 1, :], tok, None, ALU.add)
                v.drain()
                v.tensor_scalar(VALS[:, a, 0:NE, 1], VALS[:, a, 0:NE, 1], tok, None, ALU.add)
                v.tensor_scalar(RKM[:, a, 0:NE], RKM[:, a, 0:NE], -1e4, None, ALU.add)
                v.tensor_scalar(F8[:, a, 0:1], F8[:, a, 3:4], 1.0, None, ALU.add)
                v.drain()
                v.tensor_tensor(F8[:, a, 0:1], F8[:, a, 0:1], F8[:, a, 2:3], ALU.mult)
                v.drain()
                v.reciprocal(WT[:, a, 0:1], F8[:, a, 0:1])
                v.drain()
                v.tensor_tensor(WT[:, a, 1:2], WT[:, a, 0:1], F8[:, a, 3:4], ALU.mult)
            v.tensor_reduce(RC[:, 0:1], psum[7][:, 64:96], AX.X, ALU.max)
            v.drain()
            v.tensor_scalar(RC[:, 1:2], RC[:, 0:1], float(CAP), 1.0, ALU.is_gt, ALU.add)
            for t in range(2, SEQ // CAP):
                v.drain()
                v.scalar_tensor_tensor(RC[:, 1:2], RC[:, 0:1], float(t * CAP), RC[:, 1:2], ALU.is_gt, ALU.add)
            v.drain()
            v.tensor_copy(RI[:, 0:1], RC[:, 1:2])
            v.drain().then_inc(f_rd, 1)
            n_rounds = rounds(v)
            for s, by in ((x_ig, 1), (x_a, 1), (x_at, 1), (x_y1, 1),):
                v.sem_inc(s, by)

            def select(r, n, buf):
                at = r * (NE + 1) + n
                for a in range(2):
                    rank = RKM[:, a, n:n + 1] if isinstance(n, int) else RKM[:, a, ds(n, 1)]
                    v.tensor_scalar(SEL[:, buf, a, :], con_("slot"), rank, None, ALU.is_equal)
                v.drain().then_inc(x_sel, 1)
                v.wait_ge(x_idx, at + 1)
                p = psum[6]
                v.scalar_tensor_tensor(IF_[:, 0:1], p[:, 0:1], 2.0, con_("half"), ALU.mult, ALU.add)
                v.scalar_tensor_tensor(IF_[:, 1:2], p[:, 1:2], 2.0, con_("half"), ALU.mult, ALU.add)
                v.tensor_scalar(IF_[:, 2:3], p[:, 2:3], -1.0, 1.0, ALU.mult, ALU.add)
                v.drain()
                v.scalar_tensor_tensor(IF_[:, 1:2], IF_[:, 2:3], con_("trash"), IF_[:, 1:2], ALU.mult, ALU.add)
                done = r * NE if isinstance(n, int) else r * NE + n - 1
                v.drain()
                v.wait_ge(x_sd, done + 1)
                v.tensor_copy(IG[:, buf, :], IF_[:, 0:2])
                v.drain().then_inc(x_ig, 1)

            with v.Fori(0, n_rounds) as r:
                select(r, 0, 0)
                with v.Fori(0, NE // 4) as i:
                    for j in range(4):
                        b = j % 2
                        at = r * NE + i * 4 + j
                        select(r, i * 4 + (j + 1), 1 - b)
                        v.wait_ge(x_sl, at + 1)
                        v.wait_ge(x_tt, at + 1)
                        v.tensor_tensor(AA, SL, psum[2 + b][:, 256:512], ALU.mult).then_inc(x_a, 1)
                        v.wait_ge(x_tt, at + 2)
                        v.wait_ge(e_used, at * 3 + 4)
                        v.tensor_copy(ATT.rearrange("p a b -> p (a b)"), psum[7][:, 0:256]).then_inc(x_at, 1)
                        v.wait_ge(e_used, at * 3 + 7)
                        v.wait_ge(x_sd, at + 1)
                        v.tensor_copy(YS[:, 0:512], psum[4][:, :]).then_inc(x_y1, 1)
                v.wait_ge(x_idx, r * (NE + 1) + (NE + 1))
                v.tensor_scalar(RKM, RKM, -float(CAP), None, ALU.add)
                v.drain()
            v.wait_ge(z_ld, 32)
            for a in range(2):
                v.scalar_tensor_tensor(OUT[:, a, :], YA[:, a, 0, :], WT[:, a, 0:1], H2[:, a, :], ALU.mult, ALU.add)
                v.drain()
                v.scalar_tensor_tensor(OUT[:, a, :], YA[:, a, 1, :], WT[:, a, 1:2], OUT[:, a, :], ALU.mult, ALU.add)
                v.drain()
                v.tensor_tensor_reduce(OJ, OUT[:, a, :], OUT[:, a, :], 1.0, 0.0, ALU.mult, ALU.add, stats[:, 140 + a:141 + a])
                v.drain()
            v.nop().then_inc(z_sq, 1)
            v.wait_ge(z_rt, 1)
            v.reciprocal(stats[:, 142:144], stats[:, 142:144])
            v.drain()
            for a in range(2):
                v.scalar_tensor_tensor(OUT[:, a, :], OUT[:, a, :], stats[:, 142 + a:143 + a], NF, ALU.mult, ALU.mult).then_inc(z_out, 1)

        def pool_moe(pool):
            pool.drain()
            pool.sem_inc(e_used, 1)
            pool.wait_ge(f_st, 16)
            n_rounds = rounds(pool)
            for s, by in ((x_sd, 1),):
                pool.sem_inc(s, by)

            def gather(r, n, buf):
                at = r * (NE + 1) + n
                pool.wait_ge(x_ig, at + 2)
                pool.wait_ge(x_t, r * (NE + 1) + n if not isinstance(n, int) else r * (NE + 1) + 1)
                pool.sem_inc(x_go, 1)
                pool.indirect_dma_start(XG[:, buf, :], None, hn_d, bass.IndirectOffsetOnAxis(IG[:, buf, 0:1].bitcast(U32), 0)).then_inc(x_g, 16)

            with pool.Fori(0, n_rounds) as r:
                gather(r, 0, 0)
                with pool.Fori(0, NE // 4) as i:
                    for j in range(4):
                        b = j % 2
                        at = r * NE + i * 4 + j
                        gather(r, i * 4 + (j + 1), 1 - b)
                        pool.wait_ge(x_y1, at + 2)
                        pool.wait_ge(x_y2, at + 2)
                        pool.sem_inc(x_go, 1)
                        pool.indirect_dma_start(y_d, bass.IndirectOffsetOnAxis(IG[:, b, 1:2].bitcast(U32), 0), YS, None).then_inc(x_s, 16)
                        pool.wait_ge(x_s, at * 16 + 16)
                        pool.sem_inc(x_sd, 1)
            pool.sem_inc(x_end, 1)

        block = ctx.enter_context(nc.Block())
        STOP = program.stop

        @block.sync
        def _(sp):
            sp.dma_start(CONST, con).then_inc(ld, 16)
            sp.dma_start(PARAM, par).then_inc(ld, 16)
            sp.dma_start(XM[0:META], meta).then_inc(ld, 16)
            sp.dma_start(XT, x.rearrange("(a p) d -> p a d", a=2)).then_inc(ld, 16)
            win = w_in.rearrange("(k p) n -> p k n", p=128)

            def load(n, src, dst=None, turn=0, need=None):
                if n >= 4:
                    sp.wait_ge(pdone, (uses_with(n - 4) if need is None else need) + 4 * turn)
                sp.dma_start(ring[:, n % 4, :].rearrange("p (k n) -> p k n", k=src.shape[1]) if dst is None else dst,
                             src).then_inc(wld[n % 4], 16)

            def win_block(n, at, width):
                load(n, win[:, :, at:at + width], ring[:, n % 4, 0:KT * width].rearrange("p (k n) -> p k n", k=KT))

            win_block(0, IN0_BA, 16)
            for j in range(6):
                win_block(1 + j, IN0_CQ + 128 * j, 128)
            for j in range(4):
                win_block(7 + j, IN0_CKV + 128 * j, 128)
            win_block(11, IN0_KPE, 64)
            win_block(12, IN0_LORA, 128)
            win_block(13, IN0_LORA + 128, 128)
            win_block(14, IN0_LORA + 256, 32)
            with sp.Fori(0, 3) as i:
                for j in range(8):
                    load(N_QKV + j, win[:, :, ds(i * BR + 128 * j, 128)], turn=2 * i)
            wq = w_q_up.rearrange("(k p) n -> p k n", p=128)
            for h in range(8):
                load(N_QUP + h, wq[:, :, 192 * h:192 * (h + 1)],
                     ring[:, (N_QUP + h) % 4, 0:6 * 192].rearrange("p (k n) -> p k n", k=6))
            wkv = w_kv_up.rearrange("(k p) n -> p k n", p=128)
            for j in range(4):
                load(N_KVUP + j, wkv[:, :, 512 * j:512 * (j + 1)])
            for j in range(8):
                load(N_Z + j, win[:, :, 3 * BR + 128 * j:3 * BR + 128 * (j + 1)])
            if STOP == "mla":
                return
            with sp.Fori(0, 3) as i:
                for j in range(8):
                    load(N_RKV + j, win[:, :, ds(i * BR + (IN0_RKV + 128 * j), 128)], turn=2 * i)
            if STOP == "mla":
                return
            if STOP == "gdn":
                return
            sp_rest(sp, load)

        def dense(pe, m, products, turn=0):
            if m >= 2:
                pe.wait_ge(pev, m - 1 + 4 * turn)
            for rows, cols, lhs, rhs, first, last in products:
                mm = pe.matmul(psum[m % 2][0:rows, 0:cols], lhs, rhs, start=first, stop=last)
            mm.then_inc(pdone, 1)
            return mm

        def weights(eng, n, turn=0):
            eng.wait_ge(wld[n % 4], 16 * (n // 4 + 1) + 16 * turn)

        def in_block(pe, n, m, width=128, lo=0, turn=0):
            weights(pe, n, turn)
            w = ring[:, n % 4, 0:KT * width].rearrange("p (k n) -> p k n", k=KT)
            dense(pe, m, [(width, T - lo, w[:, k, :], HT[:, k, lo:T], k == 0, k == KT - 1) for k in range(KT)],
                  turn)

        @block.tensor
        def _(pe):
            pe.wait_ge(ld, 64)
            pe.wait_ge(xn_ready, 3)
            for k in range(KT):
                b = psum[4 + k % 4]
                if k >= 4:
                    pe.wait_ge(ht_ready, k - 3)
                pe.transpose(b[:, 0:META], XM[0:META, 128 * k:128 * (k + 1)], ident[0:META, 0:META])
                for a in range(2):
                    mm = pe.transpose(b[:, META + 128 * a:META + 128 * (a + 1)], XT[:, a, 128 * k:128 * (k + 1)], ident)
                mm.then_inc(ht_t, 1)
            pe.wait_ge(ht_ready, KT)
            for n in range(15):
                in_block(pe, n, n, {0: 16, 11: 64, 14: 32}.get(n, 128))
            with pe.Fori(0, 3) as i:
                for j in range(8):
                    in_block(pe, N_QKV + j, M_QKV + j, turn=2 * i)
            for i in range(10):
                pe.wait_ge(s_csq, i + 1)
                b = psum[6 if i < 6 else 7]
                pe.matmul(b[:, 0:T], con_("ones"), SQ[:, i % 2, 0:T], start=i in (0, 6), stop=i in (5, 9)).then_inc(s_csqf, 1)
            pe.wait_ge(s_cn, 10)
            for h in range(8):
                n, m = N_QUP + h, M_QUP + 2 * h
                weights(pe, n)
                w = ring[:, n % 4, 0:6 * 192].rearrange("p (k n) -> p k n", k=6)
                dense(pe, m, [(128, SEQ, w[:, k, 0:128], CQKV[:, k, META:T], k == 0, k == 5) for k in range(6)])
                dense(pe, m + 1, [(64, SEQ, w[:, k, 128:192], CQKV[:, k, META:T], k == 0, k == 5)
                                  for k in range(6)])
            for j in range(4):
                n, m = N_KVUP + j, M_KVUP + 5 * j
                weights(pe, n)
                w = ring[:, n % 4, :].rearrange("p (k h n) -> p k h n", k=4, h=2)
                for a in range(2):
                    dense(pe, m + a, [(128, T, w[:, k, a, 0:128], CQKV[:, 6 + k, :], k == 0, k == 3) for k in range(4)])
                for a, (t0, t1) in enumerate(((0, META), (META, META + 128), (META + 128, T))):
                    dense(pe, m + 2 + a, [(t1 - t0, 256, CQKV[:, 6 + k, t0:t1], w[:, k, :, 128:256],
                                                  k == 0, k == 3) for k in range(4)])
            for i in range(5):
                pe.wait_ge(pev, M_QUP + 4 * i + 4 if i < 4 else M_SMALL + 12)
                if i >= 2:
                    pe.wait_ge(s_rotd, i - 1)
                rhs = QPE[0:64, 2 * i:2 * i + 2, :] if i < 4 else KPE[0:64]
                pe.matmul(psum[4 + i % 2][0:64, 0:512 if i < 4 else T], con_("rot", 64), rhs,
                          start=True, stop=True).then_inc(s_rot, 1)
            pe.wait_ge(s_rotd, 5)
            pe.wait_ge(pev, M_Z)
            for i in range(17):
                if i < 16:
                    h, a = i // 2, i % 2
                    nk = META + 128 * (a + 1)
                    if i >= 2:
                        pe.wait_ge(a_sm, i - 1)
                    b = psum[4 + i % 2]
                    pe.matmul(b[:, 0:nk], QN[:, h, 128 * a:128 * (a + 1)], KN[:, h, 0:nk], start=True, stop=False)
                    pe.matmul(b[:, 0:nk], QPE[0:64, h, 128 * a:128 * (a + 1)], KPE[0:64, 0:nk],
                              start=False, stop=True).then_inc(a_sc, 1)
                if i % 2 and i < 16:
                    in_block(pe, N_Z + i // 2, M_Z + i // 2, lo=META)
                if i >= 1:
                    i_ = i - 1
                    h, a = i_ // 2, i_ % 2
                    pe.wait_ge(a_pn, i_ + 1)
                    if i_ >= 1:
                        pe.wait_ge(a_pc, i_)
                    for t in range(a + 1):
                        pe.transpose(psum[6][:, 128 * t:128 * (t + 1)], PX[:, i_ % 2, META + 128 * t:META + 128 * (t + 1)], ident)
                    pe.transpose(psum[6][0:META, 256:384], PX[:, i_ % 2, 0:META], ident).then_inc(a_pt, 1)
                    pe.wait_ge(a_pc, i_ + 1)
                    if i_ >= 1:
                        pe.wait_ge(a_oc, i_)
                    pe.matmul(psum[7][:, 0:128], VT[0:META, 0, 128 * h:128 * (h + 1)], PT[0:META, i_ % 2, 256:384],
                              start=True, stop=False)
                    for t in range(a + 1):
                        mm = pe.matmul(psum[7][:, 0:128], VT[:, 1 + t, 128 * h:128 * (h + 1)],
                                       PT[:, i_ % 2, 128 * t:128 * (t + 1)], start=False, stop=t == a)
                    mm.then_inc(a_o, 1)
            if STOP == "mla":
                return
            pe_gdn(pe)
            if STOP == "gdn":
                return
            pe_rest(pe)

        def evac(act, m, dst, func=ACT.Copy, rows=128, cols=T, turn=0, **kw):
            act.wait_ge(pdone, m + 1 + 4 * turn)
            act.activation(dst, psum[m % 2][0:rows, 0:cols], func, **kw).then_inc(pev, 1)

        @block.scalar
        def _(act):
            act.wait_ge(ld, 64)
            act.wait_ge(zeroed, 1)
            act.activation(XJ[:, :], XT[:, 0, :], ACT.Square, accum_out=stats[:, 0:1])
            act.drain()
            act.activation(XJ[:, :], XT[:, 1, :], ACT.Square, accum_out=stats[:, 1:2])
            act.drain()
            act.activation(XJ[0:META, :], XM[0:META, :], ACT.Square, accum_out=stats[0:META, 2:3]).then_inc(sq0, 1)
            act.drain()
            act.activation(stats[:, 4:7], stats[:, 0:3], ACT.Sqrt, scale=1.0 / D, bias=con_("eps")).then_inc(rt0, 1)
            for k in range(KT):
                act.wait_ge(ht_t, k + 1)
                act.activation(HT[:, k, :], psum[4 + k % 4][:, 0:T], ACT.Copy, scale=par_("norm_mix", k)).then_inc(ht_ready, 1)
            act.wait_ge(zeroed, 2)
            for n in range(15):
                dst = {0: BA[0:16, PAD:TP], 11: KPE[0:64], 12: LR[:, 0, PAD:TP], 13: LR[:, 1, PAD:TP],
                       14: LR[0:32, 2, PAD:TP]}.get(n, CQKV[:, max(n - 1, 0) % 10, :])
                evac(act, n, dst, rows={0: 16, 11: 64, 14: 32}.get(n, 128))
            act.drain()
            for i in range(10):
                if i >= 2:
                    act.wait_ge(s_csqf, i - 1)
                act.activation(SQ[:, i % 2, 0:T], CQKV[:, i, :], ACT.Square).then_inc(s_csq, 1)
                if i == 1:
                    with act.Fori(0, 3) as r:
                        for j in range(8):
                            evac(act, M_QKV + j, RAW[:, ds(r * 8 + j, 1), PAD:TP], turn=2 * r)
            act.wait_ge(s_csqf, 10)
            act.activation(RN[:, 0, 0:T], psum[6][:, 0:T], ACT.Sqrt, scale=1.0 / QL, bias=con_("eps")).then_inc(s_crt, 1)
            act.activation(RN[:, 1, 0:T], psum[7][:, 0:T], ACT.Sqrt, scale=1.0 / KVL, bias=con_("eps")).then_inc(s_crt, 1)
            for h in range(8):
                evac(act, M_QUP + 2 * h, QN[:, h, :], cols=SEQ)
                evac(act, M_QUP + 2 * h + 1, QPE[0:64, h, :], rows=64, cols=SEQ)
            act.wait_ge(s_conv, 24)
            for j in range(4):
                m = M_KVUP + 5 * j
                for a in range(2):
                    evac(act, m + a, KN[:, 2 * j + a, :])
                for a in range(3):
                    r = META if a == 0 else 128
                    evac(act, m + 2 + a, VT[0:r, a, 256 * j:256 * (j + 1)], rows=r, cols=256)
            for i in range(17):
                if i < 16:
                    nk = META + 128 * (i % 2 + 1)
                    act.wait_ge(a_sm, i + 1)
                    if i >= 2:
                        act.wait_ge(a_pt, i - 1)
                    act.activation(PX[:, i % 2, 0:nk], SS[:, i % 2, 0:nk], ACT.Exp, bias=stats[:, 10 + i % 2:11 + i % 2],
                                   accum_out=stats[:, 12 + i % 2:13 + i % 2]).then_inc(a_ex, 1)
                    if i % 2:
                        evac(act, M_Z + i // 2, ZR[:, i // 2, :], cols=SEQ)
                if i >= 1:
                    i_ = i - 1
                    h, a = i_ // 2, i_ % 2
                    act.wait_ge(a_pt, i_ + 1)
                    if i_ >= 2:
                        act.wait_ge(a_o, i_ - 1)
                    act.activation(PT[:, i_ % 2, 0:128 * (a + 1)], psum[6][:, 0:128 * (a + 1)], ACT.Copy)
                    act.activation(PT[0:META, i_ % 2, 256:384], psum[6][0:META, 256:384], ACT.Copy)
                    act.drain().then_inc(a_pc, 1)
                    act.wait_ge(a_o, i_ + 1)
                    act.activation(Y[:, 1, h, 128 * a:128 * (a + 1)], psum[7][:, 0:128], ACT.Copy).then_inc(a_oc, 1)
            if STOP == "mla":
                return
            act_gdn(act)
            if STOP == "gdn":
                return
            act_rest(act)

        @block.vector
        def _(v):
            v.memset(stats[:, :], 1.0).then_inc(zeroed, 1)
            v.wait_ge(rt0, 1)
            v.reciprocal(stats[:, 4:7], stats[:, 4:7])
            v.drain()
            for a in range(2):
                v.tensor_scalar(XT[:, a, :], XT[:, a, :], stats[:, 4 + a:5 + a], None, ALU.mult).then_inc(xn_ready, 1)
            v.tensor_scalar(XM[0:META], XM[0:META], stats[0:META, 6:7], None, ALU.mult).then_inc(xn_ready, 1)
            v.memset(LR[:, :, 0:PAD], 0.0)
            v.memset(BA[:, 0:PAD], 0.0)
            v.wait_ge(ht_ready, KT)
            v.memset(CV[:, :, 0:PAD], 0.0)
            v.memset(RAW[:, :, 0:PAD], 0.0)
            v.drain().then_inc(zeroed, 1)
            v.wait_ge(pev, 15)
            LD = view(A_MG, 3, TP)
            for j, mu in enumerate(("mu_wa", "mu_g1", "mu_g2")):
                r = 32 if j == 2 else 128
                v.tensor_tensor(LD[0:r, j, PAD:TP], LR[0:r, j, PAD - 1:TP - 1], LR[0:r, j, PAD:TP], ALU.subtract)
            v.drain()
            for j, mu in enumerate(("mu_wa", "mu_g1", "mu_g2")):
                r = 32 if j == 2 else 128
                v.scalar_tensor_tensor(LR[0:r, j, PAD:TP], LD[0:r, j, PAD:TP], par_(mu, 0, r), LR[0:r, j, PAD:TP], ALU.mult, ALU.add)
            v.drain().then_inc(s_lr, 1)
            v.wait_ge(s_crt, 2)
            for a in range(2):
                v.reciprocal(RN[:, a, 0:T], RN[:, a, 0:T])
            v.drain()
            for i in range(10):
                g = par_("qnorm", i) if i < 6 else par_("kvnorm", i - 6)
                v.scalar_tensor_tensor(CQKV[:, i, :], CQKV[:, i, :], g, RN[:, int(i >= 6), 0:T], ALU.mult, ALU.mult).then_inc(s_cn, 1)
            v.wait_ge(pev, M_QUP)
            with v.Fori(0, 24) as i:
                def tap(j):
                    return PARAM[:, ds(i + (PAR.at["conv"] + 24 * j), 1)]
                dst = CV[:, ds(i, 1), PAD:TP]
                v.tensor_scalar(dst, RAW[:, ds(i, 1), PAD - 3:TP - 3], tap(0), None, ALU.mult)
                for j in range(1, 4):
                    v.drain()
                    mm = v.scalar_tensor_tensor(dst, RAW[:, ds(i, 1), PAD - 3 + j:TP - 3 + j], tap(j), dst, ALU.mult, ALU.add)
                mm.then_inc(s_conv, 1)
            for i in range(5):
                v.wait_ge(s_rot, i + 1)
                if i < 4:
                    p = psum[4 + i % 2][0:64, 0:512].rearrange("p (h t) -> p h t", h=2)
                    q = QPE[0:64, 2 * i:2 * i + 2, :]
                    co = con_("cos", 64)[:, META:T].unsqueeze(1).broadcast_to([64, 2, SEQ])
                    si = con_("sin", 64)[:, META:T].unsqueeze(1).broadcast_to([64, 2, SEQ])
                    tmp = view(A_MT, 2, SEQ)[0:64]
                else:
                    p, q, co, si, tmp = psum[4][0:64, 0:T], KPE[0:64], con_("cos", 64), con_("sin", 64), view(A_MT, T)[0:64]
                v.tensor_tensor(tmp, p, si, ALU.mult)
                v.tensor_tensor(q, q, co, ALU.mult)
                v.drain()
                v.tensor_tensor(q, q, tmp, ALU.add).then_inc(s_rotd, 1)
                v.drain()
            for i in range(17):
                if i < 16:
                    a = i % 2
                    nk = META + 128 * (a + 1)
                    v.wait_ge(a_sc, i + 1)
                    v.scalar_tensor_tensor(SS[:, i % 2, 0:nk], psum[4 + i % 2][:, 0:nk], 192.0 ** -0.5,
                                           con_("causal")[:, T - nk:T], ALU.mult, ALU.add)
                    v.drain()
                    v.tensor_reduce(stats[:, 10 + i % 2:11 + i % 2], SS[:, i % 2, 0:nk], AX.X, ALU.max, negate=True).then_inc(a_sm, 1)
                if i >= 1:
                    i_ = i - 1
                    nk = META + 128 * (i_ % 2 + 1)
                    v.wait_ge(a_ex, i_ + 1)
                    v.reciprocal(stats[:, 14:15], stats[:, 12 + i_ % 2:13 + i_ % 2])
                    v.drain()
                    v.tensor_scalar(PX[:, i_ % 2, 0:nk], PX[:, i_ % 2, 0:nk], stats[:, 14:15], None, ALU.mult).then_inc(a_pn, 1)
                    v.drain()
            if STOP == "mla":
                return
            v_gdn(v)
            if STOP == "gdn":
                return
            v_rest(v)

        @block.gpsimd
        def _(pool):
            if STOP == "mla":
                return
            pool_gdn(pool)
            if STOP == "gdn":
                return
            pool_rest(pool)


program.stop = None
_INS = ["x", "meta", "par", "con", "w_in", "w_q_up", "w_kv_up", "w2", "a2", "g2", "w_branch", "w_out",
        "norm_ffn", "norm_final", "w_rg", "w_re", "b_rg", "b_re", "e_gate", "e_up", "e_down"]


def arrays_of(inputs):
    i = {k: np.ascontiguousarray(v) for k, v in inputs.items()}
    return {"x": i["x"][0], "meta": i["meta_tokens"], "par": per_channel(i), "con": constants(),
            "w_in": i["w_in"][0], "w_q_up": i["mla_w_q_up"][0], "w_kv_up": i["mla_w_kv_up"][0],
            "w2": i["rwkv_w2"][0], "a2": i["rwkv_a2"][0], "g2": i["rwkv_g2"][0],
            "w_branch": i["w_branch"][0], "w_out": i["w_out"][0],
            "norm_ffn": i["norm_ffn"], "norm_final": i["norm_final"][None],
            "w_rg": i["w_router_group"][0], "w_re": i["w_router_expert"][0],
            "b_rg": i["b_router_group"], "b_re": i["b_router_expert"],
            "e_gate": i["w_exp_gate"][0], "e_up": i["w_exp_up"][0], "e_down": i["w_exp_down"][0]}


def kernel(**inputs):
    import concourse.bacc as _bacc
    from concourse.bass_utils import run_bass_kernel_spmd as _run

    nc = _bacc.Bacc("TRN2", target_bir_lowering=False, num_devices=1)
    given = arrays_of(inputs)
    arrays, args = {}, []
    for name in _INS:
        a = np.ascontiguousarray(given[name])
        arrays[f"in_{name}"] = a
        args.append(nc.dram_tensor(f"in_{name}", a.shape, mybir.dt.from_np(a.dtype), kind="ExternalInput").ap())
    args.append(nc.dram_tensor("out_y", (SEQ, D), F32, kind="ExternalOutput").ap())
    program(nc, *args)
    r = _run(nc, [arrays], core_ids=[0])
    return r.results[0]["out_y"][None]
```

```python
from contextlib import ExitStack

import numpy as np

import concourse.bass as bass
from concourse import mybir

ALU = mybir.AluOpType
ACT = mybir.ActivationFunctionType
AX = mybir.AxisListType
F32 = mybir.dt.float32
I32 = mybir.dt.int32
U32 = mybir.dt.uint32
ds = bass.ds

D, SEQ, META = 2048, 256, 16
T = SEQ + META
PAD = 16
TP = T + PAD
C = 32
NC = TP // C
KT = D // 128
GH = 8
GQ = GH // 4
RH = 16
RQ = RH // 4
QL, KVL, ROPE, MH = 768, 512, 64, 8
BR = 1024
EPS = 1e-6
RLN_EPS = 64e-5
NE, NG, EPG, DE = 32, 4, 8, 512
CAP = 64
IN0_BA = 4096
IN0_CQ = IN0_BA + 16
IN0_CKV = IN0_CQ + QL
IN0_KPE = IN0_CKV + KVL
IN0_RKV = IN0_KPE + ROPE
IN0_LORA = IN0_RKV + 3 * BR
IN0_GATE = IN0_LORA + 288


class Columns:

    def __init__(self, widths):
        self.at, self.width, n = {}, {}, 0
        for name, w in widths:
            self.at[name], self.width[name] = n, w
            n += w
        self.n = n


PAR = Columns([("norm_mix", 16), ("conv", 96), ("alog", 2), ("dtb", 2), ("gdn_norm", 1), ("qnorm", 6),
               ("kvnorm", 4), ("mu", 24), ("mu_wa", 1), ("mu_g1", 1), ("mu_g2", 1), ("w0", 8), ("a0", 8),
               ("k_k", 8), ("k_a", 8), ("r_k", 8), ("ln_w", 8), ("ln_b", 8)])
CON = Columns([("ident", 128), ("bd_le", 128), ("bd_gt", 128), ("bd_one", 128), ("ones", 128),
               ("one64", 128), ("lt", 128), ("m_le", 32), ("m_gt", 32), ("m4", 128), ("hm", 4), ("rot", 64),
               ("cos", T), ("sin", T), ("causal", T), ("eps", 1), ("rln_eps", 1), ("scan", TP),
               ("iota8", 8), ("iota32", 32), ("slot", 128), ])


def constants():
    p = np.arange(128)
    q = np.arange(32)
    out = np.zeros((128, CON.n), np.float32)

    def put(name, a):
        a = np.asarray(a, np.float32).reshape(len(a), -1)
        out[:len(a), CON.at[name]:CON.at[name] + CON.width[name]] = a

    same = (p[:, None] // 32) == (p[None] // 32)
    put("ident", np.eye(128))
    put("bd_le", same & (p[:, None] <= p[None]))
    put("bd_gt", same & (p[:, None] > p[None]))
    put("bd_one", same)
    put("ones", np.ones((128, 128)))
    put("one64", (p[:, None] // 64) == (p[None] // 64))
    put("lt", p[:, None] < p[None])
    le = (p % 32)[:, None] <= q[None]
    gt = (p % 32)[:, None] > q[None]
    lt = (p % 32)[:, None] < q[None]
    put("m_le", le)
    put("m_gt", gt)
    put("m4", np.concatenate([gt, le, lt, le], 1))
    put("hm", (p // 32)[:, None] == np.arange(4)[None])
    rot = np.zeros((64, 64))
    for i in range(32):
        rot[i + 32, i] = -1.0
        rot[i, i + 32] = 1.0
    put("rot", rot)
    inv = np.float32(10000.0) ** (-np.arange(0, 64, 2, dtype=np.float32) / np.float32(64))
    ang = (np.arange(T, dtype=np.float32)[:, None] * inv[None].astype(np.float32)).T
    put("cos", np.concatenate([np.cos(ang)] * 2, 0))
    put("sin", np.concatenate([np.sin(ang)] * 2, 0))
    causal = np.zeros((128, T))
    causal[:, T - 128:] = np.where(p[None] <= p[:, None], 0.0, -1e30)
    put("causal", causal)
    put("eps", np.full((128, 1), EPS))
    put("rln_eps", np.full((128, 1), RLN_EPS))
    put("scan", np.tile((np.arange(TP) % C != 0)[None], (128, 1)))
    put("iota8", np.tile(np.arange(8)[None], (128, 1)))
    put("iota32", np.tile(np.arange(32)[None], (128, 1)))
    put("slot", np.tile((p % CAP)[None], (128, 1)))
    return out


def per_channel(inputs):
    out = np.zeros((128, PAR.n), np.float32)

    def put(name, a):
        out[:a.shape[0], PAR.at[name]:PAR.at[name] + PAR.width[name]] = a

    def cols(a):
        return np.ascontiguousarray(a.reshape(-1, 128).T)

    put("norm_mix", cols(inputs["norm_mix"][0]))
    put("conv", np.ascontiguousarray(inputs["gdn_conv"][0].reshape(4, 24, 128).transpose(2, 0, 1).reshape(128, 96)))
    put("alog", np.repeat(inputs["gdn_a_log"][0].reshape(2, 4).T, 32, 0))
    put("dtb", np.repeat(inputs["gdn_dt_bias"][0].reshape(2, 4).T, 32, 0))
    put("gdn_norm", inputs["gdn_norm"][0][:, None])
    put("qnorm", cols(inputs["mla_q_norm"][0]))
    put("kvnorm", cols(inputs["mla_kv_norm"][0]))
    mu = inputs["rwkv_mu"][0]
    put("mu", cols(mu[:3072]))
    put("mu_wa", mu[3072:3200, None])
    put("mu_g1", mu[3200:3328, None])
    put("mu_g2", mu[3328:3360, None])
    for name, key in (("w0", "rwkv_w0"), ("a0", "rwkv_a0"), ("k_k", "rwkv_k_k"), ("k_a", "rwkv_k_a"),
                      ("r_k", "rwkv_r_k"), ("ln_w", "rwkv_ln_w"), ("ln_b", "rwkv_ln_b")):
        put(name, cols(inputs[key][0].reshape(-1)))
    return out


N_SMALL, N_QKV, N_QUP, N_KVUP, N_Z, N_RKV, N_LORA = 0, 15, 39, 47, 51, 59, 83
N_MERGE = 86
N_OUT = N_MERGE + 72
M_SMALL, M_QKV, M_QUP, M_KVUP, M_Z, M_RKV, M_LORA = 0, 15, 39, 55, 75, 83, 107
M_MERGE = 131
M_OUT = M_MERGE + 96


def uses_with(n):
    if n < N_QUP:
        return n + 1
    if n < N_KVUP:
        return M_QUP + 2 * (n - N_QUP) + 2
    if n < N_Z:
        return M_KVUP + 5 * (n - N_KVUP) + 5
    if n < N_LORA:
        return M_Z + n - N_Z + 1
    if n < N_MERGE:
        return M_LORA + (16 if n == N_LORA else 24)
    if n < N_OUT:
        pair, what = divmod(n - N_MERGE, 3)
        return M_MERGE + 4 * pair + (4, 1, 3)[what]
    return M_OUT + 2 * ((n - N_OUT) // 2) + 2


BRANCHES = (1, 0, 2)


def program(nc, x, meta, par, con, w_in, w_q_up, w_kv_up, w2, a2, g2, w_branch, w_out,
            norm_ffn, norm_final, w_rg, w_re, b_rg, b_re, e_gate, e_up, e_down, out):
    nc_dram = {}

    def dram(name, shape, dt=F32):
        return nc.dram_tensor(name, shape, dt, kind="Internal").ap()

    gdn_a = dram("gdn_a", [GQ * 4 * NC, C * C])
    gdn_u = dram("gdn_u", [GQ * 4 * NC, C * C])
    rwkv_a = dram("rwkv_a", [RQ * 4 * NC, C * C])
    rwkv_u = dram("rwkv_u", [RQ * 4 * NC, C * C])

    with ExitStack() as ctx:
        def sem(name):
            return ctx.enter_context(nc.semaphore(name))

        arena = ctx.enter_context(nc.sbuf_tensor("arena", [128, 53200], F32))
        psum = [ctx.enter_context(nc.psum_tensor(f"bank{i}", [128, 512], F32)) for i in range(8)]
        place = [0]

        def view(at, *shape):
            n = int(np.prod(shape))
            a = arena[:, at:at + n]
            if len(shape) == 2:
                a = a.rearrange("p (a b) -> p a b", a=shape[0])
            if len(shape) == 3:
                a = a.rearrange("p (a b c) -> p a b c", a=shape[0], b=shape[1])
            if len(shape) == 4:
                a = a.rearrange("p (a b c d) -> p a b c d", a=shape[0], b=shape[1], c=shape[2])
            return a

        def new(*shape):
            at = place[0]
            place[0] += int(np.prod(shape))
            assert place[0] <= 53200, place[0]
            return view(at, *shape)

        CONST = new(CON.n)
        PARAM = new(PAR.n)

        def con_(name, rows=128):
            return CONST[0:rows, CON.at[name]:CON.at[name] + CON.width[name]]

        def par_(name, j=0, rows=128):
            return PARAM[0:rows, PAR.at[name] + j:PAR.at[name] + j + 1]

        ident = con_("ident")
        stats = new(400)
        A_RING = place[0]
        ring = new(4, 2048)
        HT = new(KT, T)
        A_Y = place[0]
        Y = new(3, 8, SEQ)
        A_MG = place[0]
        MG = new(KT, SEQ)
        W0 = place[0]
        Z = ZR = new(8, SEQ)
        CV = new(24, TP)
        AT = new(NC, GQ, C)
        AM = new(NC, GQ, C)
        TT = new(NC, GQ, C)
        DT = new(NC * GQ, C)
        DA = new(NC * GQ, C)
        S = new(8, 128)
        KD = new(2, GQ, 128)
        VB = new(2, GQ, 128)
        R = new(GQ, 128)
        VN = new(GQ, 128)
        O1 = new(GQ, 128)
        GU = view(A_MG + 3072, NC * GQ, C)
        BT = new(NC, 4)
        GS_ = new(8, NC * GQ)
        GL = new(NC * GQ, 4)
        A_SQ = place[0]
        SQ = new(2, TP)
        RN = new(2, TP)
        GM = view(A_SQ, NC * GQ, 4)
        A_RAW = place[0]
        RAW = new(24, TP)
        A_TAIL = place[0]
        CQKV = new(10, T)
        KPE = new(T)
        LR = new(3, TP)
        BA = new(TP)
        KN = view(A_RAW, 8, T)
        VT = view(A_RAW + 8 * T, 3, 1024)
        QN = view(A_Y + 2 * 8 * SEQ, 8, SEQ)
        QPE = view(A_MG, 8, SEQ)
        A_MT = A_MG + 8 * SEQ
        SS = view(A_MT, 2, T)
        PX = view(A_MT + 2 * T, 2, T)
        PT = view(A_MT + 4 * T, 2, 384)
        IA = view(A_MG, 1024)
        IU = view(A_MG + 1024, 1024)
        IT = view(A_MG + 2048, 1024)
        GU2 = view(A_MG + 2048, NC * GQ, C)
        O = view(A_MG, 8, GQ, 128)

        ld = sem("inputs_loaded")
        zeroed = sem("pads_zeroed")
        sq0 = sem("token_squares")
        rt0 = sem("token_roots")
        xn_ready = sem("tokens_normed")
        ht_t = sem("tokens_transposed")
        ht_ready = sem("ht_ready")
        wld = [sem(f"weights_loaded{i}") for i in range(4)]
        pdone = sem("products_done")
        pev = sem("products_evacuated")
        s_csq = sem("latent_squared")
        s_csqf = sem("latent_square_read")
        s_crt = sem("latent_rooted")
        s_cn = sem("latent_normed")
        s_lr = sem("lora_mixed")
        s_conv = sem("conv_done")
        s_rot = sem("rotated_by_pe")
        s_rotd = sem("rotated")
        a_sc, a_sm, a_ex, a_pn = sem("scores"), sem("masked"), sem("exps"), sem("probs")
        a_pt, a_pc, a_o, a_oc = sem("probs_turned"), sem("probs_copied"), sem("heads_out"), sem("heads_kept")

        XT = view(W0, 2, D)
        XM = view(W0 + 2 * D, D)
        XJ = view(W0 + 3 * D, D)

        b_t, b_b, b_c, b_g, b_p = sem("ba_turned"), sem("ba_copied"), sem("ba_functions"), sem("log_decays"), sem("log_decay_sums")
        b_x, b_gt, b_d = sem("decay_exps"), sem("gc_differences"), sem("decays_masked")
        l_sq, l_ss, l_rt, l_n = sem("qk_squared"), sem("qk_sums"), sem("qk_roots"), sem("qk_normed")
        s_silu = sem("conv_silu")
        g_a, g_am = sem("gdn_products"), sem("gdn_a_masked")
        d_aw, d_al, d_inv, d_uw, d_ul = sem("a_stored"), sem("a_loaded"), sem("a_inverted"), sem("inverse_stored"), sem("inverse_loaded")
        k_tok, k_tc, k_ks, k_r, k_vn, k_vc = (sem("gdn_tokens_turned"), sem("gdn_tokens_kept"), sem("state_products"),
                                              sem("gdn_rhs"), sem("v_new"), sem("v_new_kept"))
        k_su, k_s, k_o1, k_oo = sem("state_increments"), sem("state_updated"), sem("state_outputs"), sem("chunk_outputs")
        k_n, k_nr, k_t, k_y = sem("o_squares"), sem("o_roots"), sem("o_normed"), sem("o_turned")
        k_yd = sem("gdn_output")
        raw_free = sem("raw_pads_zeroed_again")
        SCQ = 128.0 ** -0.5
        INC = ((2, 0), (3, 0), (6, 256), (7, 256))
        QK = CV.rearrange("p (a h) t -> p a h t", a=3)

        def grow(j):
            return GS_[:, j, :]

        def pool_gdn(pool):
            pool.wait_ge(g_am, NC)
            for h in range(4):
                pool.dma_start(gdn_a.rearrange("(h c) (t s) -> h t c s", h=4, t=C)[h],
                             AM.rearrange("p c q s -> p (c q) s")[32 * h:32 * h + 32]).then_inc(d_aw, 16)
            pool.wait_ge(d_aw, 64)
            pool.dma_start(IA[0:72], gdn_a).then_inc(d_al, 16)
            pool.wait_ge(d_inv, 1)
            pool.dma_start(gdn_u, IU[0:72]).then_inc(d_uw, 16)
            pool.wait_ge(d_uw, 16)
            for h in range(4):
                pool.dma_start(TT.rearrange("p c q s -> p (c q) s")[32 * h:32 * h + 32],
                             gdn_u.rearrange("(h c) (s t) -> h s c t", h=4, s=C)[h]).then_inc(d_ul, 16)

        def rkv_block(pe, j):
            in_block(pe, N_RKV + j, M_RKV + j)

        def rkv_evac(act, j):
            evac(act, M_RKV + j, RAW[:, j, PAD:TP])

        def pe_gdn(pe):
            pe.wait_ge(a_oc, 16)
            pe.wait_ge(a_pc, 16)
            for c in range(NC):
                for h in range(4):
                    mm = pe.matmul(psum[6][32 * h:32 * h + 32, 4 * c:4 * c + 4], BA[0:16, C * c:C * c + C],
                                   ident[0:16, h:16:4], start=True, stop=True, tile_position=(0, 32 * h))
            mm.then_inc(b_t, 1)
            pe.wait_ge(b_g, 1)
            g = grow(1)
            pe.matmul(psum[6][:, 64:82], con_("bd_le"), g, start=True, stop=True)
            pe.matmul(psum[6][:, 96:114], con_("bd_one"), g, start=True, stop=True)
            pe.matmul(psum[6][:, 128:200], con_("ones"), GM.rearrange("p a b -> p (a b)"), start=True, stop=True).then_inc(b_p, 1)
            GUf = GU.rearrange("p a b -> p (a b)")
            for a in range(2):
                mm = pe.matmul(psum[4 + a][:, 0:288], con_("bd_gt"), GUf[:, 288 * a:288 * a + 288], start=True, stop=True)
            mm.then_inc(b_p, 1)
            pe.wait_ge(b_g, 2)
            GUf = GU2.rearrange("p a b -> p (a b)")
            pe.matmul(psum[7][:, 0:288], con_("bd_le"), GUf[:, 0:288], start=True, stop=True).then_inc(b_p, 1)
            pe.wait_ge(b_x, 2)
            pe.matmul(psum[4][:, 0:288], con_("bd_le"), GUf[:, 288:576], start=True, stop=True).then_inc(b_p, 1)
            for i in range(16):
                pe.wait_ge(l_sq, i + 1)
                if i == 0:
                    pe.wait_ge(b_x, 4)
                if i >= 2:
                    pe.wait_ge(l_rt, i - 1)
                pe.matmul(psum[4 + i % 2][:, 0:TP], con_("ones"), SQ[:, i % 2, :], start=True, stop=True).then_inc(l_ss, 1)
                if i % 4 == 3:
                    rkv_block(pe, i // 4)
            pe.wait_ge(l_n, 16)
            for c in range(NC):
                if c >= 2:
                    pe.wait_ge(g_am, c - 1)
                for h in range(8):
                    mm = pe.matmul(psum[4 + c % 2][32 * (h % 4):32 * (h % 4) + 32, 64 * (h // 4):64 * (h // 4) + 64],
                                   QK[:, 1, h, C * c:C * c + C], QK[:, 0:2, h, C * c:C * c + C],
                                   start=True, stop=True, tile_position=(0, 32 * (h % 4)))
                mm.then_inc(g_a, 1)
            for j in range(4, 13):
                rkv_block(pe, j)

            def tokens(c):
                if c:
                    pe.wait_ge(k_tc, c)
                for a in range(2):
                    for h in range(8):
                        at = 256 * a + 128 * (h // 4)
                        mm = pe.matmul(psum[4][32 * (h % 4):32 * (h % 4) + 32, at:at + 128], QK[:, 1 + a, h, C * c:C * c + C],
                                       ident, start=True, stop=True, tile_position=(0, 32 * (h % 4)))
                mm.then_inc(k_tok, 1)

            pe.wait_ge(g_am, NC)
            tokens(0)
            pe.wait_ge(d_ul, 64)
            for c in range(NC):
                if c:
                    pe.wait_ge(k_s, c)
                    if c > 1:
                        pe.wait_ge(k_o1, c - 1)
                    for a in range(2):
                        for h in range(8):
                            at = 256 * a + 128 * (h // 4)
                            mm = pe.matmul(psum[5][32 * (h % 4):32 * (h % 4) + 32, at:at + 128],
                                           QK[:, 1 - a, h, C * c:C * c + C], S[:, h, :],
                                           start=True, stop=True, tile_position=(0, 32 * (h % 4)))
                    mm.then_inc(k_ks, 1)
                pe.wait_ge(k_r, c + 1)
                for h in range(8):
                    p = slice(32 * (h % 4), 32 * (h % 4) + 32)
                    at = 128 * (h // 4)
                    mm = pe.matmul(psum[6][p, at:at + 128], TT[p, c, h // 4, :], R[p, h // 4, :], start=True, stop=True,
                                   tile_position=(32 * (h % 4), 32 * (h % 4)))
                mm.then_inc(k_vn, 1)
                if c + 1 < NC:
                    tokens(c + 1)
                pe.wait_ge(k_vc, c + 1)
                for h in range(8):
                    p = slice(32 * (h % 4), 32 * (h % 4) + 32)
                    b, at = INC[h % 4]
                    mm = pe.matmul(psum[b][:, at + 128 * (h // 4):at + 128 * (h // 4) + 128], KD[p, c % 2, h // 4, :], VN[p, h // 4, :],
                                   start=True, stop=True, tile_position=(32 * (h % 4), 0))
                mm.then_inc(k_su, 1)
                if c:
                    if c > 1:
                        pe.wait_ge(k_oo, c - 1)
                    for h in range(8):
                        p = slice(32 * (h % 4), 32 * (h % 4) + 32)
                        at = 128 * (h // 4)
                        mm = pe.matmul(psum[7][p, at:at + 128], AT[p, c, h // 4, :], VN[p, h // 4, :], start=True, stop=True,
                                       tile_position=(32 * (h % 4), 32 * (h % 4)))
                    mm.then_inc(k_t, 1)
                rkv_block(pe, 13 + c)
            rkv_block(pe, 22)
            rkv_block(pe, 23)
            pe.wait_ge(k_n, 3)
            for g in range(4):
                if g >= 2:
                    pe.wait_ge(k_yd, g - 1)
                for j in range(4):
                    mm = pe.transpose(psum[4 + g % 2][:, 128 * j:128 * j + 128], O[:, 2 * g + j // 2, j % 2, :], ident)
                mm.then_inc(k_y, 1)

        def act_gdn(act):
            act.wait_ge(s_conv, 24)
            act.activation(Z, ZR, ACT.Silu)
            for a in range(3):
                act.activation(CV[:, 8 * a:8 * a + 8, PAD:TP], CV[:, 8 * a:8 * a + 8, PAD:TP], ACT.Silu)
            act.drain().then_inc(s_silu, 1)
            act.wait_ge(b_b, 1)
            act.activation(grow(0).rearrange("p (c q) -> p c q", c=NC), BT[:, :, 0:2], ACT.Sigmoid)
            act.activation(grow(7), grow(6), ACT.Abs)
            act.activation(stats[:, 20:22], PARAM[:, PAR.at["alog"]:PAR.at["alog"] + 2], ACT.Exp)
            act.drain()
            act.activation(grow(7), grow(7), ACT.Exp, scale=-1.0)
            act.drain()
            act.activation(grow(7), grow(7), ACT.Ln, bias=con_("ones")[:, 0:1])
            act.drain().then_inc(b_c, 1)
            act.wait_ge(b_gt, 1)
            act.activation(grow(5), grow(2), ACT.Exp)
            act.activation(grow(3), grow(3), ACT.Exp)
            act.activation(GL.rearrange("p a b -> p (a b)"), psum[6][:, 128:200], ACT.Exp)
            act.drain().then_inc(b_x, 1)
            act.wait_ge(b_p, 2)
            for a in range(2):
                act.activation(DT[:, 9 * a:9 * a + 9, :], psum[4 + a][:, 0:288].rearrange("p (a b) -> p a b", a=9), ACT.Exp)
            act.drain().then_inc(b_x, 1)
            act.wait_ge(b_p, 3)
            act.activation(DA[:, 0:9, :], psum[7][:, 0:288].rearrange("p (a b) -> p a b", a=9), ACT.Exp).then_inc(b_x, 1)
            act.wait_ge(b_p, 4)
            act.activation(DA[:, 9:18, :], psum[4][:, 0:288].rearrange("p (a b) -> p a b", a=9), ACT.Exp).then_inc(b_x, 1)
            act.drain()
            for i in range(17):
                if i < 16:
                    if i >= 2:
                        act.wait_ge(l_ss, i - 1)
                    act.activation(SQ[:, i % 2, :], CV[:, i, :], ACT.Square).then_inc(l_sq, 1)
                if i:
                    act.wait_ge(l_ss, i)
                    if i > 2:
                        act.wait_ge(l_n, i - 2)
                    act.activation(RN[:, (i - 1) % 2, :], psum[4 + (i - 1) % 2][:, 0:TP], ACT.Sqrt, bias=con_("eps")).then_inc(l_rt, 1)
                    if i % 4 == 0:
                        act.wait_ge(raw_free, 1)
                        rkv_evac(act, i // 4 - 1)
            for j in range(4, 13):
                rkv_evac(act, j)

            def keep(c):
                act.wait_ge(k_tok, c + 1)
                if c >= 2:
                    act.wait_ge(k_su, c - 1)
                    act.wait_ge(k_r, c - 1)
                for q in range(GQ):
                    act.activation(KD[:, c % 2, q, :], psum[4][:, 128 * q:128 * q + 128], ACT.Copy,
                                   scale=grow(3)[:, 2 * c + q:2 * c + q + 1])
                    act.activation(VB[:, c % 2, q, :], psum[4][:, 256 + 128 * q:384 + 128 * q], ACT.Copy,
                                   scale=grow(0)[:, 2 * c + q:2 * c + q + 1])
                act.drain().then_inc(k_tc, 1)

            keep(0)
            for c in range(NC):
                act.wait_ge(k_vn, c + 1)
                if c:
                    act.wait_ge(k_su, c)
                    if c > 1:
                        act.wait_ge(k_t, c - 1)
                act.activation(VN.rearrange("p a b -> p (a b)"), psum[6][:, 0:256], ACT.Copy).then_inc(k_vc, 1)
                if c:
                    if c > 1:
                        act.wait_ge(k_oo, c - 1)
                    for q in range(GQ):
                        act.activation(O1[:, q, :], psum[5][:, 256 + 128 * q:384 + 128 * q], ACT.Copy,
                                       scale=grow(5)[:, 2 * c + q:2 * c + q + 1])
                    act.drain().then_inc(k_o1, 1)
                if c + 1 < NC:
                    keep(c + 1)
                rkv_evac(act, 13 + c)
            rkv_evac(act, 22)
            rkv_evac(act, 23)
            act.wait_ge(k_n, 1)
            act.activation(stats[:, 40:56], stats[:, 24:40], ACT.Sqrt, scale=1.0 / 128, bias=con_("eps")).then_inc(k_nr, 1)

        def invert(v, A, U, tmp, z):
            for t in range(1, C):
                a = A[:, :, t, 0:t].unsqueeze(2).broadcast_to([72, z, t, t])
                w = tmp[:, 0:z * t * t].rearrange("p (z s k) -> p z s k", z=z, s=t)
                if z == 1:
                    v.tensor_tensor(w[:, 0], U[:, 0, 0:t, 0:t], a[:, 0], ALU.mult)
                else:
                    for y in range(z):
                        v.tensor_tensor(w[:, y], U[:, y, 0:t, 0:t], a[:, y], ALU.mult)
                v.drain()
                for y in range(z):
                    v.tensor_reduce(U[:, y, 0:t, t:t + 1], w[:, y], AX.X, ALU.add)
                v.drain()

        def unit(v, U, z):
            v.memset(U, 0.0)
            v.drain()
            v.memset(U.rearrange("p (z a) -> p z a", z=z)[:, :, 0:C * C:C + 1], 1.0)
            v.drain()

        def v_gdn(v):
            v.wait_ge(a_oc, 16)
            v.memset(RAW[:, :, 0:PAD], 0.0).then_inc(raw_free, 1)
            v.wait_ge(b_t, 1)
            v.tensor_copy(BT.rearrange("p a b -> p (a b)"), psum[6][:, 0:36])
            v.drain()
            dtb = PARAM[:, PAR.at["dtb"]:PAR.at["dtb"] + 2].unsqueeze(1).broadcast_to([128, NC, 2])
            v.tensor_tensor(grow(6).rearrange("p (c q) -> p c q", c=NC), BT[:, :, 2:4], dtb, ALU.add).then_inc(b_b, 1)
            v.wait_ge(b_c, 1)
            v.scalar_tensor_tensor(grow(7), grow(6), 0.0, grow(7), ALU.max, ALU.add)
            v.drain()
            ea = stats[:, 20:22].unsqueeze(1).broadcast_to([128, NC, 2])
            v.scalar_tensor_tensor(grow(1).rearrange("p (c q) -> p c q", c=NC), grow(7).rearrange("p (c q) -> p c q", c=NC),
                                   -1.0, ea, ALU.mult, ALU.mult)
            v.drain()
            n = NC * GQ
            g4 = grow(1).unsqueeze(2)
            v.tensor_tensor(GM, g4.broadcast_to([128, n, 4]), con_("hm").unsqueeze(1).broadcast_to([128, n, 4]), ALU.mult)
            v.tensor_tensor(GU, g4.broadcast_to([128, n, C]), con_("m_le").unsqueeze(1).broadcast_to([128, n, C]), ALU.mult)
            v.drain().then_inc(b_g, 1)
            v.tensor_tensor(GU2, g4.broadcast_to([128, n, C]), con_("m_gt").unsqueeze(1).broadcast_to([128, n, C]), ALU.mult).then_inc(b_g, 1)
            v.wait_ge(b_p, 1)
            v.tensor_copy(grow(2), psum[6][:, 64:82])
            v.drain()
            v.tensor_tensor(grow(3), psum[6][:, 96:114], grow(2), ALU.subtract)
            v.drain().then_inc(b_gt, 1)
            v.wait_ge(b_x, 4)
            v.scalar_tensor_tensor(grow(4), grow(0), -1.0, grow(5), ALU.mult, ALU.mult)
            v.scalar_tensor_tensor(DT, DT, SCQ, con_("m_le").unsqueeze(1).broadcast_to([128, n, C]), ALU.mult, ALU.mult)
            v.scalar_tensor_tensor(DA, DA, -1.0, con_("m_gt").unsqueeze(1).broadcast_to([128, n, C]), ALU.mult, ALU.mult)
            v.drain()
            v.tensor_scalar(grow(5), grow(5), SCQ, None, ALU.mult)
            v.tensor_tensor(DA, DA, grow(0).unsqueeze(2).broadcast_to([128, n, C]), ALU.mult)
            v.drain()
            for i in range(16):
                v.wait_ge(l_rt, i + 1)
                v.reciprocal(RN[:, i % 2, :], RN[:, i % 2, :])
                v.drain()
                v.tensor_tensor(CV[:, i, :], CV[:, i, :], RN[:, i % 2, :], ALU.mult).then_inc(l_n, 1)
            unit(v, IU[0:72], 1)
            for c in range(NC):
                v.wait_ge(g_a, c + 1)
                b = psum[4 + c % 2][:, 0:128].rearrange("p (q a t) -> p q a t", q=2, a=2)
                v.tensor_tensor(AT[:, c], b[:, :, 0], DT[:, 2 * c:2 * c + 2], ALU.mult)
                v.tensor_tensor(AM[:, c], b[:, :, 1], DA[:, 2 * c:2 * c + 2], ALU.mult)
                v.drain().then_inc(g_am, 1)
            v.wait_ge(d_al, 16)
            invert(v, IA[0:72].rearrange("p (z t s) -> p z t s", z=1, t=C), IU[0:72].rearrange("p (z s t) -> p z s t", z=1, s=C),
                   IT[0:72], 1)
            v.drain().then_inc(d_inv, 1)
            for c in range(NC):
                v.wait_ge(k_tc, c + 1)
                if c:
                    v.wait_ge(k_ks, c)
                    v.wait_ge(k_vn, c)
                    for q in range(GQ):
                        v.scalar_tensor_tensor(R[:, q, :], psum[5][:, 128 * q:128 * q + 128], grow(4)[:, 2 * c + q:2 * c + q + 1],
                                               VB[:, c % 2, q, :], ALU.mult, ALU.add)
                else:
                    v.tensor_copy(R, VB[:, 0])
                v.drain().then_inc(k_r, 1)
                v.wait_ge(k_su, c + 1)
                if c:
                    for h in (0, 4, 1, 5, 2, 6, 3, 7):
                        b, at = INC[h % 4]
                        if h == 3:
                            v.wait_ge(k_t, c)
                        v.scalar_tensor_tensor(S[:, h, :], S[:, h, :], GL[:, 2 * c + h // 4, h % 4:h % 4 + 1],
                                               psum[b][:, at + 128 * (h // 4):at + 128 * (h // 4) + 128], ALU.mult, ALU.add)
                else:
                    for a in range(4):
                        b, at = INC[a]
                        v.tensor_copy(S[:, a:8:4, :], psum[b][:, at:at + 256].rearrange("p (a b) -> p a b", a=2))
                v.drain().then_inc(k_s, 1)
                if c:
                    v.wait_ge(k_o1, c)
                    v.tensor_tensor(O[:, c - 1], psum[7][:, 0:256].rearrange("p (a b) -> p a b", a=2), O1, ALU.add).then_inc(k_oo, 1)
            v.drain()
            O3, Q3 = O.rearrange("p c q n -> p (c q) n"), view(A_MG + 2048, 16, 128)
            v.tensor_tensor(Q3, O3, O3, ALU.mult)
            v.drain()
            v.tensor_reduce(stats[:, 24:40].unsqueeze(2), Q3, AX.X, ALU.add)
            v.drain().then_inc(k_n, 1)
            v.wait_ge(k_nr, 1)
            v.reciprocal(stats[:, 40:56], stats[:, 40:56])
            v.drain()
            v.tensor_tensor(O3, O3, stats[:, 40:56].unsqueeze(2).broadcast_to([128, 16, 128]), ALU.mult)
            v.drain().then_inc(k_n, 2)
            for g in range(4):
                v.wait_ge(k_y, g + 1)
                for j in range(4):
                    c, q = 2 * g + j // 2, j % 2
                    v.scalar_tensor_tensor(Y[:, 0, 4 * q:4 * q + 4, C * c:C * c + C],
                                           psum[4 + g % 2][:, 128 * j:128 * j + 128].rearrange("p (h t) -> p h t", h=4), par_("gdn_norm"),
                                           Z[:, 4 * q:4 * q + 4, C * c:C * c + C], ALU.mult, ALU.mult)
                v.drain().then_inc(k_yd, 1)

        CW = float(np.exp(-0.5))
        XR = view(W0, 3, 8, TP)
        XR24 = view(W0, 24, TP)
        SG = view(W0 + 24 * TP, 8, TP)
        CS = view(W0 + 32 * TP, 8, TP)
        RA = view(W0 + 40 * TP, 8, TP)
        RG = view(W0 + 48 * TP, 8, SEQ)
        PC = view(W0 + 48 * TP + 8 * SEQ, 8, NC)
        assert W0 + 48 * TP + 8 * SEQ + 8 * NC <= A_RAW
        T1, T2, T3 = (view(A_RAW + 8 * TP * i, 8, TP) for i in range(3))
        BON = Y[:, 2]
        BPR = view(W0 + 32 * TP, 8, SEQ)
        GB = view(A_TAIL, 2, SEQ)
        BB = view(A_TAIL + 512, 2, SEQ)
        IT2 = view(A_TAIL + 1024, 2 * 31 * 31)
        YO = view(A_TAIL + 1024, NC - 1, RQ, 64)
        AM4 = view(W0 + 32 * TP, NC, RQ, 128)
        IA2, IU2 = view(A_RAW, 2 * C * C), view(A_RAW + 8 * TP, 2 * C * C)
        TT2 = view(A_RAW, NC, RQ, C)
        SR = view(A_RAW + 1152, RQ, 64)
        SK = view(A_RAW + 1408, RQ, 64)
        RS = view(A_RAW + 1664, 8, 64)
        BK = view(A_RAW + 8 * TP, 2, RQ, 2, 64)
        VV = view(A_RAW + 8 * TP + 1024, 2, RQ, 64)
        YD = view(W0 + 16 * TP, 32, 64)
        YT = view(A_RAW + 8 * TP, 8, SEQ)
        RK = arena[:, W0:W0 + 48 * TP].rearrange("p (a h t) -> p a h t", a=2, h=24)[:, :, 0:8, :]
        H2 = view(A_RING + 8192, 2, D)

        r_lr, r_mix = sem("lora_inputs"), sem("rkv_mixed")
        r_ksq, r_kss, r_krt = sem("kk_squared"), sem("kk_sums"), sem("kk_roots")
        r_bin, r_bs, r_bd = sem("bonus_inputs"), sem("bonus_sums"), sem("bonus_done")
        r_cs, r_ex, r_el = sem("decay_sums"), sem("decay_factors"), sem("rwkv_operands")
        r_a, r_am = sem("rwkv_products"), sem("rwkv_products_masked")
        q_aw, q_al, q_inv, q_uw, q_ul = (sem("rwkv_a_stored"), sem("rwkv_a_loaded"), sem("rwkv_a_inverted"),
                                         sem("rwkv_inverse_stored"), sem("rwkv_inverse_loaded"))
        r_tok, r_tk, r_s0, r_sr, r_sa, r_ss = (sem("rwkv_tokens_turned"), sem("rwkv_tokens_kept"), sem("sa_rhs"),
                                               sem("sa_rhs_kept"), sem("sa_solved"), sem("sa_kept"))
        r_up, r_st, r_yo, r_yp = sem("rwkv_increments"), sem("rwkv_state"), sem("rwkv_chunk_kept"), sem("rwkv_chunk_out")
        r_yn, r_yt, r_v1, r_v2, r_y = sem("y_normed"), sem("y_turned"), sem("y_variance"), sem("y_root"), sem("rwkv_output")
        mg_in, mg_done = sem("merge_inputs"), sem("merged")
        xh, h2s = sem("residual_loaded"), sem("residual_added")

        U_SUMS, U_EXPS, U_PREP, U_CHAIN = 4, 7, 10, 20
        FILL = [U_CHAIN + 2 * c if c < 3 else U_CHAIN + 3 + c for c in range(NC)]
        FILL2 = [U_CHAIN + 2 * c + 1 if c < 3 else None for c in range(NC)]

        def half(h):
            return slice(64 * (h % 2), 64 * (h % 2) + 64)

        def quad(h):
            return slice(32 * (h % 4), 32 * (h % 4) + 32)

        def sp_rest(sp, load):
            load(N_LORA, w2, ring[0:64, N_LORA % 4, 0:BR])
            sp.dma_start(ring[64:128, N_LORA % 4, 0:BR], a2).then_inc(wld[N_LORA % 4], 16)
            load(N_LORA + 1, g2[0:128], ring[:, (N_LORA + 1) % 4, 0:BR])
            load(N_LORA + 2, g2[128:160], ring[0:32, (N_LORA + 2) % 4, 0:BR])
            win = w_in.rearrange("(k p) n -> p k n", p=128)

            def merge_loads(turn, s):
                b = BRANCHES[turn]
                wb = w_branch[b].rearrange("(k p) n -> p k n", p=128)
                for pair in range(4):
                    n = N_MERGE + 24 * turn + 12 * s + 3 * pair
                    at = BR * s + 256 * pair
                    load_w(n, wb[:, :, at:at + 256], 8, 256)
                    for j in range(2):
                        load_w(n + 1 + j, win[:, :, IN0_GATE + D * b + at + 128 * j:IN0_GATE + D * b + at + 128 * (j + 1)], 16, 128)

            def load_w(n, src, k, width):
                load(n, src, ring[:, n % 4, :].rearrange("p (k n) -> p k n", k=k))

            for turn in range(3):
                for s in range(2):
                    merge_loads(turn, s)
            if STOP == "mix":
                return
            sp_moe(sp)

        def pe_rest(pe):
            pe.wait_ge(r_lr, 1)
            n = N_LORA
            pe.wait_ge(wld[n % 4], 16 * (n // 4 + 1) + 16)
            m = M_LORA
            for p, rows in ((slice(0, 64), 0), (slice(64, 128), 64)):
                for j in range(8):
                    pe.wait_ge(pev, m - 1)
                    pe.matmul(psum[m % 2][:, 0:T], ring[p, n % 4, 128 * j:128 * (j + 1)], LR[p, 0, PAD:TP],
                              start=True, stop=True, tile_position=(rows, 0)).then_inc(pdone, 1)
                    m += 1
            weights1(pe, n + 1)
            weights1(pe, n + 2)
            for j in range(8):
                dense(pe, m, [(128, SEQ, ring[:, (n + 1) % 4, 128 * j:128 * (j + 1)], LR[:, 1, PAD + META:TP], True, False),
                              (128, SEQ, ring[0:32, (n + 2) % 4, 128 * j:128 * (j + 1)], LR[0:32, 2, PAD + META:TP], False, True)])
                m += 1
            for u in range(U_SUMS):
                merge_block(pe, u)
            for i in range(8):
                pe.wait_ge(r_ksq, 1)
                if i >= 2:
                    pe.wait_ge(r_krt, i - 1)
                pe.matmul(psum[4 + i % 2][:, 0:TP], con_("one64"), T2[:, i, :], start=True, stop=True).then_inc(r_kss, 1)
            for i in range(8):
                pe.wait_ge(r_bin, 1)
                if i >= 2:
                    pe.wait_ge(r_bd, i - 1)
                pe.matmul(psum[6 + i % 2][:, 0:SEQ], con_("one64"), BPR[:, i, :], start=True, stop=True).then_inc(r_bs, 1)
            for u in range(U_SUMS, U_PREP):
                merge_block(pe, u)
            pe.wait_ge(r_el, 1)
            for c in range(NC):
                if c >= 2:
                    pe.wait_ge(r_am, c - 1)
                t = slice(C * c, C * c + C)
                for h in range(RH):
                    i, at, b = h // 2, 128 * (h // 4), psum[4 + c % 2]
                    tp = (64 * (h % 2), 32 * (h % 4))
                    pe.matmul(b[quad(h), at:at + 32], SG[half(h), i, t], T3[half(h), i, t], start=True, stop=True, tile_position=tp)
                    pe.matmul(b[quad(h), at + 32:at + 96], XR[half(h), 1, i, t], RK[half(h), :, i, t],
                              start=True, stop=True, tile_position=tp)
                    mm = pe.matmul(b[quad(h), at + 96:at + 128], T3[half(h), i, t], XR[half(h), 0, i, t],
                                   start=True, stop=True, tile_position=tp)
                mm.then_inc(r_a, 1)
            for u in range(U_PREP, U_CHAIN):
                merge_block(pe, u)

            def tokens(c):
                if c:
                    pe.wait_ge(r_tk, c)
                    pe.wait_ge(r_st, c)
                t = slice(C * c, C * c + C)
                for h in range(RH):
                    i, q = h // 2, h // 4
                    for j, src in enumerate((T3[half(h), i, t], XR[half(h), 1, i, t], XR[half(h), 2, i, t])):
                        b, at = (psum[4], 128 * q + 64 * j) if j < 2 else (psum[5], 64 * q)
                        mm = pe.matmul(b[quad(h), at:at + 64], src, ident[half(h), half(h)], start=True, stop=True,
                                       tile_position=(64 * (h % 2), 32 * (h % 4)))
                mm.then_inc(r_tok, 1)

            pe.wait_ge(r_am, NC)
            tokens(0)
            pe.wait_ge(q_ul, 64)
            for c in range(NC):
                t = slice(C * c, C * c + C)
                pe.wait_ge(r_tk, c + 1)
                if c:
                    pe.wait_ge(r_st, c)
                for h in range(RH):
                    q, o = h // 4, psum[6][quad(h), 64 * (h // 4):64 * (h // 4) + 64]
                    if c:
                        pe.matmul(o, SG[half(h), h // 2, t], RS[half(h), h // 2, :], start=h < 4, stop=False,
                                  tile_position=(64 * (h % 2), 32 * (h % 4)), skip_group_check=True)
                for h in range(RH):
                    q, o = h // 4, psum[6][quad(h), 64 * (h // 4):64 * (h // 4) + 64]
                    mm = pe.matmul(o, AM4[quad(h), c, q, 64:96], VV[quad(h), c % 2, q, :], start=not c and h < 4, stop=True,
                                   tile_position=(32 * (h % 4), 32 * (h % 4)), skip_group_check=True)
                mm.then_inc(r_s0, 1)
                merge_block(pe, FILL[c])
                pe.wait_ge(r_sr, c + 1)
                for h in range(RH):
                    q = h // 4
                    mm = pe.matmul(psum[6][quad(h), 256 + 64 * q:320 + 64 * q], TT2[quad(h), c, q, :], SR[quad(h), q, :],
                                   start=True, stop=True, tile_position=(32 * (h % 4), 32 * (h % 4)))
                mm.then_inc(r_sa, 1)
                if FILL2[c] is not None:
                    merge_block(pe, FILL2[c])
                pe.wait_ge(r_ss, c + 1)
                for j, (what, src) in enumerate(((0, SK), (1, None))):
                    for h in range(RH):
                        q = h // 4
                        rhs = SK[quad(h), q, :] if j == 0 else VV[quad(h), c % 2, q, :]
                        mm = pe.matmul(psum[5 + 2 * ((h % 4) // 2)][half(h), 256 + 64 * q:320 + 64 * q],
                                       BK[quad(h), c % 2, q, j, :], rhs, start=j == 0 and h < 4, stop=j == 1,
                                       tile_position=(32 * (h % 4), 64 * (h % 2)), skip_group_check=True)
                mm.then_inc(r_up, 1)
                if c:
                    if c > 1:
                        pe.wait_ge(r_yo, c - 1)
                    for h in range(RH):
                        o = psum[2][quad(h), 64 * (h // 4):64 * (h // 4) + 64]
                        pe.matmul(o, XR[half(h), 0, h // 2, t], RS[half(h), h // 2, :], start=h < 4, stop=False,
                                  tile_position=(64 * (h % 2), 32 * (h % 4)), skip_group_check=True)
                    for h in range(RH):
                        q, o = h // 4, psum[2][quad(h), 64 * (h // 4):64 * (h // 4) + 64]
                        pe.matmul(o, AM4[quad(h), c, q, 32:64], VV[quad(h), c % 2, q, :], start=False, stop=False,
                                  tile_position=(32 * (h % 4), 32 * (h % 4)), skip_group_check=True)
                        mm = pe.matmul(o, AM4[quad(h), c, q, 96:128], SK[quad(h), q, :], start=False, stop=True,
                                       tile_position=(32 * (h % 4), 32 * (h % 4)), skip_group_check=True)
                    mm.then_inc(r_yp, 1)
                if c + 1 < NC:
                    tokens(c + 1)
            pe.wait_ge(r_yn, 1)
            for g in range(2):
                for c in range(4 * g, 4 * g + 4):
                    for h in range(RH):
                        mm = pe.matmul(psum[4 + 2 * g + (h % 4) // 2][half(h), 128 * (c % 4) + 32 * (h // 4):128 * (c % 4) + 32 * (h // 4) + 32],
                                       YD[quad(h), 4 * c + h // 4, :], ident[quad(h), quad(h)], start=True, stop=True,
                                       tile_position=(32 * (h % 4), 64 * (h % 2)))
                mm.then_inc(r_yt, 1)
            pe.wait_ge(r_y, 1)
            pe.sem_inc(e_used, 2)
            for u in range(32, 48):
                merge_block(pe, u)
            pe.wait_ge(mg_done, 48)
            pe.sem_inc(e_used, 1)

            def turn_sum(p):
                pe.wait_ge(f_pn, p + 1)
                if p >= 2:
                    pe.wait_ge(f_tc, p - 1)
                for k in range(2):
                    for a in range(2):
                        mm = pe.transpose(psum[4 + p % 2][:, 256 * k + 128 * a:256 * k + 128 * a + 128],
                                          HN[:, a, 256 * p + 128 * k:256 * p + 128 * k + 128], ident)
                mm.then_inc(f_t, 1)

            def logits(p):
                pe.wait_ge(f_tc, p + 1)
                for a in range(2):
                    for k in range(2):
                        mm = pe.matmul(psum[6 + a][:, 0:36], HNT[:, p % 2, k, 128 * a:128 * (a + 1)], WR[:, 2 * p + k, :],
                                       start=p == 0 and k == 0, stop=p == 7 and k == 1)
                mm.then_inc(f_lg, 1)

            pe.wait_ge(f_ld, 80)
            for p in range(8):
                n = N_OUT + 2 * p
                weights1(pe, n)
                weights1(pe, n + 1)
                w = ring[:, n % 4:n % 4 + 2, :].rearrange("p s (k n) -> p (s k) n", k=8)
                for a in range(2):
                    m = M_OUT + 2 * p + a
                    if m < M_OUT + 2:
                        pe.wait_ge(pev, m - 1)
                    else:
                        pe.wait_ge(h2s, m - 1 - M_OUT)
                    for k in range(KT):
                        mm = pe.matmul(psum[m % 2][:, 0:256], MG[:, k, 128 * a:128 * (a + 1)], w[:, k, :], start=k == 0, stop=k == KT - 1)
                    mm.then_inc(pdone, 1)
                if p >= 1:
                    turn_sum(p - 1)
                if p >= 2:
                    logits(p - 2)
            turn_sum(7)
            logits(6)
            logits(7)
            if STOP == "mix":
                return
            pe_moe(pe)

        def weights1(eng, n):
            eng.wait_ge(wld[n % 4], 16 * (n // 4 + 1) + (16 if n % 4 == N_LORA % 4 else 0))

        def merge_block(pe, u):
            turn, blk = divmod(u, 16)
            b = BRANCHES[turn]
            pair, j = divmod(blk, 2)
            n = N_MERGE + 24 * turn + 3 * pair
            m = M_MERGE + 2 * u
            weights1(pe, n + 1 + j)
            wg = ring[:, (n + 1 + j) % 4, :].rearrange("p (k n) -> p k n", k=KT)
            dense(pe, m, [(128, SEQ, wg[:, k, :], HT[:, k, META:T], k == 0, k == KT - 1) for k in range(KT)])
            weights1(pe, n)
            wb = ring[:, n % 4, :].rearrange("p (k n) -> p k n", k=8)
            dense(pe, m + 1, [(128, SEQ, wb[:, k, 128 * j:128 * (j + 1)], Y[:, b, k, :], k == 0, k == 7) for k in range(8)])

        def merge_evac(act, u):
            m = M_MERGE + 2 * u
            if u >= 2:
                act.wait_ge(mg_done, u - 1)
            evac(act, m, GB[:, u % 2, :], ACT.Sigmoid, cols=SEQ)
            evac(act, m + 1, BB[:, u % 2, :], cols=SEQ)

        def out_load(act, p):
            n = N_OUT + 2 * p
            act.wait_ge(pdone, uses_with(n - 3))
            for a in range(2):
                act.dma_start(ring[:, (n + a) % 4, :].rearrange("p (k n) -> p k n", k=8),
                              w_out.rearrange("(k p) n -> p k n", p=128)[:, 8 * a:8 * a + 8, 256 * p:256 * (p + 1)]
                              ).then_inc(wld[(n + a) % 4], 16)

        def act_rest(act):
            act.wait_ge(s_lr, 1)
            act.activation(LR[0:64, 0, PAD:TP], LR[0:64, 0, PAD:TP], ACT.Tanh)
            act.activation(LR[:, 1, PAD:TP], LR[:, 1, PAD:TP], ACT.Sigmoid)
            act.activation(LR[0:32, 2, PAD:TP], LR[0:32, 2, PAD:TP], ACT.Sigmoid)
            act.drain().then_inc(r_lr, 1)
            act.wait_ge(k_yd, 4)
            m = M_LORA
            for dst, bias in ((SG, "w0"), (RA, "a0")):
                for j in range(8):
                    evac(act, m, dst[:, j, PAD:TP], ACT.Sigmoid, bias=par_(bias, j))
                    m += 1
            for j in range(8):
                evac(act, m, RG[:, j, :], cols=SEQ)
                m += 1
            for u in range(U_SUMS):
                merge_evac(act, u)
            for i in range(8):
                act.wait_ge(r_kss, i + 1)
                act.activation(T3[:, i, :], psum[4 + i % 2][:, 0:TP], ACT.Sqrt, bias=con_("eps")).then_inc(r_krt, 1)
            for u in range(U_SUMS, U_EXPS):
                merge_evac(act, u)
            act.wait_ge(r_cs, 1)
            act.activation(T3, T3, ACT.Exp, scale=-CW)
            act.activation(T2, CS, ACT.Exp, scale=-CW)
            act.drain()
            act.activation(CS, CS, ACT.Exp, scale=CW)
            act.drain().then_inc(r_ex, 1)
            for u in range(U_EXPS, U_CHAIN):
                merge_evac(act, u)

            def keep(c):
                act.wait_ge(r_tok, c + 1)
                if c == 0:
                    act.wait_ge(q_uw, 16)
                if c >= 2:
                    act.wait_ge(r_up, c - 1)
                    act.wait_ge(r_yp, c - 2) if c > 2 else None
                act.activation(BK[:, c % 2], psum[4][:, :].rearrange("p (q a n) -> p q a n", q=4, a=2), ACT.Copy)
                act.activation(VV[:, c % 2], psum[5][:, 0:256].rearrange("p (q n) -> p q n", q=4), ACT.Copy)
                act.drain().then_inc(r_tk, 1)

            keep(0)
            for c in range(NC):
                act.wait_ge(r_s0, c + 1)
                if c == 0:
                    act.wait_ge(q_inv, 1)
                act.activation(SR.rearrange("p a b -> p (a b)"), psum[6][:, 0:256], ACT.Copy).then_inc(r_sr, 1)
                merge_evac(act, FILL[c])
                act.wait_ge(r_sa, c + 1)
                if c > 1:
                    act.wait_ge(r_yp, c - 1)
                act.activation(SK.rearrange("p a b -> p (a b)"), psum[6][:, 256:512], ACT.Copy).then_inc(r_ss, 1)
                if FILL2[c] is not None:
                    merge_evac(act, FILL2[c])
                if c:
                    act.wait_ge(r_yp, c)
                    act.activation(YO[:, c - 1].rearrange("p a b -> p (a b)"), psum[2][:, 0:256], ACT.Copy).then_inc(r_yo, 1)
                if c + 1 < NC:
                    keep(c + 1)
            act.wait_ge(r_v1, 1)
            act.activation(stats[:, 96:128], stats[:, 96:128], ACT.Sqrt, scale=1.0 / 64, bias=con_("rln_eps")).then_inc(r_v2, 1)
            for u in range(32, 48):
                merge_evac(act, u)
                if u == 32:
                    act.wait_ge(r_y, 1)
                    act.dma_start(FN, norm_ffn.broadcast_to([128, D])).then_inc(f_ld, 16)
                    act.dma_start(WR[:, :, 0:NG], w_rg.rearrange("(k p) n -> p k n", p=128)).then_inc(f_ld, 16)
                    act.dma_start(WR[:, :, NG:36], w_re.rearrange("(k p) n -> p k n", p=128)).then_inc(f_ld, 16)
                    act.dma_start(RB[:, 0:NG], b_rg.broadcast_to([128, NG])).then_inc(f_ld, 16)
                    act.dma_start(RB[:, NG:36], b_re.broadcast_to([128, NE])).then_inc(f_ld, 16)
            out_load(act, 0)
            act.dma_start(H2, x.rearrange("(a p) d -> p a d", a=2)).then_inc(xh, 16)
            out_load(act, 1)
            for p in range(8):
                act.wait_ge(h2s, 2 * p + 2)
                if p < 6:
                    out_load(act, p + 2)
                for a in range(2):
                    act.activation(psum[2 + a][:, 0:256], H2[:, a, 256 * p:256 * (p + 1)], ACT.Square,
                                   accum_out=stats[:, 144 + 8 * a + p:145 + 8 * a + p])
                act.drain().then_inc(f_sq, 1)
                act.wait_ge(f_t, p + 1)
                if p >= 2:
                    act.wait_ge(f_lg, p - 1)
                act.activation(HNT[:, p % 2], psum[4 + p % 2][:, :].rearrange("p (k t) -> p k t", k=2), ACT.Copy).then_inc(f_tc, 1)
            if STOP == "mix":
                return
            act_moe(act)

        def bc(name, n, j=0):
            at = PAR.at[name] + j
            return PARAM[:, at:at + 8].unsqueeze(2).broadcast_to([128, 8, n])

        def v_rest(v):
            XK, XRr, XV = XR[:, 1], XR[:, 0], XR[:, 2]
            v.wait_ge(pev, M_LORA)
            v.memset(SG[:, :, 0:PAD], 0.0)
            v.memset(RA[:, :, 0:PAD], 0.0)
            v.memset(XR24[:, :, 0:PAD], 0.0)
            v.tensor_tensor(XR24[:, :, PAD:TP], RAW[:, :, PAD - 1:TP - 1], RAW[:, :, PAD:TP], ALU.subtract)
            v.drain()
            with v.Fori(0, 24) as i:
                d = XR24[:, ds(i, 1), PAD:TP]
                v.scalar_tensor_tensor(d, d, PARAM[:, ds(i + PAR.at["mu"], 1)], RAW[:, ds(i, 1), PAD:TP], ALU.mult, ALU.add)
            v.drain()
            v.tensor_tensor(T1, XK, bc("k_k", TP), ALU.mult)
            v.drain()
            v.tensor_tensor(T2, T1, T1, ALU.mult).then_inc(r_ksq, 1)
            v.wait_ge(pev, M_MERGE)
            v.scalar_tensor_tensor(CS, RA, -1.0, bc("k_a", TP), ALU.add, ALU.mult)
            v.drain()
            v.scalar_tensor_tensor(XK, CS, 1.0, XK, ALU.add, ALU.mult)
            v.drain()
            v.tensor_tensor(BPR, XRr[:, :, 2 * PAD:TP], XK[:, :, 2 * PAD:TP], ALU.mult)
            v.drain()
            v.tensor_tensor(BPR, BPR, bc("r_k", SEQ), ALU.mult).then_inc(r_bin, 1)
            for i in range(8):
                v.wait_ge(r_krt, i + 1)
                v.reciprocal(T3[:, i, :], T3[:, i, :])
            v.drain()
            v.tensor_tensor(T1, T1, T3, ALU.mult)
            for i in range(8):
                v.wait_ge(r_bs, i + 1)
                v.tensor_tensor(BON[:, i, :], psum[6 + i % 2][:, 0:SEQ], XV[:, i, 2 * PAD:TP], ALU.mult).then_inc(r_bd, 1)
            v.drain()
            for i in range(8):
                v.tensor_tensor_scan(CS[:, i, :], con_("scan"), SG[:, i, :], 0.0, ALU.mult, ALU.add)
            v.drain()
            v.tensor_tensor(T3, CS, SG, ALU.subtract)
            v.drain().then_inc(r_cs, 1)
            v.wait_ge(r_ex, 1)
            v.scalar_tensor_tensor(SG, T1, -1.0, T3, ALU.mult, ALU.mult)
            v.tensor_tensor(XRr, XRr, T2, ALU.mult)
            v.tensor_copy(PC, T2[:, :, C - 1:TP:C])
            v.tensor_tensor(XK, XK, CS, ALU.mult)
            v.drain()
            v.tensor_tensor(T3, T1, RA, ALU.mult)
            v.drain()
            v.tensor_tensor(T3, T3, CS, ALU.mult)
            v.drain().then_inc(r_el, 1)
            unit(v, IU2[0:72], 2)
            for c in range(NC):
                v.wait_ge(r_a, c + 1)
                v.tensor_tensor(AM4[:, c], psum[4 + c % 2][:, :].rearrange("p (q n) -> p q n", q=4),
                                con_("m4").unsqueeze(1).broadcast_to([128, 4, 128]), ALU.mult).then_inc(r_am, 1)
            v.wait_ge(q_al, 16)
            invert(v, IA2[0:72].rearrange("p (z t s) -> p z t s", z=2, t=C), IU2[0:72].rearrange("p (z s t) -> p z s t", z=2, s=C),
                   IT2[0:72], 2)
            v.drain().then_inc(q_inv, 1)
            for c in range(NC):
                v.wait_ge(r_up, c + 1)
                if c:
                    v.wait_ge(r_yp, c)
                S4 = RS.rearrange("p (q j) n -> p q j n", j=2)
                for j in range(2):
                    inc = psum[5 + 2 * j][:, 256:512].rearrange("p (q n) -> p q n", q=4)
                    if c:
                        v.tensor_tensor(S4[:, :, j], S4[:, :, j], inc, ALU.add)
                    else:
                        v.tensor_copy(S4[:, :, j], inc)
                v.drain()
                v.tensor_tensor(RS, RS, PC[:, :, c:c + 1].broadcast_to([128, 8, 64]), ALU.mult)
                v.drain().then_inc(r_st, 1)
            v.wait_ge(r_yo, NC - 1)
            Y3 = YO.rearrange("p c q n -> p (c q) n")
            st = stats[:, 64:96]
            v.tensor_reduce(st.unsqueeze(2), Y3, AX.X, ALU.add)
            v.drain()
            v.tensor_scalar(st, st, 1.0 / 64, None, ALU.mult)
            v.drain()
            v.tensor_tensor(Y3, Y3, st.unsqueeze(2).broadcast_to([128, 32, 64]), ALU.subtract)
            v.drain()
            v.tensor_tensor(YD, Y3, Y3, ALU.mult)
            v.drain()
            v.tensor_reduce(stats[:, 96:128].unsqueeze(2), YD, AX.X, ALU.add)
            v.drain().then_inc(r_v1, 1)
            v.wait_ge(r_v2, 1)
            v.reciprocal(stats[:, 96:128], stats[:, 96:128])
            v.drain()
            v.tensor_tensor(YD, Y3, stats[:, 96:128].unsqueeze(2).broadcast_to([128, 32, 64]), ALU.mult)
            v.drain().then_inc(r_yn, 1)
            for g in range(2):
                v.wait_ge(r_yt, g + 1)
                for j in range(2):
                    src = psum[4 + 2 * g + j][:, :].rearrange("p (c q t) -> p q c t", c=4, q=4)
                    dst = YT[:, j:8:2, 128 * g:128 * g + 128].rearrange("p q (c t) -> p q c t", c=4)
                    w = PARAM[:, PAR.at["ln_w"] + j:PAR.at["ln_w"] + 8:2].unsqueeze(2).unsqueeze(3).broadcast_to([128, 4, 4, C])
                    v.tensor_tensor(dst, src, w, ALU.mult)
            v.drain()
            v.tensor_tensor(YT, YT, bc("ln_b", SEQ), ALU.add)
            v.drain()
            v.tensor_tensor(YT, YT, BON, ALU.add)
            v.drain()
            v.tensor_tensor(BON, YT, RG, ALU.mult)
            v.drain().then_inc(r_y, 1)
            v.wait_ge(xh, 16)
            for p in range(8):
                for a in range(2):
                    m = M_OUT + 2 * p + a
                    v.wait_ge(pdone, m + 1)
                    h = H2[:, a, 256 * p:256 * (p + 1)]
                    v.tensor_tensor(h, h, psum[m % 2][:, 0:256], ALU.add).then_inc(h2s, 1)
            if STOP == "mix":
                return
            v_moe(v)

        def pool_rest(pool):
            pool.wait_ge(k_yd, 4)
            for turn in range(3):
                for j in range(16):
                    u = 16 * turn + j
                    if u == U_PREP:
                        pool.wait_ge(r_am, NC)
                        for h in range(4):
                            pool.dma_start(rwkv_a.rearrange("(h c) (t s) -> h t c s", h=4, t=C)[h],
                                           AM4.rearrange("p c q s -> p (c q) s")[32 * h:32 * h + 32, :, 0:C]).then_inc(q_aw, 16)
                        pool.wait_ge(q_aw, 64)
                        pool.dma_start(IA2[0:72], rwkv_a.rearrange("(p z) a -> p (z a)", z=2)).then_inc(q_al, 16)
                    if u == U_CHAIN:
                        pool.wait_ge(q_inv, 1)
                        pool.dma_start(rwkv_u.rearrange("(p z) a -> p (z a)", z=2), IU2[0:72]).then_inc(q_uw, 16)
                        pool.wait_ge(q_uw, 16)
                        for h in range(4):
                            pool.dma_start(TT2.rearrange("p c q s -> p (c q) s")[32 * h:32 * h + 32],
                                           rwkv_u.rearrange("(h c) (s t) -> h s c t", h=4, s=C)[h]).then_inc(q_ul, 16)
                    pool.wait_ge(pev, M_MERGE + 2 * u + 2)
                    dst = MG[:, j, :]
                    if turn == 0:
                        pool.tensor_tensor(dst, GB[:, u % 2, :], BB[:, u % 2, :], ALU.mult).then_inc(mg_done, 1)
                    else:
                        pool.tensor_tensor(BB[:, u % 2, :], GB[:, u % 2, :], BB[:, u % 2, :], ALU.mult)
                        pool.drain()
                        pool.tensor_tensor(dst, dst, BB[:, u % 2, :], ALU.add).then_inc(mg_done, 1)
            pool.wait_ge(f_ld, 80)
            for p in range(8):
                pool.wait_ge(h2s, 2 * p + 2)
                c = slice(256 * p, 256 * (p + 1))
                pool.tensor_tensor(HN[:, :, c], H2[:, :, c], FN[:, c].unsqueeze(1).broadcast_to([128, 2, 256]), ALU.mult).then_inc(f_pn, 1)

        HN = view(A_RING + 8192 + 4096, 2, D)
        HNT = view(A_RING + 8192 + 8192, 2, 2, SEQ)
        FN = view(W0, D)
        WR = view(W0 + D, KT, 36)
        RB = stats[:, 200:236]
        A_RS = A_RING + 6912
        LG = view(A_RS + 36, 2, 36)
        G8 = view(A_RS + 108, 2, 8)
        M8 = view(A_RS + 124, 2, 8)
        I8 = view(A_RS + 140, 2, 8).bitcast(U32)
        F8 = view(A_RS + 156, 2, 4)
        GH_ = view(A_RS + 164, 2, 4)
        E8 = view(A_RS + 172, 2, 8)
        O01 = view(A_RS + 188, 2, 2, NE)
        OS = view(A_RS + 316, 2, NE)
        RKM = view(A_RS + 380, 2, NE + 2)
        WTE = view(A_RS + 448, 2, NE)
        W1 = view(A_RS + 512, 2, NE)
        WT = view(A_RS + 652, 2, 2)
        RC = view(A_RS + 656, 8)
        RI = view(A_RS + 664, 4).bitcast(I32)
        SEL = view(A_RS + 680, 2, 2, CAP)
        SELW = view(A_RS + 936, 2, 128)
        GE = view(A_RS + 1192, 2, NG, EPG)
        assert A_RS + 1192 + 64 <= A_RING + 8192
        SELT = view(A_RING + 8192 + 8192, 2, 2 * 128)
        XG = view(A_RING + 5888, 1024)
        YS = view(A_RING + 4864, 1024)
        XGT = view(A_RING, 2, 8, 128)
        SL = view(A_RING + 2048, 256)
        AA = view(A_RING + 2304, 256)
        ATT = view(A_RING + 2560, 2, 128)
        A_E = 53200 - 4 * 8192
        ering = view(A_E, 4, 8192)
        NF = view(A_RING + 2816, D)
        OUT = view(A_E + 8192, 2, D)
        OJ = view(A_E + 8192 + 4096, 2, D)
        assert W0 + D + KT * 36 <= A_E + 8192

        eld = [sem(f"expert_weights_loaded{i}") for i in range(4)]
        e_used = sem("expert_slots_free")
        f_sq, f_rt, f_hn, f_ld = sem("ffn_squares"), sem("ffn_roots"), sem("ffn_normed"), sem("router_loaded")
        f_pn, f_sr, f_rc = sem("sum_times_norm"), sem("squares_summed"), sem("ffn_reciprocals")
        f_t, f_tc, f_lg = sem("ffn_turned"), sem("ffn_turned_kept"), sem("logits")
        f_l, f_ex, f_oh, f_rk, f_rd = sem("gate_inputs"), sem("gate_exps"), sem("chosen"), sem("ranks"), sem("rounds_known")
        x_sel, x_gp, x_gk = sem("rows_selected"), sem("rows_gathered"), sem("rows_kept")
        x_t, x_gt, x_sl, x_a, x_tt, x_at = (sem("rows_turned"), sem("rows_turned_kept"), sem("silu_done"), sem("hidden_done"),
                                            sem("hidden_turned"), sem("hidden_turned_kept"))
        x_w, x_st = sem("weighted_rows"), sem("weighted_rows_turned_kept")
        x_y1, x_y2, x_c, x_cd = (sem("result_kept_low"), sem("result_kept_high"), sem("results_by_token"),
                                 sem("results_added_by_token"))
        z_nf, z_sm = sem("final_norm_loaded"), sem("results_added")
        z_rt, z_out, z_st = sem("final_roots"), sem("final_normed"), sem("stored")

        AHEAD = 2

        def rounds(eng):
            eng.wait_ge(f_rd, 1)
            return eng.value_load(RI[0:1, 0:1], min_val=1, max_val=SEQ // CAP)

        def sp_moe(sp):
            def one_round(r):
                with sp.Fori(0, NE // 4) as i:
                    for j in range(4):
                        for part in range(3):
                            c = 3 * j + part
                            sp.wait_ge(e_used, (r * (NE // 4) + i) * 12 + (c + 1))
                            slot = (c + 1) % 4
                            if part < 2:
                                dst = ering[:, slot, :].rearrange("p (a j n) -> p a j n", a=2, j=8)
                                for a, w in enumerate((e_gate, e_up)):
                                    src = w[ds(i * 4 + j, 1), 1024 * part:1024 * (part + 1), :].rearrange("e (p j) n -> p (e j) n", j=8)
                                    sp.dma_start(dst[:, a], src).then_inc(eld[slot], 16)
                            else:
                                dst = ering[:, slot, :].rearrange("p (k n) -> p k n", k=4)
                                src = e_down[ds(i * 4 + j, 1), :, :].rearrange("e (k p) n -> p (e k) n", p=128)
                                for a in range(2):
                                    sp.dma_start(dst[:, 2 * a:2 * a + 2], src[:, 2 * a:2 * a + 2]).then_inc(eld[slot], 16)

            one_round(0)
            n_rounds = rounds(sp)
            with sp.If(n_rounds > 1), sp.Fori(1, n_rounds) as r:
                one_round(r)
            for a in range(2):
                sp.wait_ge(z_out, a + 1)
                sp.dma_start(out[128 * a:128 * (a + 1)], OUT[:, a]).then_inc(z_st, 16)
            sp.wait_ge(z_st, 32)

        def pe_moe(pe):
            pe.drain()
            pe.sem_inc(e_used, 1)
            pe.wait_ge(f_oh, 1)
            pe.matmul(psum[5][:, 0:32], con_("lt"), OS[:, 0], start=True, stop=True)
            pe.matmul(psum[5][:, 32:64], con_("ones"), OS[:, 0], start=True, stop=False)
            pe.matmul(psum[5][:, 32:64], con_("lt"), OS[:, 1], start=False, stop=True)
            pe.matmul(psum[5][:, 64:96], con_("ones"), OS[:, 0], start=True, stop=False)
            pe.matmul(psum[5][:, 64:96], con_("ones"), OS[:, 1], start=False, stop=True).then_inc(f_rk, 1)
            pe.sem_inc(x_tt, 1)
            pe.wait_ge(f_hn, 1)

            def gather(r, n, buf):
                at = r * (NE + 1) + n
                pe.wait_ge(x_sel, r * (NE + AHEAD) + n + 1)
                if not (isinstance(r, int) and isinstance(n, int)):
                    pe.wait_ge(x_gt, at)
                for q in range(2):
                    for a in range(2):
                        for m in range(2):
                            mm = pe.matmul(psum[q][64 * m:64 * m + 64, :], SEL[:, buf, a, :], HN[:, a, 1024 * m + 512 * q:1024 * m + 512 * (q + 1)],
                                           start=a == 0, stop=a == 1, tile_position=(0, 64 * m), skip_group_check=True)
                mm.then_inc(x_gp, 1)

            def turn(r, n):
                pe.wait_ge(x_gk, r * (NE + 1) + n + 1)
                for j in range(8):
                    mm = pe.transpose(psum[j // 4][:, 128 * (j % 4):128 * (j % 4) + 128], XG[:, j:1024:8], ident)
                mm.then_inc(x_t, 1)

            def combine(at, k, buf):
                a, q = divmod(k, 2)
                if k == 0:
                    pe.wait_ge(x_y1, at + 1)
                    pe.wait_ge(x_y2, at + 1)
                    pe.wait_ge(x_st, at + 1)
                pe.wait_ge(x_cd, at * 4 + (k + 1))
                for m in range(2):
                    mm = pe.matmul(psum[3 + 3 * m][:, :], SELT[64 * m:64 * m + 64, buf, 128 * a:128 * a + 128],
                                   YS[64 * m:64 * m + 64, 512 * q:512 * (q + 1)], start=True, stop=True, tile_position=(64 * m, 0))
                mm.then_inc(x_c, 1)

            def one_round(r):
                gather(r, 0, 0)
                turn(r, 0)
                with pe.Fori(0, NE // 4) as i:
                    for j in range(4):
                        b = j % 2
                        at = r * NE + i * 4 + j
                        gather(r, i * 4 + (j + 1), 1 - b)
                        combine(at, 0, 1 - b)
                        pe.wait_ge(x_gt, r * (NE + 1) + i * 4 + (j + 1))
                        pe.wait_ge(x_a, at + 1)
                        for h in range(2):
                            c = 3 * j + h
                            pe.wait_ge(eld[(c + 1) % 4], ((r * (NE // 4) + i) * 3 + (c // 4 + 1)) * 32)
                            w = ering[:, (c + 1) % 4, :].rearrange("p (a j n) -> p a j n", a=2, j=8)
                            for k in range(8):
                                for n in range(2):
                                    mm = pe.matmul(psum[2][64 * n:64 * n + 64, :], XGT[:, b, k, 64 * h:64 * h + 64],
                                                   w[:, :, k, 256 * n:256 * n + 256], start=h == 0 and k == 0, stop=h == 1 and k == 7,
                                                   tile_position=(0, 64 * n), skip_group_check=True)
                            mm.then_inc(e_used, 1)
                            if h == 0:
                                turn(r, i * 4 + (j + 1))
                            combine(at, 1 + h, 1 - b)
                        pe.wait_ge(x_a, at + 2)
                        pe.wait_ge(x_w, at + 1)
                        pe.wait_ge(x_at, at + 1)
                        pe.wait_ge(x_st, at + 1)
                        for k in range(2):
                            pe.transpose(psum[7][:, 128 * k:128 * k + 128], AA[:, 128 * k:128 * k + 128], ident)
                        for a in range(2):
                            mm = pe.transpose(psum[7][:, 256 + 128 * a:384 + 128 * a], SELW[:, a, :], ident)
                        mm.then_inc(x_tt, 1)
                        combine(at, 3, 1 - b)
                        pe.wait_ge(x_at, at + 2)
                        c = 3 * j + 2
                        pe.wait_ge(eld[(c + 1) % 4], ((r * (NE // 4) + i) * 3 + (c // 4 + 1)) * 32)
                        w = ering[:, (c + 1) % 4, :].rearrange("p (k n) -> p k n", k=4)
                        for q in range(2):
                            for k in range(4):
                                for m in range(2):
                                    mm = pe.matmul(psum[4 + q][64 * m:64 * m + 64, :], ATT[:, k % 2, 64 * (k // 2):64 * (k // 2) + 64],
                                                   w[:, k, 1024 * m + 512 * q:1024 * m + 512 * (q + 1)], start=k == 0, stop=k == 3,
                                                   tile_position=(0, 64 * m), skip_group_check=True)
                        mm.then_inc(e_used, 1)

            one_round(0)
            n_rounds = rounds(pe)
            with pe.If(n_rounds > 1), pe.Fori(1, n_rounds) as r:
                one_round(r)
            for k in range(4):
                combine(n_rounds * NE, k, 1)

        def act_moe(act):
            act.wait_ge(f_sr, 1)
            act.activation(stats[:, 132:134], stats[:, 130:132], ACT.Sqrt, scale=1.0 / D, bias=con_("eps")).then_inc(f_rt, 1)
            act.wait_ge(f_rc, 1)
            act.wait_ge(f_t, 8)
            for a in range(2):
                act.activation(HN[:, a, :], HN[:, a, :], ACT.Copy, scale=stats[:, 132 + a:133 + a])
            act.drain().then_inc(f_hn, 1)
            act.dma_start(NF, norm_final.broadcast_to([128, D])).then_inc(z_nf, 16)
            act.wait_ge(f_l, 1)
            for a in range(2):
                act.activation(GH_[:, a, :], LG[:, a, 0:NG], ACT.Exp, bias=F8[:, a, 1:2], accum_out=F8[:, a, 2:3])
                act.activation(F8[:, a, 3:4], F8[:, a, 3:4], ACT.Exp)
            act.drain().then_inc(f_ex, 1)
            for s in (x_y2, x_at, x_st):
                act.sem_inc(s, 1)

            def keep(r, n, buf):
                at = r * (NE + 1) + n
                act.wait_ge(x_gp, at + 1)
                if not (isinstance(r, int) and isinstance(n, int)):
                    act.wait_ge(x_t, at)
                for a in range(2):
                    act.activation(XG[:, 512 * a:512 * (a + 1)], psum[a][:, :], ACT.Copy)
                act.drain().then_inc(x_gk, 1)
                act.wait_ge(x_t, at + 1)
                act.wait_ge(e_used, (r * NE + n) * 3 + 1)
                for a in range(2):
                    act.activation(XGT[:, buf, 4 * a:4 * a + 4, :].rearrange("p a b -> p (a b)"), psum[a][:, :], ACT.Copy)
                act.drain().then_inc(x_gt, 1)

            def one_round(r):
                keep(r, 0, 0)
                with act.Fori(0, NE // 4) as i:
                    for j in range(4):
                        b = j % 2
                        at = r * NE + i * 4 + j
                        keep(r, i * 4 + (j + 1), 1 - b)
                        act.wait_ge(e_used, at * 3 + 6)
                        act.wait_ge(x_a, at + 1)
                        act.activation(SL, psum[2][:, 0:256], ACT.Silu).then_inc(x_sl, 1)
                        act.wait_ge(x_tt, at + 2)
                        act.activation(ATT.rearrange("p a b -> p (a b)"), psum[7][:, 0:256], ACT.Copy).then_inc(x_at, 1)
                        act.activation(SELT[:, b, :], psum[7][:, 256:512], ACT.Copy).then_inc(x_st, 1)
                        act.wait_ge(e_used, at * 3 + 7)
                        act.activation(YS[:, 512:1024], psum[5][:, :], ACT.Copy).then_inc(x_y2, 1)

            one_round(0)
            n_rounds = rounds(act)
            with act.If(n_rounds > 1), act.Fori(1, n_rounds) as r:
                one_round(r)
            for a in range(2):
                act.wait_ge(z_sm, a + 1)
                act.activation(OJ[:, a, :], H2[:, a, :], ACT.Square, accum_out=stats[:, 140 + a:141 + a])
                act.drain()
                act.activation(stats[:, 142 + a:143 + a], stats[:, 140 + a:141 + a], ACT.Sqrt, scale=1.0 / D, bias=con_("eps")).then_inc(z_rt, 1)

        def v_moe(v):
            v.memset(G8, -3e38)
            v.memset(RKM, -1e4)
            v.wait_ge(f_sq, 8)
            v.tensor_reduce(stats[:, 130:132].unsqueeze(2), stats[:, 144:160].rearrange("p (a n) -> p a n", a=2), AX.X, ALU.add)
            v.drain().then_inc(f_sr, 1)
            v.wait_ge(f_rt, 1)
            v.reciprocal(stats[:, 132:134], stats[:, 132:134])
            v.drain().then_inc(f_rc, 1)
            v.wait_ge(f_lg, 8)
            for a in range(2):
                v.scalar_tensor_tensor(LG[:, a, :], psum[6 + a][:, 0:36], stats[:, 132 + a:133 + a], RB, ALU.mult, ALU.add)
            v.drain()
            v.tensor_copy(G8[:, :, 0:NG], LG[:, :, 0:NG])
            v.drain()
            for a in range(2):
                v.max(M8[:, a, :], G8[:, a, :])
            v.drain()
            for a in range(2):
                v.max_index(I8[:, a, :], M8[:, a, :], G8[:, a, :])
            v.tensor_scalar(F8[:, :, 1:2], M8[:, :, 0:1], -1.0, None, ALU.mult)
            v.drain()
            v.tensor_copy(F8[:, :, 0:1], I8[:, :, 0:1])
            v.drain()
            v.tensor_tensor(GH_, con_("iota8")[:, 0:NG].unsqueeze(1).broadcast_to([128, 2, NG]),
                            F8[:, :, 0:1].broadcast_to([128, 2, NG]), ALU.is_equal)
            v.drain()
            v.tensor_tensor(GE, LG[:, :, NG:36].rearrange("p a (g e) -> p a g e", g=NG),
                            GH_.unsqueeze(3).broadcast_to([128, 2, NG, EPG]), ALU.mult)
            v.drain()
            v.tensor_reduce(E8.unsqueeze(3), GE.rearrange("p a g e -> p a e g"), AX.X, ALU.add)
            v.drain()
            for a in range(2):
                v.max(M8[:, a, :], E8[:, a, :])
            v.drain()
            for a in range(2):
                v.max_index(I8[:, a, :], M8[:, a, :], E8[:, a, :])
            v.tensor_tensor(F8[:, :, 3:4], M8[:, :, 1:2], M8[:, :, 0:1], ALU.subtract)
            v.tensor_scalar(F8[:, :, 0:1], F8[:, :, 0:1], float(EPG), None, ALU.mult)
            v.drain()
            v.tensor_copy(G8[:, :, 0:2], I8[:, :, 0:2])
            v.drain()
            v.tensor_tensor(G8[:, :, 0:2], G8[:, :, 0:2], F8[:, :, 0:1].broadcast_to([128, 2, 2]), ALU.add)
            v.drain()
            v.tensor_tensor(O01, con_("iota32").unsqueeze(1).unsqueeze(1).broadcast_to([128, 2, 2, NE]),
                            G8[:, :, 0:2].unsqueeze(3).broadcast_to([128, 2, 2, NE]), ALU.is_equal)
            v.drain()
            v.tensor_tensor(OS, O01[:, :, 0, :], O01[:, :, 1, :], ALU.add)
            v.drain().then_inc(f_oh, 1)
            v.nop().then_inc(f_l, 1)
            v.wait_ge(f_rk, 1)
            v.scalar_tensor_tensor(RKM[:, :, 0:NE], OS, 1e4, psum[5][:, 0:64].rearrange("p (a n) -> p a n", a=2), ALU.mult, ALU.add)
            v.drain()
            v.tensor_scalar(RKM[:, :, 0:NE], RKM[:, :, 0:NE], -1e4, None, ALU.add)
            v.drain()

            def after_routing():
                v.wait_ge(f_ex, 1)
                v.tensor_scalar(F8[:, :, 0:1], F8[:, :, 3:4], 1.0, None, ALU.add)
                v.drain()
                v.tensor_tensor(F8[:, :, 0:1], F8[:, :, 0:1], F8[:, :, 2:3], ALU.mult)
                v.drain()
                v.reciprocal(WT[:, :, 0:1], F8[:, :, 0:1])
                v.drain()
                v.tensor_tensor(WT[:, :, 1:2], WT[:, :, 0:1], F8[:, :, 3:4], ALU.mult)
                v.drain()
                v.tensor_tensor(WTE, O01[:, :, 0, :], WT[:, :, 0:1].broadcast_to([128, 2, NE]), ALU.mult)
                v.tensor_tensor(W1, O01[:, :, 1, :], WT[:, :, 1:2].broadcast_to([128, 2, NE]), ALU.mult)
                v.drain()
                v.tensor_tensor(WTE, WTE, W1, ALU.add)
                v.tensor_reduce(RC[:, 0:1], psum[5][:, 64:96], AX.X, ALU.max)
                v.drain()
                v.tensor_scalar(RC[:, 1:2], RC[:, 0:1], float(CAP), 1.0, ALU.is_gt, ALU.add)
                for t in range(2, SEQ // CAP):
                    v.drain()
                    v.scalar_tensor_tensor(RC[:, 1:2], RC[:, 0:1], float(t * CAP), RC[:, 1:2], ALU.is_gt, ALU.add)
                v.drain()
                v.tensor_copy(RI[:, 0:1], RC[:, 1:2])
                v.drain().then_inc(f_rd, 1)

            v.memset(YS, 0.0)
            v.memset(SELT, 0.0)
            v.drain()
            for s in (x_a, x_y1, x_cd):
                v.sem_inc(s, 1)

            def select(r, n, buf):
                if not isinstance(n, int):
                    v.wait_ge(x_gp, r * (NE + 1) + (n - 1))
                elif not isinstance(r, int):
                    v.wait_ge(x_gp, r * (NE + 1))
                for a in range(2):
                    rank = RKM[:, a, n:n + 1] if isinstance(n, int) else RKM[:, a, ds(n, 1)]
                    v.tensor_scalar(SEL[:, buf, a, :], con_("slot")[:, 0:CAP], rank, None, ALU.is_equal)
                v.drain().then_inc(x_sel, 1)

            def add(at, k):
                a, q = divmod(k, 2)
                v.wait_ge(x_c, at * 4 + (k + 1))
                for m in range(2):
                    h = H2[:, a, 1024 * m + 512 * q:1024 * m + 512 * (q + 1)]
                    mm = v.tensor_tensor(h, h, psum[3 + 3 * m][:, :], ALU.add)
                v.drain().then_inc(x_cd, 1)

            def one_round(r):
                select(r, 0, 0)
                select(r, 1, 1)
                if isinstance(r, int):
                    after_routing()
                with v.Fori(0, NE // 4) as i:
                    for j in range(4):
                        b = j % 2
                        at = r * NE + i * 4 + j
                        select(r, i * 4 + (j + AHEAD), b)
                        v.wait_ge(x_tt, at + 1)
                        for a in range(2):
                            v.tensor_scalar(SELW[:, a, :], con_("slot"), RKM[:, a, ds(i * 4 + j, 1)], WTE[:, a, ds(i * 4 + j, 1)],
                                            ALU.is_equal, ALU.mult)
                        v.drain().then_inc(x_w, 1)
                        add(at, 0)
                        add(at, 1)
                        v.wait_ge(x_sl, at + 1)
                        v.tensor_tensor(AA, SL, psum[2][:, 256:512], ALU.mult).then_inc(x_a, 1)
                        add(at, 2)
                        add(at, 3)
                        v.wait_ge(e_used, at * 3 + 7)
                        v.tensor_copy(YS[:, 0:512], psum[4][:, :]).then_inc(x_y1, 1)
                v.drain()
                v.tensor_scalar(RKM, RKM, -float(CAP), None, ALU.add)
                v.drain()

            one_round(0)
            n_rounds = rounds(v)
            with v.If(n_rounds > 1), v.Fori(1, n_rounds) as r:
                one_round(r)
            for k in range(4):
                add(n_rounds * NE, k)
                if k % 2:
                    v.nop().then_inc(z_sm, 1)
            v.wait_ge(z_nf, 16)
            for a in range(2):
                v.wait_ge(z_rt, a + 1)
                v.reciprocal(stats[:, 142 + a:143 + a], stats[:, 142 + a:143 + a])
                v.drain()
                v.scalar_tensor_tensor(OUT[:, a, :], H2[:, a, :], stats[:, 142 + a:143 + a], NF, ALU.mult, ALU.mult).then_inc(z_out, 1)

        block = ctx.enter_context(nc.Block())
        STOP = program.stop

        @block.sync
        def _(sp):
            sp.dma_start(CONST, con).then_inc(ld, 16)
            sp.dma_start(PARAM, par).then_inc(ld, 16)
            sp.dma_start(XM[0:META], meta).then_inc(ld, 16)
            sp.dma_start(XT, x.rearrange("(a p) d -> p a d", a=2)).then_inc(ld, 16)
            win = w_in.rearrange("(k p) n -> p k n", p=128)

            def load(n, src, dst=None, turn=0, need=None):
                if n >= 4:
                    sp.wait_ge(pdone, (uses_with(n - 4) if need is None else need) + 4 * turn)
                sp.dma_start(ring[:, n % 4, :].rearrange("p (k n) -> p k n", k=src.shape[1]) if dst is None else dst,
                             src).then_inc(wld[n % 4], 16)

            def win_block(n, at, width):
                load(n, win[:, :, at:at + width], ring[:, n % 4, 0:KT * width].rearrange("p (k n) -> p k n", k=KT))

            win_block(0, IN0_BA, 16)
            for j in range(6):
                win_block(1 + j, IN0_CQ + 128 * j, 128)
            for j in range(4):
                win_block(7 + j, IN0_CKV + 128 * j, 128)
            win_block(11, IN0_KPE, 64)
            win_block(12, IN0_LORA, 128)
            win_block(13, IN0_LORA + 128, 128)
            win_block(14, IN0_LORA + 256, 32)
            with sp.Fori(0, 3) as i:
                for j in range(8):
                    load(N_QKV + j, win[:, :, ds(i * BR + 128 * j, 128)], turn=2 * i)
            wq = w_q_up.rearrange("(k p) n -> p k n", p=128)
            for h in range(8):
                load(N_QUP + h, wq[:, :, 192 * h:192 * (h + 1)],
                     ring[:, (N_QUP + h) % 4, 0:6 * 192].rearrange("p (k n) -> p k n", k=6))
            wkv = w_kv_up.rearrange("(k p) n -> p k n", p=128)
            for j in range(4):
                load(N_KVUP + j, wkv[:, :, 512 * j:512 * (j + 1)])
            for j in range(8):
                load(N_Z + j, win[:, :, 3 * BR + 128 * j:3 * BR + 128 * (j + 1)])
            if STOP == "mla":
                return
            with sp.Fori(0, 3) as i:
                for j in range(8):
                    load(N_RKV + j, win[:, :, ds(i * BR + (IN0_RKV + 128 * j), 128)], turn=2 * i)
            if STOP == "mla":
                return
            if STOP == "gdn":
                return
            sp_rest(sp, load)

        def dense(pe, m, products, turn=0):
            if m >= 2:
                pe.wait_ge(pev, m - 1 + 4 * turn)
            for rows, cols, lhs, rhs, first, last in products:
                mm = pe.matmul(psum[m % 2][0:rows, 0:cols], lhs, rhs, start=first, stop=last)
            mm.then_inc(pdone, 1)
            return mm

        def weights(eng, n, turn=0):
            eng.wait_ge(wld[n % 4], 16 * (n // 4 + 1) + 16 * turn)

        def in_block(pe, n, m, width=128, lo=0, turn=0):
            weights(pe, n, turn)
            w = ring[:, n % 4, 0:KT * width].rearrange("p (k n) -> p k n", k=KT)
            dense(pe, m, [(width, T - lo, w[:, k, :], HT[:, k, lo:T], k == 0, k == KT - 1) for k in range(KT)],
                  turn)

        @block.tensor
        def _(pe):
            pe.wait_ge(ld, 64)
            pe.wait_ge(xn_ready, 3)
            for k in range(KT):
                b = psum[4 + k % 4]
                if k >= 4:
                    pe.wait_ge(ht_ready, k - 3)
                pe.transpose(b[:, 0:META], XM[0:META, 128 * k:128 * (k + 1)], ident[0:META, 0:META])
                for a in range(2):
                    mm = pe.transpose(b[:, META + 128 * a:META + 128 * (a + 1)], XT[:, a, 128 * k:128 * (k + 1)], ident)
                mm.then_inc(ht_t, 1)
            pe.wait_ge(ht_ready, KT)
            for n in range(15):
                in_block(pe, n, n, {0: 16, 11: 64, 14: 32}.get(n, 128))
            with pe.Fori(0, 3) as i:
                for j in range(8):
                    in_block(pe, N_QKV + j, M_QKV + j, turn=2 * i)
            for i in range(10):
                pe.wait_ge(s_csq, i + 1)
                b = psum[6 if i < 6 else 7]
                pe.matmul(b[:, 0:T], con_("ones"), SQ[:, i % 2, 0:T], start=i in (0, 6), stop=i in (5, 9)).then_inc(s_csqf, 1)
            pe.wait_ge(s_cn, 10)
            for h in range(8):
                n, m = N_QUP + h, M_QUP + 2 * h
                weights(pe, n)
                w = ring[:, n % 4, 0:6 * 192].rearrange("p (k n) -> p k n", k=6)
                dense(pe, m, [(128, SEQ, w[:, k, 0:128], CQKV[:, k, META:T], k == 0, k == 5) for k in range(6)])
                dense(pe, m + 1, [(64, SEQ, w[:, k, 128:192], CQKV[:, k, META:T], k == 0, k == 5)
                                  for k in range(6)])
            for j in range(4):
                n, m = N_KVUP + j, M_KVUP + 5 * j
                weights(pe, n)
                w = ring[:, n % 4, :].rearrange("p (k h n) -> p k h n", k=4, h=2)
                for a in range(2):
                    dense(pe, m + a, [(128, T, w[:, k, a, 0:128], CQKV[:, 6 + k, :], k == 0, k == 3) for k in range(4)])
                for a, (t0, t1) in enumerate(((0, META), (META, META + 128), (META + 128, T))):
                    dense(pe, m + 2 + a, [(t1 - t0, 256, CQKV[:, 6 + k, t0:t1], w[:, k, :, 128:256],
                                                  k == 0, k == 3) for k in range(4)])
            for i in range(5):
                pe.wait_ge(pev, M_QUP + 4 * i + 4 if i < 4 else M_SMALL + 12)
                if i >= 2:
                    pe.wait_ge(s_rotd, i - 1)
                rhs = QPE[0:64, 2 * i:2 * i + 2, :] if i < 4 else KPE[0:64]
                pe.matmul(psum[4 + i % 2][0:64, 0:512 if i < 4 else T], con_("rot", 64), rhs,
                          start=True, stop=True).then_inc(s_rot, 1)
            pe.wait_ge(s_rotd, 5)
            pe.wait_ge(pev, M_Z)
            for i in range(17):
                if i < 16:
                    h, a = i // 2, i % 2
                    nk = META + 128 * (a + 1)
                    if i >= 2:
                        pe.wait_ge(a_sm, i - 1)
                    b = psum[4 + i % 2]
                    pe.matmul(b[:, 0:nk], QN[:, h, 128 * a:128 * (a + 1)], KN[:, h, 0:nk], start=True, stop=False)
                    pe.matmul(b[:, 0:nk], QPE[0:64, h, 128 * a:128 * (a + 1)], KPE[0:64, 0:nk],
                              start=False, stop=True).then_inc(a_sc, 1)
                if i % 2 and i < 16:
                    in_block(pe, N_Z + i // 2, M_Z + i // 2, lo=META)
                if i >= 1:
                    i_ = i - 1
                    h, a = i_ // 2, i_ % 2
                    pe.wait_ge(a_pn, i_ + 1)
                    if i_ >= 1:
                        pe.wait_ge(a_pc, i_)
                    for t in range(a + 1):
                        pe.transpose(psum[6][:, 128 * t:128 * (t + 1)], PX[:, i_ % 2, META + 128 * t:META + 128 * (t + 1)], ident)
                    pe.transpose(psum[6][0:META, 256:384], PX[:, i_ % 2, 0:META], ident).then_inc(a_pt, 1)
                    pe.wait_ge(a_pc, i_ + 1)
                    if i_ >= 1:
                        pe.wait_ge(a_oc, i_)
                    pe.matmul(psum[7][:, 0:128], VT[0:META, 0, 128 * h:128 * (h + 1)], PT[0:META, i_ % 2, 256:384],
                              start=True, stop=False)
                    for t in range(a + 1):
                        mm = pe.matmul(psum[7][:, 0:128], VT[:, 1 + t, 128 * h:128 * (h + 1)],
                                       PT[:, i_ % 2, 128 * t:128 * (t + 1)], start=False, stop=t == a)
                    mm.then_inc(a_o, 1)
            if STOP == "mla":
                return
            pe_gdn(pe)
            if STOP == "gdn":
                return
            pe_rest(pe)

        def evac(act, m, dst, func=ACT.Copy, rows=128, cols=T, turn=0, **kw):
            act.wait_ge(pdone, m + 1 + 4 * turn)
            act.activation(dst, psum[m % 2][0:rows, 0:cols], func, **kw).then_inc(pev, 1)

        @block.scalar
        def _(act):
            act.wait_ge(ld, 64)
            act.wait_ge(zeroed, 1)
            act.activation(XJ[:, :], XT[:, 0, :], ACT.Square, accum_out=stats[:, 0:1])
            act.drain()
            act.activation(XJ[:, :], XT[:, 1, :], ACT.Square, accum_out=stats[:, 1:2])
            act.drain()
            act.activation(XJ[0:META, :], XM[0:META, :], ACT.Square, accum_out=stats[0:META, 2:3]).then_inc(sq0, 1)
            act.drain()
            act.activation(stats[:, 4:7], stats[:, 0:3], ACT.Sqrt, scale=1.0 / D, bias=con_("eps")).then_inc(rt0, 1)
            for k in range(KT):
                act.wait_ge(ht_t, k + 1)
                act.activation(HT[:, k, :], psum[4 + k % 4][:, 0:T], ACT.Copy, scale=par_("norm_mix", k)).then_inc(ht_ready, 1)
            act.wait_ge(zeroed, 2)
            for n in range(15):
                dst = {0: BA[0:16, PAD:TP], 11: KPE[0:64], 12: LR[:, 0, PAD:TP], 13: LR[:, 1, PAD:TP],
                       14: LR[0:32, 2, PAD:TP]}.get(n, CQKV[:, max(n - 1, 0) % 10, :])
                evac(act, n, dst, rows={0: 16, 11: 64, 14: 32}.get(n, 128))
            act.drain()
            for i in range(10):
                if i >= 2:
                    act.wait_ge(s_csqf, i - 1)
                act.activation(SQ[:, i % 2, 0:T], CQKV[:, i, :], ACT.Square).then_inc(s_csq, 1)
                if i == 1:
                    with act.Fori(0, 3) as r:
                        for j in range(8):
                            evac(act, M_QKV + j, RAW[:, ds(r * 8 + j, 1), PAD:TP], turn=2 * r)
            act.wait_ge(s_csqf, 10)
            act.activation(RN[:, 0, 0:T], psum[6][:, 0:T], ACT.Sqrt, scale=1.0 / QL, bias=con_("eps")).then_inc(s_crt, 1)
            act.activation(RN[:, 1, 0:T], psum[7][:, 0:T], ACT.Sqrt, scale=1.0 / KVL, bias=con_("eps")).then_inc(s_crt, 1)
            for h in range(8):
                evac(act, M_QUP + 2 * h, QN[:, h, :], cols=SEQ)
                evac(act, M_QUP + 2 * h + 1, QPE[0:64, h, :], rows=64, cols=SEQ)
            act.wait_ge(s_conv, 24)
            for j in range(4):
                m = M_KVUP + 5 * j
                for a in range(2):
                    evac(act, m + a, KN[:, 2 * j + a, :])
                for a in range(3):
                    r = META if a == 0 else 128
                    evac(act, m + 2 + a, VT[0:r, a, 256 * j:256 * (j + 1)], rows=r, cols=256)
            for i in range(17):
                if i < 16:
                    nk = META + 128 * (i % 2 + 1)
                    act.wait_ge(a_sm, i + 1)
                    if i >= 2:
                        act.wait_ge(a_pt, i - 1)
                    act.activation(PX[:, i % 2, 0:nk], SS[:, i % 2, 0:nk], ACT.Exp, bias=stats[:, 10 + i % 2:11 + i % 2],
                                   accum_out=stats[:, 12 + i % 2:13 + i % 2]).then_inc(a_ex, 1)
                    if i % 2:
                        evac(act, M_Z + i // 2, ZR[:, i // 2, :], cols=SEQ)
                if i >= 1:
                    i_ = i - 1
                    h, a = i_ // 2, i_ % 2
                    act.wait_ge(a_pt, i_ + 1)
                    if i_ >= 2:
                        act.wait_ge(a_o, i_ - 1)
                    act.activation(PT[:, i_ % 2, 0:128 * (a + 1)], psum[6][:, 0:128 * (a + 1)], ACT.Copy)
                    act.activation(PT[0:META, i_ % 2, 256:384], psum[6][0:META, 256:384], ACT.Copy)
                    act.drain().then_inc(a_pc, 1)
                    act.wait_ge(a_o, i_ + 1)
                    act.activation(Y[:, 1, h, 128 * a:128 * (a + 1)], psum[7][:, 0:128], ACT.Copy).then_inc(a_oc, 1)
            if STOP == "mla":
                return
            act_gdn(act)
            if STOP == "gdn":
                return
            act_rest(act)

        @block.vector
        def _(v):
            v.memset(stats[:, :], 1.0).then_inc(zeroed, 1)
            v.wait_ge(rt0, 1)
            v.reciprocal(stats[:, 4:7], stats[:, 4:7])
            v.drain()
            for a in range(2):
                v.tensor_scalar(XT[:, a, :], XT[:, a, :], stats[:, 4 + a:5 + a], None, ALU.mult).then_inc(xn_ready, 1)
            v.tensor_scalar(XM[0:META], XM[0:META], stats[0:META, 6:7], None, ALU.mult).then_inc(xn_ready, 1)
            v.memset(LR[:, :, 0:PAD], 0.0)
            v.memset(BA[:, 0:PAD], 0.0)
            v.wait_ge(ht_ready, KT)
            v.memset(CV[:, :, 0:PAD], 0.0)
            v.memset(RAW[:, :, 0:PAD], 0.0)
            v.drain().then_inc(zeroed, 1)
            v.wait_ge(pev, 15)
            LD = view(A_MG, 3, TP)
            for j, mu in enumerate(("mu_wa", "mu_g1", "mu_g2")):
                r = 32 if j == 2 else 128
                v.tensor_tensor(LD[0:r, j, PAD:TP], LR[0:r, j, PAD - 1:TP - 1], LR[0:r, j, PAD:TP], ALU.subtract)
            v.drain()
            for j, mu in enumerate(("mu_wa", "mu_g1", "mu_g2")):
                r = 32 if j == 2 else 128
                v.scalar_tensor_tensor(LR[0:r, j, PAD:TP], LD[0:r, j, PAD:TP], par_(mu, 0, r), LR[0:r, j, PAD:TP], ALU.mult, ALU.add)
            v.drain().then_inc(s_lr, 1)
            v.wait_ge(s_crt, 2)
            for a in range(2):
                v.reciprocal(RN[:, a, 0:T], RN[:, a, 0:T])
            v.drain()
            for i in range(10):
                g = par_("qnorm", i) if i < 6 else par_("kvnorm", i - 6)
                v.scalar_tensor_tensor(CQKV[:, i, :], CQKV[:, i, :], g, RN[:, int(i >= 6), 0:T], ALU.mult, ALU.mult).then_inc(s_cn, 1)
            v.wait_ge(pev, M_QUP)
            with v.Fori(0, 24) as i:
                def tap(j):
                    return PARAM[:, ds(i + (PAR.at["conv"] + 24 * j), 1)]
                dst = CV[:, ds(i, 1), PAD:TP]
                v.tensor_scalar(dst, RAW[:, ds(i, 1), PAD - 3:TP - 3], tap(0), None, ALU.mult)
                for j in range(1, 4):
                    v.drain()
                    mm = v.scalar_tensor_tensor(dst, RAW[:, ds(i, 1), PAD - 3 + j:TP - 3 + j], tap(j), dst, ALU.mult, ALU.add)
                mm.then_inc(s_conv, 1)
            for i in range(5):
                v.wait_ge(s_rot, i + 1)
                if i < 4:
                    p = psum[4 + i % 2][0:64, 0:512].rearrange("p (h t) -> p h t", h=2)
                    q = QPE[0:64, 2 * i:2 * i + 2, :]
                    co = con_("cos", 64)[:, META:T].unsqueeze(1).broadcast_to([64, 2, SEQ])
                    si = con_("sin", 64)[:, META:T].unsqueeze(1).broadcast_to([64, 2, SEQ])
                    tmp = view(A_MT, 2, SEQ)[0:64]
                else:
                    p, q, co, si, tmp = psum[4][0:64, 0:T], KPE[0:64], con_("cos", 64), con_("sin", 64), view(A_MT, T)[0:64]
                v.tensor_tensor(tmp, p, si, ALU.mult)
                v.tensor_tensor(q, q, co, ALU.mult)
                v.drain()
                v.tensor_tensor(q, q, tmp, ALU.add).then_inc(s_rotd, 1)
                v.drain()
            for i in range(17):
                if i < 16:
                    a = i % 2
                    nk = META + 128 * (a + 1)
                    v.wait_ge(a_sc, i + 1)
                    v.scalar_tensor_tensor(SS[:, i % 2, 0:nk], psum[4 + i % 2][:, 0:nk], 192.0 ** -0.5,
                                           con_("causal")[:, T - nk:T], ALU.mult, ALU.add)
                    v.drain()
                    v.tensor_reduce(stats[:, 10 + i % 2:11 + i % 2], SS[:, i % 2, 0:nk], AX.X, ALU.max, negate=True).then_inc(a_sm, 1)
                if i >= 1:
                    i_ = i - 1
                    nk = META + 128 * (i_ % 2 + 1)
                    v.wait_ge(a_ex, i_ + 1)
                    v.reciprocal(stats[:, 14:15], stats[:, 12 + i_ % 2:13 + i_ % 2])
                    v.drain()
                    v.tensor_scalar(PX[:, i_ % 2, 0:nk], PX[:, i_ % 2, 0:nk], stats[:, 14:15], None, ALU.mult).then_inc(a_pn, 1)
                    v.drain()
            if STOP == "mla":
                return
            v_gdn(v)
            if STOP == "gdn":
                return
            v_rest(v)

        @block.gpsimd
        def _(pool):
            if STOP == "mla":
                return
            pool_gdn(pool)
            if STOP == "gdn":
                return
            pool_rest(pool)


program.stop = None
_INS = ["x", "meta", "par", "con", "w_in", "w_q_up", "w_kv_up", "w2", "a2", "g2", "w_branch", "w_out",
        "norm_ffn", "norm_final", "w_rg", "w_re", "b_rg", "b_re", "e_gate", "e_up", "e_down"]


def arrays_of(inputs):
    i = {k: np.ascontiguousarray(v) for k, v in inputs.items()}
    return {"x": i["x"][0], "meta": i["meta_tokens"], "par": per_channel(i), "con": constants(),
            "w_in": i["w_in"][0], "w_q_up": i["mla_w_q_up"][0], "w_kv_up": i["mla_w_kv_up"][0],
            "w2": i["rwkv_w2"][0], "a2": i["rwkv_a2"][0], "g2": i["rwkv_g2"][0],
            "w_branch": i["w_branch"][0], "w_out": i["w_out"][0],
            "norm_ffn": i["norm_ffn"], "norm_final": i["norm_final"][None],
            "w_rg": i["w_router_group"][0], "w_re": i["w_router_expert"][0],
            "b_rg": i["b_router_group"], "b_re": i["b_router_expert"],
            "e_gate": i["w_exp_gate"][0], "e_up": i["w_exp_up"][0], "e_down": i["w_exp_down"][0]}


def kernel(**inputs):
    import concourse.bacc as _bacc
    from concourse.bass_utils import run_bass_kernel_spmd as _run

    nc = _bacc.Bacc("TRN2", target_bir_lowering=False, num_devices=1)
    given = arrays_of(inputs)
    arrays, args = {}, []
    for name in _INS:
        a = np.ascontiguousarray(given[name])
        arrays[f"in_{name}"] = a
        args.append(nc.dram_tensor(f"in_{name}", a.shape, mybir.dt.from_np(a.dtype), kind="ExternalInput").ap())
    args.append(nc.dram_tensor("out_y", (SEQ, D), F32, kind="ExternalOutput").ap())
    program(nc, *args)
    r = _run(nc, [arrays], core_ids=[0])
    return r.results[0]["out_y"][None]
```
